# Optimizing a Trainium2 kernel written in Bass

```python
import jax, jax.numpy as jnp
from jax import lax
import numpy as np

D_MODEL = 1024
BATCH = 1
SEQ = 1024
DEPTH = 1
DEC_BATCH = 8
DEC_SEQ = 16
PAST_LEN = 1024

CHUNK = 64
ML_HEADS = 4
ML_DH = D_MODEL // ML_HEADS
ML_W = ML_HEADS * ML_DH
CONV_CH = D_MODEL
CONV_W = 31
CONV_BUF = CONV_W - 1
XA_HEADS = 4
XA_DH = D_MODEL // XA_HEADS
XA_W = XA_HEADS * XA_DH
MEM_LEN = 256
N_BRANCH = 3
BRANCH_W = 1024
D_FF = -(-8 * D_MODEL // (3 * 256)) * 256
IN_SIZES = (ML_W, ML_W, ML_W, ML_W, ML_HEADS, ML_HEADS, 2 * CONV_CH, XA_W, N_BRANCH * D_MODEL)
N_IN = sum(IN_SIZES)
IN_SPLITS = tuple(int(s) for s in np.cumsum(IN_SIZES)[:-1])
RMS_EPS = 1e-6
LN_EPS = 1e-5

kernel_name = "hybrid_mlstm_conformer_memxattn_stream_step"

def rms_norm(x, g):
    xf = x.astype(jnp.float32)
    y = xf * lax.rsqrt(jnp.mean(xf * xf, axis=-1, keepdims=True) + RMS_EPS)
    return (y * g.astype(jnp.float32)).astype(x.dtype)

def layer_norm(x, g, b):
    xf = x.astype(jnp.float32)
    mu = jnp.mean(xf, axis=-1, keepdims=True)
    xc = xf - mu
    y = xc * lax.rsqrt(jnp.mean(xc * xc, axis=-1, keepdims=True) + LN_EPS)
    return (y * g.astype(jnp.float32) + b.astype(jnp.float32)).astype(x.dtype)

def _mlstm_block(carry, blk):
    c, n, m = carry
    q, k, v, ig, lf = blk
    L = q.shape[2]
    b = jnp.cumsum(lf, axis=-1)
    causal = jnp.tril(jnp.ones((L, L), dtype=bool))
    d = jnp.where(causal, b[..., :, None] - b[..., None, :] + ig[..., None, :], -jnp.inf)
    a = b + m[..., None]
    m_row = jnp.maximum(a, jnp.max(d, axis=-1))
    s = jnp.einsum('bhjd,bhsd->bhjs', q, k) * jnp.exp(d - m_row[..., None])
    w_inter = jnp.exp(a - m_row)
    num = w_inter[..., None] * jnp.einsum('bhjd,bhed->bhje', q, c) + jnp.einsum('bhjs,bhse->bhje', s, v)
    den = w_inter * jnp.einsum('bhjd,bhd->bhj', q, n) + jnp.sum(s, axis=-1)
    h = num / jnp.maximum(jnp.abs(den), jnp.exp(-m_row))[..., None]
    b_last = b[..., -1]
    g = b_last[..., None] - b + ig
    m_new = jnp.maximum(b_last + m, jnp.max(g, axis=-1))
    w_old = jnp.exp(b_last + m - m_new)
    w_s = jnp.exp(g - m_new[..., None])
    c_new = w_old[..., None, None] * c + jnp.einsum('bhs,bhse,bhsd->bhed', w_s, v, k)
    n_new = w_old[..., None] * n + jnp.einsum('bhs,bhsd->bhd', w_s, k)
    return (c_new, n_new, m_new), h

def mlstm(q, k, v, ig, lf, state, block):
    B, T = q.shape[0], q.shape[1]
    nb = T // block

    def to_blocks(t):
        t = t.reshape((B, nb, block) + t.shape[2:])
        return jnp.swapaxes(jnp.moveaxis(t, 1, 0), 2, 3)

    xs = (to_blocks(q), to_blocks(k), to_blocks(v), to_blocks(ig), to_blocks(lf))
    state, hs = lax.scan(_mlstm_block, state, xs)
    h = jnp.moveaxis(jnp.swapaxes(hs, 2, 3), 0, 1).reshape(B, T, ML_HEADS, ML_DH)
    return h, state

def causal_dwconv(u, buf, w, b):
    ext = jnp.concatenate([buf.astype(u.dtype), u], axis=1)
    y = lax.conv_general_dilated(ext, w[:, None, :].astype(u.dtype), window_strides=(1,), padding='VALID',
                                 dimension_numbers=('NWC', 'WIO', 'NWC'), feature_group_count=u.shape[-1])
    return y + b.astype(u.dtype), ext[:, -CONV_BUF:]

def mem_kv(mem, g, w):
    B = mem.shape[0]
    kv = rms_norm(mem, g) @ w
    mk, mv = jnp.split(kv, 2, axis=-1)
    return mk.reshape(B, MEM_LEN, XA_HEADS, XA_DH), mv.reshape(B, MEM_LEN, XA_HEADS, XA_DH)

def mem_attention(q, mk, mv):
    s = jnp.einsum('bthd,bmhd->bhtm', q, mk.astype(q.dtype)).astype(jnp.float32) * (XA_DH ** -0.5)
    p = jax.nn.softmax(s, axis=-1).astype(q.dtype)
    return jnp.einsum('bhtm,bmhd->bthd', p, mv.astype(q.dtype))

def layer(x, ml_state, conv_buf, mk, mv, g_mix_pre, g_mix_post, g_ffn_pre, g_ffn_post, w_in, b_gate,
          g_mhead, conv_w, conv_b, ln_g, ln_b, w_branch, w_out, w_ffn_in, w_ffn_out):
    f32 = jnp.float32
    B, T, _ = x.shape
    block = min(CHUNK, T)
    xn = rms_norm(x, g_mix_pre)
    q, k, v, o, ig, fg, glu, xq, gates = jnp.split(xn @ w_in, IN_SPLITS, axis=-1)

    heads = lambda t: t.reshape(B, T, ML_HEADS, ML_DH).astype(f32)
    ig_t = ig.astype(f32) + b_gate[:ML_HEADS].astype(f32)
    lf_t = jax.nn.log_sigmoid(fg.astype(f32) + b_gate[ML_HEADS:].astype(f32))
    h, ml_state = mlstm(heads(q), heads(k) * (ML_DH ** -0.5), heads(v), ig_t, lf_t, ml_state, block)
    h = h * lax.rsqrt(jnp.mean(h * h, axis=-1, keepdims=True) + RMS_EPS) * g_mhead.astype(f32).reshape(ML_HEADS, ML_DH)
    y_ml = (h.reshape(B, T, ML_W) * jax.nn.sigmoid(o.astype(f32))).astype(x.dtype)

    ga, gb = jnp.split(glu, 2, axis=-1)
    u = ga * jax.nn.sigmoid(gb)
    c, conv_buf = causal_dwconv(u, conv_buf, conv_w, conv_b)
    y_cv = jax.nn.silu(layer_norm(c, ln_g, ln_b))

    y_xa = mem_attention(xq.reshape(B, T, XA_HEADS, XA_DH), mk, mv).reshape(B, T, XA_W)

    mixed = (jax.nn.sigmoid(gates[..., 0:D_MODEL]) * (y_ml @ w_branch[0])
             + jax.nn.sigmoid(gates[..., D_MODEL:2 * D_MODEL]) * (y_cv @ w_branch[1])
             + jax.nn.sigmoid(gates[..., 2 * D_MODEL:]) * (y_xa @ w_branch[2]))
    x = x + rms_norm(mixed @ w_out, g_mix_post)

    fa, fb = jnp.split(rms_norm(x, g_ffn_pre) @ w_ffn_in, 2, axis=-1)
    x = x + rms_norm((jax.nn.silu(fa) * fb) @ w_ffn_out, g_ffn_post)
    return x, ml_state, conv_buf

def setup_inputs(seed: int = 0) -> dict:
    key = jax.random.key(seed)
    ks = jax.random.split(key, 32)
    nrm = lambda k, shape, s: jax.random.normal(k, shape, jnp.float32) * s
    gain = lambda k, shape: 1.0 + 0.05 * jax.random.normal(k, shape, jnp.float32)
    f_bias = jnp.linspace(3.0, 6.0, ML_HEADS, dtype=jnp.float32)[None, :] + nrm(ks[0], (DEPTH, ML_HEADS), 0.1)
    i_bias = nrm(ks[1], (DEPTH, ML_HEADS), 0.1)
    return {
        "x_prompt": nrm(ks[2], (BATCH, SEQ, D_MODEL), 1.0),
        "x_sample": nrm(ks[3], (DEC_BATCH, DEC_SEQ, D_MODEL), 1.0),
        "mem_prompt": nrm(ks[4], (BATCH, MEM_LEN, D_MODEL), 1.0),
        "state_mlstm_c": nrm(ks[5], (DEPTH, DEC_BATCH, ML_HEADS, ML_DH, ML_DH), ML_DH ** -0.5),
        "state_mlstm_n": nrm(ks[6], (DEPTH, DEC_BATCH, ML_HEADS, ML_DH), 0.1),
        "state_mlstm_m": nrm(ks[7], (DEPTH, DEC_BATCH, ML_HEADS), 0.5),
        "state_conv": nrm(ks[8], (DEPTH, DEC_BATCH, CONV_BUF, CONV_CH), 0.5),
        "cache_mem_k": nrm(ks[9], (DEPTH, DEC_BATCH, MEM_LEN, XA_HEADS, XA_DH), 1.0),
        "cache_mem_v": nrm(ks[10], (DEPTH, DEC_BATCH, MEM_LEN, XA_HEADS, XA_DH), 1.0),
        "norm_mix_pre": gain(ks[11], (DEPTH, D_MODEL)),
        "norm_mix_post": gain(ks[12], (DEPTH, D_MODEL)),
        "norm_ffn_pre": gain(ks[13], (DEPTH, D_MODEL)),
        "norm_ffn_post": gain(ks[14], (DEPTH, D_MODEL)),
        "w_in": nrm(ks[15], (DEPTH, D_MODEL, N_IN), D_MODEL ** -0.5),
        "b_gate": jnp.concatenate([i_bias, f_bias], axis=-1),
        "mlstm_head_norm": gain(ks[16], (DEPTH, ML_W)),
        "conv_w": nrm(ks[17], (DEPTH, CONV_W, CONV_CH), CONV_W ** -0.5),
        "conv_b": nrm(ks[18], (DEPTH, CONV_CH), 0.02),
        "conv_ln_g": gain(ks[19], (DEPTH, CONV_CH)),
        "conv_ln_b": nrm(ks[20], (DEPTH, CONV_CH), 0.02),
        "mem_norm": gain(ks[21], (DEPTH, D_MODEL)),
        "w_mem_kv": nrm(ks[22], (DEPTH, D_MODEL, 2 * XA_W), D_MODEL ** -0.5),
        "w_branch": nrm(ks[23], (DEPTH, N_BRANCH, BRANCH_W, D_MODEL), BRANCH_W ** -0.5),
        "w_out": nrm(ks[24], (DEPTH, D_MODEL, D_MODEL), D_MODEL ** -0.5),
        "w_ffn_in": nrm(ks[25], (DEPTH, D_MODEL, 2 * D_FF), D_MODEL ** -0.5),
        "w_ffn_out": nrm(ks[26], (DEPTH, D_FF, D_MODEL), D_FF ** -0.5),
    }

def reference(x_prompt, x_sample, mem_prompt, state_mlstm_c, state_mlstm_n, state_mlstm_m, state_conv,
              cache_mem_k, cache_mem_v, norm_mix_pre, norm_mix_post, norm_ffn_pre, norm_ffn_post, w_in, b_gate,
              mlstm_head_norm, conv_w, conv_b, conv_ln_g, conv_ln_b, mem_norm, w_mem_kv, w_branch, w_out,
              w_ffn_in, w_ffn_out):
    f32 = jnp.float32
    bp = x_prompt.shape[0]
    yp, ys = x_prompt, x_sample
    pc, pn, pm, pconv, pmk, pmv = [], [], [], [], [], []
    sc, sn, sm, sconv = [], [], [], []
    for l in range(DEPTH):
        p = (norm_mix_pre[l], norm_mix_post[l], norm_ffn_pre[l], norm_ffn_post[l], w_in[l], b_gate[l],
             mlstm_head_norm[l], conv_w[l], conv_b[l], conv_ln_g[l], conv_ln_b[l], w_branch[l], w_out[l],
             w_ffn_in[l], w_ffn_out[l])
        mk_p, mv_p = mem_kv(mem_prompt, mem_norm[l], w_mem_kv[l])
        zero_state = (jnp.zeros((bp, ML_HEADS, ML_DH, ML_DH), f32), jnp.zeros((bp, ML_HEADS, ML_DH), f32),
                      jnp.zeros((bp, ML_HEADS), f32))
        zero_buf = jnp.zeros((bp, CONV_BUF, CONV_CH), x_prompt.dtype)
        yp, (c1, n1, m1), buf1 = layer(yp, zero_state, zero_buf, mk_p, mv_p, *p)
        s_state = (state_mlstm_c[l].astype(f32), state_mlstm_n[l].astype(f32), state_mlstm_m[l].astype(f32))
        ys, (c2, n2, m2), buf2 = layer(ys, s_state, state_conv[l], cache_mem_k[l], cache_mem_v[l], *p)
        pc.append(c1); pn.append(n1); pm.append(m1); pconv.append(buf1); pmk.append(mk_p); pmv.append(mv_p)
        sc.append(c2); sn.append(n2); sm.append(m2); sconv.append(buf2)
    return (yp, ys, jnp.stack(pc), jnp.stack(pn), jnp.stack(pm), jnp.stack(pconv), jnp.stack(pmk), jnp.stack(pmv),
            jnp.stack(sc), jnp.stack(sn), jnp.stack(sm), jnp.stack(sconv))


_drawn_inputs = setup_inputs


def setup_inputs(seed=0):
    import zlib

    import numpy as np

    out = dict(_drawn_inputs(seed))
    spreads = {}
    factors = {'conv_ln_b': 4.655}
    for name, (base, spread) in spreads.items():
        noise = np.random.default_rng([zlib.crc32(name.encode()), seed]).standard_normal(out[name].shape)
        drawn = base * np.exp(spread * noise) if base else spread * noise
        out[name] = __import__('jax').numpy.asarray(drawn.astype(out[name].dtype))
    for name, factor in factors.items():
        out[name] = (out[name] * factor).astype(out[name].dtype)
    return out
```

```python
from contextlib import ExitStack

import concourse.bass as bass
from concourse import mybir

F32 = mybir.dt.float32
F32R = mybir.dt.float32r
ACT = mybir.ActivationFunctionType
ALU = mybir.AluOpType
AX_X = mybir.AxisListType.X

P = 128
D = 1024
KT = D // P
SEQ = 1024
NB, TS = 8, 16
NTOK = SEQ + NB * TS
NT = NTOK // P
NPT = SEQ // P
TC = NTOK // 3
H, DH = 4, 256
MEM = 256
CW = 31
CB = CW - 1
DFF = 2816
FT = DFF // P
FK = FT // 2
RMS_EPS, LN_EPS = 1e-6, 1e-5
BIG = 1e30
NSEG = NPT + NB

RAW, SPLIT = 4, 2
GA, GB, QQ, KK, VV, OO, XQ, GT = 0, 8, 16, 24, 32, 40, 48, 56
NPROJ = 80
COLS = ((0, 16, 4104), (16, 32, 0), (48, 32, 6152))
IF_COL = 4096
V_MIX, V_FFN, V_MEM, V_HEAD, V_CB, V_LG, V_LB = range(7)
U_MEM, U_PROJ = 0, 16
U_BR = U_PROJ + NPROJ
U_TH = U_BR + 3 * KT
TH_UNITS = KT + 2 * FT + 2 * KT
CONV, MLSTM, XATT = 1, 0, 2


class Steps:

    def __init__(self, eng, sem):
        self.eng, self.sem, self.base, self.n = eng, sem, 0, 0

    def mark(self, ins):
        ins.then_inc(self.sem, 1)
        self.n += 1

    def wait(self, back=0):
        self.eng.wait_ge(self.sem, self.base + self.n - back)

    def link(self, ins):
        self.mark(ins)
        self.wait()

    def enter(self, i, per):
        self.saved = (self.base, self.n, per)
        self.base, self.n = self.base + self.n + per * i, 0

    def leave(self, trips):
        base, n, per = self.saved
        assert self.n == per, (self.n, per)
        self.base, self.n = base, n + per * trips


def hybrid_step(nc, a, o):
    ctx = ExitStack()
    with ctx:
        def sb(name, shape, dt=F32, scope=ctx):
            return scope.enter_context(nc.sbuf_tensor(name, shape, dt))

        def sem(name):
            return ctx.enter_context(nc.semaphore(name))

        A_hi, A_lo = sb("A_hi", [P, KT, NTOK], F32R), sb("A_lo", [P, KT, NTOK], F32R)
        w_raw = sb("w_raw", [P, RAW, FK, P])
        w_hi, w_lo = sb("w_hi", [P, SPLIT, FK, P], F32R), sb("w_lo", [P, SPLIT, FK, P], F32R)
        ident = sb("ident", [P, P])
        mean_mat = sb("mean_mat", [P, P])
        sel = sb("sel", [H, H, P])
        later = sb("later", [P, 2, P])
        minus_half = sb("minus_half", [P, H])
        ln_eps = sb("ln_eps", [P, 1])
        own = sb("own", [P, NB])
        cols = sb("cols", [P, 7, KT])
        taps = sb("taps", [P, CW, KT])
        gate_cols = sb("gate_cols", [P, NT, 4, H])
        keep_b = sb("keep_b", [P, H, NSEG])
        M_rows = sb("M_rows", [H, NTOK])
        keep_r = sb("keep_r", [H, NSEG])
        PS = ctx.enter_context(nc.psum_tensor("PS", [P, 8, 512], F32))

        u_tail = sb("u_tail", [P, KT, CB + P])

        s_early = ExitStack()
        stage = sb("stage", [P, 2, NTOK], F32, s_early)
        hist_T = sb("hist_T", [P, KT, NB, CB], F32, s_early)
        wif = sb("wif", [P, KT, P], F32, s_early)
        wif_hi, wif_lo = sb("wif_hi", [P, KT, P], F32R, s_early), sb("wif_lo", [P, KT, P], F32R, s_early)
        s_norm = ExitStack()
        x_in = sb("x_in", [P, 2, D], F32, s_norm)
        sq = sb("sq", [P, D], F32, s_norm)
        x_s = sb("x_s", [P, 2, D], F32, s_norm)
        x_ss = sb("x_ss", [P, 2], F32, s_norm)
        x_r0 = sb("x_r0", [P, 2], F32, s_norm)
        x_r = sb("x_r", [P, 2], F32, s_norm)
        x_T = sb("x_T", [P, 2, 4, P], F32, s_norm)
        vec_in = sb("vec_in", [7 * KT, P], F32, s_norm)
        tap_in = sb("tap_in", [124, 2, P], F32, s_norm)
        hist_in = stage[0:4 * CB, :, 0:D]
        mem_hi, mem_lo = sb("mem_hi", [P, KT, MEM], F32R, s_norm), sb("mem_lo", [P, KT, MEM], F32R, s_norm)
        s_norm.close()
        s_memkv = ExitStack()
        kv_T = sb("kv_T", [P, 2, MEM], F32, s_memkv)
        kv_nat = sb("kv_nat", [P, 2, 2, P], F32, s_memkv)
        s_memkv.close()
        s_gate = ExitStack()
        g_i = sb("g_i", [H, NTOK], F32, s_gate)
        g_f = sb("g_f", [H, NTOK], F32, s_gate)
        g_a = sb("g_a", [H, NTOK], F32, s_gate)
        g_b = sb("g_b", [H, NTOK], F32, s_gate)
        restart_mul = sb("restart_mul", [H, NTOK], F32, s_gate)
        restart_add = sb("restart_add", [H, NTOK], F32, s_gate)
        g_rows = sb("g_rows", [P, NTOK], F32, s_gate)
        g_bias = sb("g_bias", [P, 2], F32, s_gate)
        m_prev = sb("m_prev", [H, NSEG], F32, s_gate)
        m_new = sb("m_new", [H, NSEG], F32, s_gate)
        b_last = sb("b_last", [H, NSEG], F32, s_gate)
        M_last = sb("M_last", [H, NSEG], F32, s_gate)
        s_gate.close()
        s_conv = ExitStack()
        glu = sb("glu", [P, 2, 2, NTOK], F32, s_conv)
        EXT = CB + SEQ + NB * (CB + TS)
        ext = sb("ext", [P, 2, EXT], F32, s_conv)
        c_out = sb("c_out", [P, 2, NTOK], F32, s_conv)
        s_conv.close()
        s_early.close()
        s_ml = ExitStack()
        E1 = DH + 1
        q_in, k_in = sb("q_in", [P, 2, KT, P], F32, s_ml), sb("k_in", [P, 2, KT, P], F32, s_ml)
        v_in, o_in = sb("v_in", [P, KT, P], F32, s_ml), sb("o_in", [P, KT, P], F32, s_ml)
        v1 = sb("v1", [P, H, E1], F32, s_ml)
        oy = sb("oy", [P, 2, H, DH], F32, s_ml)
        kw = sb("kw", [P, H, DH], F32, s_ml)
        decay = sb("decay", [P, H, P], F32, s_ml)
        sT = sb("sT", [P, H, P], F32, s_ml)
        num = sb("num", [P, H, E1], F32, s_ml)
        C_T = sb("C_T", [P, H, 2, E1], F32, s_ml)
        y_T = sb("y_T", [P, 2, 4, P], F32, s_ml)
        den, rden, ssq, hr0, hr, hs = (sb(n, [P, H], F32, s_ml) for n in ("den", "rden", "ssq", "hr0", "hr", "hs"))
        qm = sb("qm", [P, 2, NB * (P + TS)], F32, s_ml)
        Cb_T = sb("Cb_T", [P, 2, 2, E1], F32, s_ml)
        v_own = sb("v_own", [P, 2, DH], F32, s_ml)
        n_in = y_T[0:NB * H, 0, 0:2].rearrange("p k c -> p (k c)")
        n_T = sb("n_T", [P, 2, NB * H], F32, s_ml)
        n_cols = sb("n_cols", [P, KT], F32, s_ml)
        n_row = o_in[0:KT, 0]
        keep8 = sb("keep8", [NB, H], F32, s_ml)
        s_ml.close()
        s_ff = ExitStack()
        m_hi, m_lo = sb("m_hi", [P, KT, TC], F32R, s_ff), sb("m_lo", [P, KT, TC], F32R, s_ff)
        mix_in = sb("mix_in", [P, KT, TC], F32, s_ff)
        x2 = sb("x2", [P, 3, D], F32, s_ff)
        nat = sb("nat", [P, 3, D], F32, s_ff)
        post = sb("post", [P, 2, D], F32, s_ff)
        ff_tmp = sb("ff_tmp", [P, 4, TC], F32, s_ff)
        n_ss, n_v, n_r = (sb(n, [P, 9], F32, s_ff) for n in ("n_ss", "n_v", "n_r"))
        oT, th = ff_tmp[:, 0:2], ff_tmp[:, 2:4]
        n_junk = ff_tmp[:].rearrange("p a n -> p (a n)")[:, 0:D]
        nT = u_tail[:].rearrange("p k n -> p (k n)")[:, 0:D].rearrange("p (n k c) -> p n k c", n=2, k=4)
        s_ff.close()
        s_xa = ExitStack()
        xq_in = sb("xq_in", [P, 2, KT, P], F32, s_xa)
        mk_T, mv = sb("mk_T", [P, KT, MEM], F32, s_xa), sb("mv", [P, 2, D], F32, s_xa)
        prob = sb("prob", [P, 2, H, MEM], F32, s_xa)
        prob_T = sb("prob_T", [P, 2, 2, H, P], F32, s_xa)
        xa_T = sb("xa_T", [P, 2, 4, P], F32, s_xa)
        cache_in = sb("cache_in", [P, 4, 2, D], F32, s_xa)
        xqm = prob_T[:].rearrange("p b m h j -> p b (m h) j")
        smax, ssum, rsum = (sb(n, [P, 2, H], F32, s_xa) for n in ("smax", "ssum", "rsum"))
        s_xa.close()
        s_br = ExitStack()
        gate_in = sb("gate_in", [P, 2, NTOK], F32, s_br)
        part_out = sb("part_out", [P, 2, NTOK], F32, s_br)
        s_ln = ExitStack()
        cT = sb("cT", [P, KT, NTOK], F32, s_ln)
        ln_x = sb("ln_x", [P, KT, TC], F32, s_ln)
        ln_r = sb("ln_r", [P, TC], F32, s_ln)
        s_ln.close()
        prev_in = sb("prev_in", [P, 2, NTOK], F32, s_br)
        s_br.close()

        proj_d = nc.dram_tensor("proj_d", (NPROJ, P, NTOK), F32, kind="Internal").ap()
        conv_d = nc.dram_tensor("conv_d", (KT, P, NTOK), F32, kind="Internal").ap()
        kvT_d = nc.dram_tensor("kvT_d", (2 * KT, P, MEM), F32, kind="Internal").ap()
        part_d = nc.dram_tensor("part_d", (KT, P, NTOK), F32, kind="Internal").ap()


        early_sems = ExitStack()
        early = []

        def early_sem(name):
            early.append(early_sems.enter_context(nc.semaphore(name)))
            return early[-1]

        def clear_early(eng):
            eng.sem_clear(range(min(x.num for x in early), max(x.num for x in early) + 1))

        w_loaded = [sem(f"w_loaded{s}") for s in range(RAW)]
        w_hi_done, w_lo_done, w_used = sem("w_hi_done"), sem("w_lo_done"), sem("w_used")
        phase_done = sem("phase_done")
        act_steps, dve_steps, pool_steps = sem("act_steps"), sem("dve_steps"), sem("pool_steps")
        st = {}

        w_in_v = a["w_in"][0].rearrange("(k p) c -> p k c", p=P)
        w_kv_v = a["w_mem_kv"][0].rearrange("(k p) c -> p k c", p=P)
        w_br_v = a["w_branch"][0].rearrange("b (k p) c -> b p k c", p=P)
        w_out_v = a["w_out"][0].rearrange("(k p) c -> p k c", p=P)
        w_fi_v = a["w_ffn_in"][0].rearrange("(k p) c -> p k c", p=P)
        w_fo_v = a["w_ffn_out"][0].rearrange("(z k p) c -> z p k c", p=P, k=FK)

        def load_w(sp, u, s, src, kt=KT):
            if not isinstance(u, int) or u >= RAW:
                sp.wait_ge(w_lo_done, u - RAW + 1)
            sp.dma_start(w_raw[:, s, 0:kt], src).then_inc(w_loaded[s], 16)

        def split_hi(act, u, lap, s, kt=KT):
            act.wait_ge(w_loaded[s], 16 * (lap + 1))
            if not isinstance(u, int) or u >= SPLIT:
                act.wait_ge(w_used, u - SPLIT + 1)
            nc.scalar.copy(w_hi[:, s % SPLIT, 0:kt], w_raw[:, s, 0:kt]).then_inc(w_hi_done, 1)

        def split_lo(pool, u, s, kt=KT):
            pool.wait_ge(w_hi_done, u + 1)
            nc.gpsimd.tensor_tensor(w_lo[:, s % SPLIT, 0:kt], w_raw[:, s, 0:kt],
                                    w_hi[:, s % SPLIT, 0:kt].bitcast(F32), ALU.subtract).then_inc(w_lo_done, 1)

        def product(outs, wh, wl, mh, ml, kt, start=True, stop=True):
            for k in range(kt):
                for n, (w, m) in enumerate(((wh, mh), (wh, ml), (wl, mh))):
                    for c, out in enumerate(outs):
                        last = nc.tensor.matmul(out, w[:, k], m(k, c), start=start and k == 0 and n == 0,
                                                stop=stop and k == kt - 1 and n == 2)
            return last

        def use_unit(pe, u, s, outs, mh, ml, kt=KT, start=True, stop=True):
            pe.wait_ge(w_lo_done, u + 1)
            product(outs, w_hi[:, s % SPLIT], w_lo[:, s % SPLIT], mh, ml, kt, start, stop).then_inc(w_used, 1)

        def end_phase(eng, n):
            eng.drain().then_inc(phase_done, 1)
            eng.wait_ge(phase_done, 5 * n)

        wif_lo_done = sem("wif_lo_done")

        vec_loaded, tap_loaded, hist_loaded, wif_loaded = (early_sem(n) for n in ("vec_loaded", "tap_loaded", "hist_loaded", "wif_loaded"))
        consts_ready, vec_T, vec_copied, hist_Tr = (early_sem(n) for n in ("consts_ready", "vec_T", "vec_copied", "hist_Tr"))
        wif_zero, wif_hi_done = sem("wif_zero"), sem("wif_hi_done")
        x_loaded = [early_sem("x_loaded0"), early_sem("x_loaded1")]
        x_sq, x_scaled, x_turned, x_gained, x_hi, x_lo = (early_sem(n) for n in ("x_sq", "x_scaled", "x_turned", "x_gained", "x_hi", "x_lo"))
        x_var, x_rstd = early_sem("x_var"), early_sem("x_rstd")
        N_IN = NT + MEM // P
        x_src = a["x_prompt"][0].rearrange("(t p) d -> t p d", p=P)
        s_src = a["x_sample"].rearrange("b t d -> (b t) d")
        m_src = a["mem_prompt"][0].rearrange("(t p) d -> t p d", p=P)

        def sp_norm(sp):
            for s in range(RAW):
                load_w(sp, s, s, w_kv_v[:, :, s * P:(s + 1) * P])
            for t in range(2):
                sp.dma_start(x_in[:, t], x_src[t]).then_inc(x_loaded[t], 16)
            for v, name in enumerate(("norm_mix_pre", "norm_ffn_pre", "mem_norm", "mlstm_head_norm",
                                      "conv_b", "conv_ln_g", "conv_ln_b")):
                sp.dma_start(vec_in[v * KT:(v + 1) * KT, :], a[name][0].rearrange("(k p) -> k p", p=P)).then_inc(vec_loaded, 16)
            sp.dma_start(tap_in[:], a["conv_w"][0].rearrange("w (k p) -> (w k) p", p=P)
                         .rearrange("(g r) p -> r g p", g=2)).then_inc(tap_loaded, 16)
            sp.dma_start(hist_in, a["state_conv"][0].rearrange("(g b) r c -> (b r) g c", g=2)).then_inc(hist_loaded, 16)
            sp.wait_ge(wif_zero, 1)
            for g in range(2):
                sp.dma_start(wif[:, :, 32 * g:32 * g + H], w_in_v[:, :, IF_COL + H * g:IF_COL + H * (g + 1)]).then_inc(wif_loaded, 16)

            def load_x(t, b, src):
                sp.wait_ge(x_scaled, t - 1)
                sp.dma_start(x_in[:, b], src).then_inc(x_loaded[b], 16)
            with sp.Fori(1, NPT // 2) as i:
                for b in range(2):
                    load_x(2 * i + b, b, x_src[bass.ds(2 * i + b, 1)].rearrange("a p d -> (a p) d"))
            load_x(NPT, 0, s_src)
            load_x(NPT + 1, 1, m_src[0])
            load_x(NPT + 2, 0, m_src[1])

        def pool_norm(pool):
            steps = st["pool"] = Steps(pool, pool_steps)
            pool.sem_inc(x_lo, 2)
            steps.mark(nc.gpsimd.memset(wif[:], 0.0))
            pool.wait_ge(pool_steps, 1)
            pool.sem_inc(wif_zero, 1)
            for t, v in ((ident[:], 0.0), (sel[:], 0.0), (later[:], 0.0), (own[:], 1.0), (minus_half[:], -0.5), (ln_eps[:], LN_EPS)):
                steps.mark(nc.gpsimd.memset(t, v))
            steps.wait()
            steps.mark(nc.gpsimd.affine_select(out=ident[:], in_=ident[:], compare_op=ALU.not_equal, fill=1.0, base=0,
                                               pattern=[[-1, P]], channel_multiplier=1))
            steps.mark(nc.gpsimd.affine_select(out=sel[:], in_=sel[:], compare_op=ALU.not_equal, fill=1.0, base=0,
                                               pattern=[[-1, H], [0, P]], channel_multiplier=1))
            for g in range(2):
                steps.mark(nc.gpsimd.affine_select(out=later[:, g], in_=later[:, g], compare_op=ALU.is_ge, fill=BIG, base=0,
                                                   pattern=[[1, P]], channel_multiplier=-1))
            steps.mark(nc.gpsimd.affine_select(out=own[:], in_=own[:], compare_op=ALU.is_ge, fill=0.0, base=0,
                                               pattern=[[-TS, NB]], channel_multiplier=1))
            steps.wait()
            v = later[:, 1].rearrange("p (b r) -> p b r", b=NB)
            steps.mark(nc.gpsimd.affine_select(out=v, in_=v, compare_op=ALU.is_ge, fill=BIG, base=0,
                                               pattern=[[-TS, NB], [0, TS]], channel_multiplier=1))
            steps.mark(nc.gpsimd.affine_select(out=own[:], in_=own[:], compare_op=ALU.is_ge, fill=0.0, base=TS - 1,
                                               pattern=[[TS, NB]], channel_multiplier=-1))
            steps.wait()
            pool.sem_inc(consts_ready, 1)
            for s in range(SPLIT):
                split_lo(pool, s, s)
            pool.wait_ge(wif_hi_done, 1)
            nc.gpsimd.tensor_tensor(wif_lo[:], wif[:], wif_hi[:].bitcast(F32), ALU.subtract).then_inc(wif_lo_done, 1)

            def lo(t, dst):
                for h in range(2):
                    pool.wait_ge(x_hi, 2 * t + h + 1)
                    d_hi, d_lo = dst(h)
                    pool.wait_ge(consts_ready, 1)
                    nc.gpsimd.tensor_tensor(d_lo, x_T[:, h], d_hi.bitcast(F32), ALU.subtract).then_inc(x_lo, 1)

            def rstd(t, b):
                pool.wait_ge(x_var, t + 1)
                nc.gpsimd.tensor_tensor(x_r[:, b:b + 1], x_r0[:, b:b + 1], minus_half[:, 0:1], ALU.pow).then_inc(x_rstd, 1)
            rstd(0, 0)
            rstd(1, 1)
            lo(0, lambda h: norm_dst(0, h))
            with pool.Fori(1, NPT // 2) as i:
                for b in range(2):
                    rstd(2 * i + b, b)
                    c = P * (2 * i + b - 1)
                    lo(2 * i + b - 1, lambda h: (A_hi[:, 4 * h:4 * h + 4, bass.ds(c, P)], A_lo[:, 4 * h:4 * h + 4, bass.ds(c, P)]))
            for t in range(NPT, N_IN):
                rstd(t, t % 2)
                lo(t - 1, lambda h: norm_dst(t - 1, h))
            lo(N_IN - 1, lambda h: norm_dst(N_IN - 1, h))

        def norm_dst(t, h):
            if t < NT:
                return A_hi[:, 4 * h:4 * h + 4, P * t:P * (t + 1)], A_lo[:, 4 * h:4 * h + 4, P * t:P * (t + 1)]
            c = P * (t - NT)
            return mem_hi[:, 4 * h:4 * h + 4, c:c + P], mem_lo[:, 4 * h:4 * h + 4, c:c + P]

        def act_norm(act):
            st["act"] = Steps(act, act_steps)
            split_hi(act, 0, 0, 0)
            split_hi(act, 1, 0, 1)
            act.wait_ge(wif_loaded, 32)
            nc.scalar.copy(wif_hi[:], wif[:]).then_inc(wif_hi_done, 1)

            def square(t, b, lap):
                act.wait_ge(x_loaded[b], 16 * (lap + 1))
                if not isinstance(t, int) or t:
                    act.wait_ge(x_sq, t)
                    act.wait_ge(x_scaled, t)
                act.wait_ge(wif_hi_done, 1)
                nc.scalar.activation(sq[:], x_in[:, b], ACT.Square, accum_out=x_ss[:, b:b + 1]).then_inc(x_sq, 1)

            def hi(t, dst):
                for h in range(2):
                    act.wait_ge(x_gained, 2 * t + h + 1)
                    act.wait_ge(wif_hi_done, 1)
                    nc.scalar.copy(dst(h), x_T[:, h]).then_inc(x_hi, 1)
            square(0, 0, 0)
            square(1, 1, 0)
            hi(0, lambda h: norm_dst(0, h)[0])
            with act.Fori(1, NPT // 2) as i:
                for b in range(2):
                    square(2 * i + b, b, i)
                    hi(2 * i + b - 1, lambda h: A_hi[:, 4 * h:4 * h + 4, bass.ds(P * (2 * i + b - 1), P)])
            for t in range(NPT, N_IN):
                square(t, t % 2, t // 2)
                hi(t - 1, lambda h: norm_dst(t - 1, h)[0])
            hi(N_IN - 1, lambda h: norm_dst(N_IN - 1, h)[0])

        def pe_norm(pe):
            pe.wait_ge(consts_ready, 1)
            pe.wait_ge(vec_loaded, 7 * 16)
            nc.tensor.transpose(PS[:, 5, 0:7 * KT], vec_in[:], ident[0:7 * KT, 0:7 * KT])
            pe.wait_ge(tap_loaded, 16)
            for g in range(2):
                last = nc.tensor.transpose(PS[:, 5, 64 + 124 * g:188 + 124 * g], tap_in[:, g], ident[0:124, 0:124])
            last.then_inc(vec_T, 1)
            pe.wait_ge(hist_loaded, 16)
            for n, bank in enumerate((6, 7, 4, 5)):
                if bank == 5:
                    pe.wait_ge(vec_copied, 1)
                for q in range(4):
                    k = 4 * (n % 2) + q
                    last = nc.tensor.transpose(PS[:, bank, 120 * q:120 * (q + 1)], hist_in[:, n // 2, k * P:(k + 1) * P], ident[0:120, 0:120])
                last.then_inc(hist_Tr, 1)

            def turn(t, b):
                pe.wait_ge(x_scaled, t + 1)
                for h in range(2):
                    if not isinstance(t, int) or t > 1:
                        pe.wait_ge(x_gained, 2 * (t - 2) + h + 1)
                    for q in range(4):
                        last = nc.tensor.transpose(PS[:, 2 * b + h, P * q:P * (q + 1)], x_s[:, b, P * (4 * h + q):P * (4 * h + q + 1)], ident[:])
                    last.then_inc(x_turned, 1)
            turn(0, 0)
            turn(1, 1)
            with pe.Fori(1, NPT // 2) as i:
                for b in range(2):
                    turn(2 * i + b, b)
            for t in range(NPT, N_IN):
                turn(t, t % 2)

        def dve_norm(dve):
            steps = st["dve"] = Steps(dve, dve_steps)
            steps.mark(nc.vector.memset(mean_mat[:], 1.0 / D))
            dve.wait_ge(vec_T, 1)
            steps.mark(nc.vector.tensor_copy(cols[:].rearrange("p v k -> p (v k)"), PS[:, 5, 0:7 * KT]))
            nc.vector.tensor_copy(taps[:].rearrange("p w k -> p (w k)"), PS[:, 5, 64:64 + CW * KT]).then_inc(vec_copied, 1)
            dve.wait_ge(vec_copied, 1)
            steps.mark(nc.vector.tensor_scalar(cols[:, V_HEAD], cols[:, V_HEAD], 0.25, None, ALU.mult))
            steps.mark(nc.vector.tensor_scalar(cols[:, V_LG:V_LB + 1], cols[:, V_LG:V_LB + 1], 0.25, None, ALU.mult))
            for n, bank in enumerate((6, 7, 4, 5)):
                dve.wait_ge(hist_Tr, n + 1)
                g, k = n // 2, 4 * (n % 2)
                steps.mark(nc.vector.tensor_copy(hist_T[:, k:k + 4, 4 * g:4 * g + 4].rearrange("p k b r -> p k (b r)"),
                                                 PS[:, bank, 0:480].rearrange("p (k r) -> p k r", k=4)))

            def scale(t, b):
                dve.wait_ge(x_sq, t + 1)
                nc.vector.tensor_scalar(x_r0[:, b:b + 1], x_ss[:, b:b + 1], 1.0 / D, RMS_EPS, ALU.mult, ALU.add).then_inc(x_var, 1)
                dve.wait_ge(x_rstd, t + 1)
                if not isinstance(t, int) or t > 1:
                    dve.wait_ge(x_turned, 2 * (t - 1))
                nc.vector.tensor_scalar(x_s[:, b], x_in[:, b], x_r[:, b:b + 1], None, ALU.mult).then_inc(x_scaled, 1)

            def gain(t, b, v):
                for h in range(2):
                    dve.wait_ge(x_turned, 2 * t + h + 1)
                    dve.wait_ge(x_lo, 2 * t + h + 1)
                    nc.vector.tensor_tensor(x_T[:, h], PS[:, 2 * b + h].rearrange("p (k c) -> p k c", k=4),
                                            cols[:, v, 4 * h:4 * h + 4].unsqueeze(2).broadcast_to([P, 4, P]),
                                            ALU.mult).then_inc(x_gained, 1)
            scale(0, 0)
            scale(1, 1)
            gain(0, 0, V_MIX)
            with dve.Fori(1, NPT // 2) as i:
                for b in range(2):
                    scale(2 * i + b, b)
                    gain(2 * i + b - 1, 1 - b, V_MIX)
            for t in range(NPT, N_IN):
                scale(t, t % 2)
                gain(t - 1, (t - 1) % 2, V_MIX if t - 1 < NT else V_MEM)
            gain(N_IN - 1, (N_IN - 1) % 2, V_MEM)

        kv_copied, kv_turned, kv_nat_ready = early_sem("kv_copied"), early_sem("kv_turned"), early_sem("kv_nat_ready")
        kvT_stored = [early_sem("kvT_stored0"), early_sem("kvT_stored1")]
        kv_stored = [early_sem("kv_stored0"), early_sem("kv_stored1")]
        NKV = 2 * KT

        def sp_memkv(sp):
            mk, mv = (o[n][0, 0].rearrange("(z m) h d -> m z (h d)", m=P) for n in ("p_mem_k", "p_mem_v"))

            def lap(g, dst, i, src):
                for s in range(RAW):
                    load_w(sp, KT * g + RAW * i + s + RAW, s, src(s))
                    sp.wait_ge(kv_nat_ready, KT * g + RAW * i + s + 1)
                    sp.dma_start(dst[:, :, bass.ds(P * (RAW * i + s), P)], kv_nat[:, s % 2]).then_inc(kv_stored[s % 2], 16)
            with sp.Fori(0, 2) as i:
                lap(0, mk, i, lambda s: w_kv_v[:, :, bass.ds(P * (RAW * (i + 1) + s), P)])
            lap(1, mv, 0, lambda s: w_kv_v[:, :, (12 + s) * P:(13 + s) * P])
            lap(1, mv, 1, lambda s: w_in_v[:, :, COLS[0][2] + s * P:COLS[0][2] + (s + 1) * P])
            for b in range(2):
                sp.wait_ge(kv_stored[b], 16 * NKV // 2)

        def kv_steps(eng, body, per=0):
            for s in range(RAW):
                body(s, 0, s)
            with eng.Fori(1, NKV // RAW) as i:
                if per:
                    st["x"].enter(i - 1, per)
                for s in range(RAW):
                    body(RAW * i + s, i, s)

        def act_memkv(act):
            def body(j, lap, s):
                split_hi(act, j + SPLIT, lap + (s + SPLIT) // RAW, (s + SPLIT) % RAW)
                act.wait_ge(w_used, j + 1)
                if not isinstance(j, int) or j > 1:
                    act.wait_ge(kv_turned, j - 1)
                    if s < 2:
                        act.wait_ge(kvT_stored[s % 2], 16 * (2 * lap))
                    else:
                        act.wait_ge(kvT_stored[s % 2], 16 * (2 * lap + 1))
                nc.scalar.copy(kv_T[:, s % 2], PS[:, s % 2, 0:MEM]).then_inc(kv_copied, 1)
                act.wait_ge(kv_copied, j + 1)
                dst = kvT_d[j] if isinstance(j, int) else kvT_d[bass.ds(j, 1)].rearrange("a p m -> (a p) m")
                act.dma_start(dst, kv_T[:, s % 2]).then_inc(kvT_stored[s % 2], 16)
            kv_steps(act, body)
            for b in range(2):
                act.wait_ge(kvT_stored[b], 16 * NKV // 2)

        def pool_memkv(pool):
            with pool.Fori(0, NKV // RAW) as i:
                for s in range(RAW):
                    split_lo(pool, RAW * i + s + SPLIT, (s + SPLIT) % RAW)

        def pe_memkv(pe):
            def turn(j, b):
                pe.wait_ge(kv_copied, j + 1)
                if not isinstance(j, int) or j > 1:
                    pe.wait_ge(kv_nat_ready, j - 1)
                for z in range(2):
                    last = nc.tensor.transpose(PS[:, 2 + b, P * z:P * (z + 1)], kv_T[:, b, P * z:P * (z + 1)], ident[:])
                last.then_inc(kv_turned, 1)

            def body(j, lap, s):
                if not isinstance(j, int) or j > 1:
                    pe.wait_ge(kv_copied, j - 1)
                use_unit(pe, j, s, [PS[:, s % 2, 0:MEM]], lambda k, c: mem_hi[:, k], lambda k, c: mem_lo[:, k])
                if not isinstance(j, int) or j > 0:
                    turn(j - 1, (s + 1) % 2)
            kv_steps(pe, body)
            turn(NKV - 1, 1)

        def dve_memkv(dve):
            def body(j, lap, s):
                dve.wait_ge(kv_turned, j + 1)
                if not isinstance(j, int) or j > 1:
                    dve.wait_ge(kv_stored[s % 2], 16 * (2 * lap + s // 2))
                nc.vector.tensor_copy(kv_nat[:, s % 2].rearrange("p z c -> p (z c)"), PS[:, 2 + s % 2, 0:MEM]).then_inc(kv_nat_ready, 1)
            kv_steps(dve, body)

        state_m_loaded, wif_used, gate_read = sem("state_m_loaded"), sem("wif_used"), sem("gate_read")
        g_dve, g_act, gate_turned, gates_done, m_stored = sem("g_dve"), sem("g_act"), sem("gate_turned"), sem("gates_done"), sem("m_stored")
        p_copied = sem("p_copied")
        stage_stored = [sem("stage_stored0"), sem("stage_stored1")]
        glu_loaded, c_stored = [sem("glu_loaded0"), sem("glu_loaded1")], [sem("c_stored0"), sem("c_stored1")]
        conv_done = sem("conv_done")
        cT_loaded, tail_turned, tail_read, tail_stored, hist_moved = sem("cT_loaded"), sem("tail_turned"), sem("tail_read"), sem("tail_stored"), sem("hist_moved")
        ln_mean, ln_centred, ln_sq, ln_var, ln_std, ln_scaled, ln_z, ln_tanh, ln_y, ln_hi, ln_lo = (
            sem(n) for n in ("ln_mean", "ln_centred", "ln_sq", "ln_var", "ln_std", "ln_scaled", "ln_z", "ln_tanh", "ln_y", "ln_hi", "ln_lo"))
        tail_p, tail_s = part_out[0:CB, 0, 0:D], part_out[:, 1, 0:D]
        LN_LAP = NPROJ // RAW - 6

        def cut(t, c):
            return t[:, :, TC * c:TC * (c + 1)] if isinstance(c, int) else t[:, :, bass.ds(TC * c, TC)]

        LAPS = NPROJ // RAW
        i_ = slice(0, H)

        def dtile(t, j):
            return t[j] if isinstance(j, int) else t[bass.ds(j, 1)].rearrange("a p n -> (a p) n")

        def thirds(t):
            return t.rearrange("p (c n) -> p c n", c=3)

        def seg(t, n):
            return (t[:, 0:SEQ].rearrange("h (s r) -> h s r", r=P) if n == 0 else
                    t[:, SEQ:NTOK].rearrange("h (s r) -> h s r", r=TS))

        def seg_of(t, n):
            v = t[:, 0:NPT] if n == 0 else t[:, NPT:NSEG]
            return v.unsqueeze(2).broadcast_to([H, 8, P if n == 0 else TS])

        def sp_proj(sp):
            sp.dma_start(g_bias[0:H, 0:1], a["b_gate"][0, 0:H].unsqueeze(1)).then_inc(state_m_loaded, 16)
            sp.dma_start(g_bias[32:32 + H, 0:1], a["b_gate"][0, H:2 * H].unsqueeze(1)).then_inc(state_m_loaded, 16)
            with nc.allow_non_contiguous_dma(reason="32 values"):
                sp.dma_start(m_prev[:, NPT:NSEG], a["state_mlstm_m"][0].rearrange("b h -> h b")).then_inc(state_m_loaded, 16)

            def lap(i, col):
                for s in range(RAW):
                    load_w(sp, U_PROJ + RAW * (i + 1) + s, s, w_in_v[:, :, bass.ds(col + P * s, P)])

            def load_glu(k, b):
                for g, t in enumerate((GA, GB)):
                    sp.dma_start(glu[:, b, g], dtile(proj_d, t + k)).then_inc(glu_loaded[b], 16)

            def store_c(k, b):
                sp.wait_ge(conv_done, k + 1)
                sp.dma_start(dtile(conv_d, k), c_out[:, b]).then_inc(c_stored[b], 16)

            def col(i):
                t = RAW * (i + 1)
                return COLS[1][2] + P * (t - COLS[1][0])
            with sp.Fori(0, 3) as i:
                lap(i, COLS[0][2] + P * RAW * (i + 1))
            lap(3, col(3))
            sp.wait_ge(g_dve, 8)
            with nc.allow_non_contiguous_dma(reason="36 values"):
                sp.dma_start(o["p_m"][0].rearrange("b h -> h b"), m_new[:, NPT - 1:NPT]).then_inc(m_stored, 16)
                sp.dma_start(o["s_m"][0].rearrange("b h -> h b"), m_new[:, NPT:NSEG]).then_inc(m_stored, 16)
            sp.wait_ge(m_stored, 32)
            for b in range(2):
                sp.wait_ge(stage_stored[b], 16 * 8)
            sp.wait_ge(gates_done, 1)
            load_glu(0, 0)
            lap(4, col(4))
            load_glu(1, 1)
            with sp.Fori(0, 3) as i:
                for b in range(2):
                    k = 2 * i + b + 2
                    lap(k + 3, COLS[1][2] + P * (RAW * (k + 4) - COLS[1][0]))
                    store_c(k - 2, b)
                    load_glu(k, b)
            with sp.Fori(0, 3) as i:
                lap(i + 11, COLS[2][2] + P * RAW * i)
            for b in range(2):
                store_c(KT - 2 + b, b)
            for b in range(2):
                sp.wait_ge(c_stored[b], 16 * KT // 2 + 16)
            sp.dma_start(cT[:], conv_d.rearrange("k p n -> p k n")).then_inc(cT_loaded, 16)
            sp.dma_start(o["s_conv"][0][:, 0:CB - TS, :], a["state_conv"][0][:, TS:CB, :]).then_inc(hist_moved, 16)
            with sp.Fori(3, 8) as i:
                lap(i + 11, COLS[2][2] + P * RAW * i)
            sp.wait_ge(tail_read, 4)
            sp.dma_start(o["p_conv"][0, 0], tail_p).then_inc(tail_stored, 16)
            for b in range(NB):
                sp.dma_start(o["s_conv"][0, b, CB - TS:CB, :], tail_s[TS * b:TS * (b + 1), :]).then_inc(tail_stored, 16)
            for s in range(RAW):
                load_w(sp, U_BR + s, s, w_br_v[CONV][:, :, s * P:(s + 1) * P])
            sp.wait_ge(tail_stored, 16 * (NB + 1))
            sp.wait_ge(hist_moved, 16)

        def act_proj(act):
            def lap(i, func, scale, between=()):
                for s in range(RAW):
                    j = RAW * i + s
                    u = U_PROJ + j
                    split_hi(act, u + SPLIT, U_PROJ // RAW + i + (s + SPLIT) // RAW, (s + SPLIT) % RAW)
                    act.wait_ge(w_used, u + 1)
                    if not isinstance(j, int) or j > 1:
                        act.wait_ge(stage_stored[s % 2], 16 * (2 * i + s // 2))
                    nc.scalar.activation(thirds(stage[:, s % 2]), PS[:, 3 * (s % 2):3 * (s % 2) + 3, 0:TC], func,
                                         scale=scale).then_inc(p_copied, 1)
                    act.wait_ge(p_copied, j + 1)
                    act.dma_start(dtile(proj_d, j), stage[:, s % 2]).then_inc(stage_stored[s % 2], 16)
                    if s < len(between):
                        between[s](act)

            def soft_exp(act):
                act.wait_ge(g_dve, 1)
                nc.scalar.activation(g_b[:], g_a[:], ACT.Exp).then_inc(g_act, 1)

            def soft_ln(act):
                act.wait_ge(g_act, 1)
                nc.scalar.activation(g_a[:], g_b[:], ACT.Ln, bias=1.0).then_inc(g_act, 1)

            def exps(act):
                act.wait_ge(g_dve, 9)
                nc.scalar.activation(g_rows[32:32 + H, :], g_f[:], ACT.Exp)
                nc.scalar.activation(g_rows[64:64 + H, :], g_a[:], ACT.Exp, scale=-1.0)
                nc.scalar.activation(keep_r[:], keep_r[:], ACT.Exp)
                nc.scalar.activation(g_rows[96:96 + H, :], g_b[:], ACT.Exp).then_inc(g_act, 1)
            lap(0, ACT.Copy, 0.5, (soft_exp, soft_ln))
            lap(1, ACT.Copy, 0.5, (exps,))
            for lo, hi, func, scale in ((2, 4, ACT.Tanh, 0.5), (4, 6, ACT.Copy, 1.0), (6, 8, ACT.Copy, DH ** -0.5),
                                        (8, 10, ACT.Copy, 1.0), (10, 12, ACT.Tanh, 0.5),
                                        (12, 14, ACT.Copy, DH ** -0.5)):
                with act.Fori(lo, hi) as i:
                    lap(i, func, scale)

            def square(c):
                act.wait_ge(ln_centred, c + 1)
                nc.scalar.activation(ln_x[:], cut(cT, c), ACT.Square).then_inc(ln_sq, 1)

            def std(c):
                act.wait_ge(ln_var, c + 1)
                nc.scalar.activation(ln_r[:], PS[:, 7, 0:TC], ACT.Sqrt, bias=ln_eps[:, 0:1]).then_inc(ln_std, 1)

            def affine(c):
                act.wait_ge(ln_scaled, c + 1)
                for k in range(KT):
                    v = cT[:, k, TC * c:TC * (c + 1)]
                    last = nc.scalar.activation(v, v, ACT.Identity, scale=cols[:, V_LG, k:k + 1], bias=cols[:, V_LB, k:k + 1])
                last.then_inc(ln_z, 1)

            def half_tanh(c):
                act.wait_ge(ln_z, c + 1)
                nc.scalar.activation(ln_x[:], cut(cT, c), ACT.Tanh, scale=2.0).then_inc(ln_tanh, 1)

            def none(c):
                pass
            for c in range(3):
                for h, steps_ in enumerate(((none, square, none, std), (affine, half_tanh, none, none))):
                    lap(2 * c + (LN_LAP + h), ACT.Tanh, 0.5, [lambda eng, f=f, c=c: f(c) for f in steps_])
            for b in range(2):
                act.wait_ge(stage_stored[b], 16 * NPROJ // 2)

        def pool_proj(pool):
            with pool.Fori(0, LAPS) as i:
                for s in range(RAW):
                    split_lo(pool, U_PROJ + RAW * i + s + SPLIT, (s + SPLIT) % RAW)

        def a_hi(k, c):
            return A_hi[:, k, TC * c:TC * (c + 1)]

        def a_lo(k, c):
            return A_lo[:, k, TC * c:TC * (c + 1)]

        def banks(b):
            return [PS[:, 3 * b + c, 0:TC] for c in range(3)]

        def pe_proj(pe):
            pe.wait_ge(wif_lo_done, 1)
            product(banks(1), wif_hi, wif_lo, a_hi, a_lo, KT).then_inc(wif_used, 1)

            def lap(i, between=None):
                for s in range(RAW):
                    j = RAW * i + s
                    if isinstance(j, int) and j == 1:
                        pe.wait_ge(gate_read, 1)
                    if not isinstance(j, int) or j > 1:
                        pe.wait_ge(p_copied, j - 1)
                    use_unit(pe, U_PROJ + j, s, banks(s % 2), a_hi, a_lo)
                    if between and s in between:
                        between[s]()
            lap(0)
            lap(1)
            lap(2)
            pe.wait_ge(g_act, 3)
            pe.wait_ge(g_dve, 9)
            for n in range(2):
                for q in range(4):
                    t = 4 * n + q
                    last = nc.tensor.transpose(PS[:, 6 + n, P * q:P * (q + 1)], g_rows[:, P * t:P * (t + 1)], ident[:])
                last.then_inc(gate_turned, 1)
            pe.wait_ge(gate_read, 2)
            nc.tensor.transpose(PS[:, 6, 0:P], g_rows[:, P * NPT:NTOK], ident[:])
            for h in range(H):
                last = nc.tensor.matmul(PS[:, 6, P + NSEG * h:P + NSEG * (h + 1)], sel[:, h], keep_r[:], start=True, stop=True)
            last.then_inc(gate_turned, 1)
            with pe.Fori(3, LN_LAP) as i:
                lap(i)
            pe.wait_ge(conv_done, KT)
            for g in range(2):
                for h in range(2):
                    if g:
                        pe.wait_ge(tail_read, h + 1)
                    for q in range(4):
                        k = 4 * h + q
                        out = PS[0:CB, 6 + h, P * q:P * (q + 1)] if g == 0 else PS[:, 6 + h, P * q:P * (q + 1)]
                        last = nc.tensor.transpose(out, u_tail[:, k, 0:CB] if g == 0 else u_tail[:, k, CB:CB + P], ident[:])
                    last.then_inc(tail_turned, 1)
            pe.wait_ge(cT_loaded, 16)
            pe.wait_ge(tail_read, 4)

            def average(src, bank, done):
                for k in range(KT):
                    last = nc.tensor.matmul(PS[:, bank, 0:TC], mean_mat[:], src(k), start=k == 0, stop=k == KT - 1)
                last.then_inc(done, 1)

            with pe.Fori(0, 3) as c:
                def mean():
                    average(lambda k: cT[:, k, bass.ds(TC * c, TC)], 6, ln_mean)

                def variance():
                    pe.wait_ge(ln_sq, c + 1)
                    average(lambda k: ln_x[:, k], 7, ln_var)
                lap(2 * c + LN_LAP, {0: mean, 2: variance})
                lap(2 * c + (LN_LAP + 1))

        def dve_proj(dve):
            steps = st["dve"]
            dve.sem_inc(c_stored[0], 16)
            dve.sem_inc(c_stored[1], 16)
            for t, v, w in ((restart_mul, 1.0, 0.0), (restart_add, 0.0, -BIG)):
                steps.link(nc.vector.memset(t[:], v))
                for n in range(2):
                    steps.mark(nc.vector.memset(seg(t, n)[:, :, 0:1], w))
            steps.mark(nc.vector.memset(g_rows[:], 0.0))
            steps.mark(nc.vector.memset(m_prev[:, 0:1], 0.0))
            steps.wait()
            dve.wait_ge(state_m_loaded, 48)
            dve.wait_ge(wif_used, 1)
            steps.mark(nc.vector.tensor_scalar(thirds(g_i[:]), PS[0:H, 3:6, 0:TC], g_bias[0:H, 0:1], None, ALU.add))
            nc.vector.tensor_scalar(thirds(g_f[:]), PS[32:32 + H, 3:6, 0:TC], g_bias[32:32 + H, 0:1], None, ALU.add).then_inc(gate_read, 1)
            dve.wait_ge(gate_read, 1)
            nc.vector.scalar_tensor_tensor(out=g_a[:], in0=g_f[:], scalar=-1.0, in1=g_f[:], op0=ALU.mult, op1=ALU.min).then_inc(g_dve, 1)
            dve.wait_ge(g_act, 2)
            nc.vector.scalar_tensor_tensor(out=g_f[:], in0=g_f[:], scalar=0.0, in1=g_a[:], op0=ALU.min, op1=ALU.subtract).then_inc(g_dve, 1)
            dve.wait_ge(g_dve, 2)
            nc.vector.tensor_tensor_scan(g_b[:], restart_mul[:], g_f[:], 0.0, ALU.mult, ALU.add).then_inc(g_dve, 1)
            dve.wait_ge(g_dve, 3)
            nc.vector.tensor_tensor(g_i[:], g_i[:], g_b[:], ALU.subtract).then_inc(g_dve, 1)
            dve.wait_ge(g_dve, 4)
            nc.vector.tensor_tensor_scan(g_a[:], restart_add[:], g_i[:], -BIG, ALU.add, ALU.max).then_inc(g_dve, 1)
            dve.wait_ge(g_dve, 5)
            for n, r in ((0, P), (1, TS)):
                lo = NPT * n
                steps.mark(nc.vector.tensor_copy(b_last[:, lo:lo + 8], seg(g_b, n)[:, :, r - 1]))
                steps.mark(nc.vector.tensor_copy(M_last[:, lo:lo + 8], seg(g_a, n)[:, :, r - 1]))
            steps.wait()
            steps.link(nc.vector.tensor_tensor_scan(m_new[:, 0:NPT], M_last[:, 0:NPT], b_last[:, 0:NPT], 0.0, ALU.max, ALU.add))
            steps.link(nc.vector.tensor_copy(m_prev[:, 1:NPT], m_new[:, 0:NPT - 1]))
            nc.vector.tensor_tensor(M_last[:], M_last[:], m_prev[:], ALU.max).then_inc(g_dve, 1)
            for n in range(2):
                steps.mark(nc.vector.tensor_tensor(seg(M_rows, n), seg(g_a, n), seg_of(m_prev, n), ALU.max))
            dve.wait_ge(g_dve, 6)
            steps.mark(nc.vector.tensor_tensor(keep_r[:], m_prev[:], M_last[:], ALU.subtract))
            nc.vector.tensor_tensor(m_new[:, NPT:NSEG], M_last[:, NPT:NSEG], b_last[:, NPT:NSEG], ALU.add).then_inc(g_dve, 1)
            steps.wait()
            nc.vector.tensor_tensor(g_a[:], g_b[:], M_rows[:], ALU.add).then_inc(g_dve, 1)
            dve.wait_ge(g_dve, 8)
            for n in range(2):
                steps.mark(nc.vector.tensor_tensor(seg(g_f, n), seg_of(m_prev, n), seg(M_rows, n), ALU.subtract))
                steps.mark(nc.vector.tensor_tensor(seg(g_b, n), seg(g_i, n), seg_of(M_last, n), ALU.subtract))
            steps.wait()
            nc.vector.tensor_copy(g_rows[0:H, :], g_i[:]).then_inc(g_dve, 1)
            for n in range(2):
                dve.wait_ge(gate_turned, n + 1)
                nc.vector.tensor_copy(gate_cols[:, 4 * n:4 * n + 4], PS[:, 6 + n].rearrange("p (t q c) -> p t q c", t=4, q=4)[:, :, :, 0:H]).then_inc(gate_read, 1)
            dve.wait_ge(gate_turned, 3)
            steps.mark(nc.vector.tensor_copy(gate_cols[:, NPT], PS[:, 6, 0:P].rearrange("p (q c) -> p q c", q=4)[:, :, 0:H]))
            steps.link(nc.vector.tensor_copy(keep_b[:].rearrange("p h s -> p (h s)"), PS[:, 6, P:P + H * NSEG]))
            dve.sem_inc(gates_done, 1)

            dve.wait_ge(m_stored, 32)
            steps.mark(nc.vector.memset(ext[:, 0, 0:CB], 0.0))
            steps.link(nc.vector.memset(ext[:, 1, 0:CB], 0.0))

            def tap_scalar(w, k):
                return taps[:, w, k:k + 1] if isinstance(k, int) else taps[:, w, bass.ds(k, 1)]
            with dve.Fori(0, KT // 2) as i:
                steps.enter(i, 2 * (4 + 2 * CW))
                for b in range(2):
                    k = 2 * i + b
                    ep, es = ext[:, b, 0:CB + SEQ], ext[:, b, CB + SEQ:EXT].rearrange("p (s r) -> p s r", s=NB)
                    cp, cs = c_out[:, b, 0:SEQ], c_out[:, b, SEQ:NTOK].rearrange("p (s r) -> p s r", s=NB)
                    dve.wait_ge(glu_loaded[b], 32 * (i + 1))
                    steps.mark(nc.vector.scalar_tensor_tensor(out=ep[:, CB:CB + SEQ], in0=glu[:, b, 1, 0:SEQ], scalar=1.0,
                                                              in1=glu[:, b, 0, 0:SEQ], op0=ALU.add, op1=ALU.mult))
                    steps.mark(nc.vector.scalar_tensor_tensor(out=es[:, :, CB:CB + TS], in0=glu[:, b, 1, SEQ:NTOK].rearrange("p (s r) -> p s r", s=NB),
                                                              scalar=1.0, in1=glu[:, b, 0, SEQ:NTOK].rearrange("p (s r) -> p s r", s=NB),
                                                              op0=ALU.add, op1=ALU.mult))
                    steps.link(nc.vector.tensor_copy(es[:, :, 0:CB], hist_T[:, bass.ds(k, 1)].rearrange("p k b r -> p (k b) r")))
                    dve.wait_ge(c_stored[b], 16 * (i + 1))
                    for e, c, n in ((ep, cp, SEQ), (es, cs, TS)):
                        src = e[:, 0:n] if n == SEQ else e[:, :, 0:n]
                        steps.mark(nc.vector.tensor_scalar(c, src, tap_scalar(0, k), cols[:, V_CB, bass.ds(k, 1)], ALU.mult, ALU.add))
                    for w in range(1, CW):
                        for e, c, n in ((ep, cp, SEQ), (es, cs, TS)):
                            src = e[:, w:w + n] if n == SEQ else e[:, :, w:w + n]
                            steps.wait(1)
                            steps.mark(nc.vector.scalar_tensor_tensor(out=c, in0=src, scalar=tap_scalar(w, k), in1=c,
                                                                      op0=ALU.mult, op1=ALU.add))
                    ut = u_tail[:, bass.ds(k, 1)].rearrange("p k n -> p (k n)")
                    steps.mark(nc.vector.tensor_copy(ut[:, 0:CB], ep[:, SEQ:SEQ + CB]))
                    steps.wait(1)
                    nc.vector.tensor_copy(ut[:, CB:CB + P].rearrange("p (s r) -> p s r", s=NB), es[:, :, CB:CB + TS]).then_inc(conv_done, 1)
                steps.leave(KT // 2)
            for g in range(2):
                for h in range(2):
                    dve.wait_ge(tail_turned, 2 * g + h + 1)
                    dst, src = (tail_p, PS[0:CB, 6 + h]) if g == 0 else (tail_s, PS[:, 6 + h])
                    nc.vector.tensor_copy(dst[:, 512 * h:512 * (h + 1)], src).then_inc(tail_read, 1)
            with dve.Fori(0, 3) as c:
                steps.enter(c, 1)
                dve.wait_ge(ln_mean, c + 1)
                nc.vector.tensor_tensor(cut(cT, c), cut(cT, c), PS[:, 6, 0:TC].unsqueeze(1).broadcast_to([P, KT, TC]),
                                        ALU.subtract).then_inc(ln_centred, 1)
                dve.wait_ge(ln_std, c + 1)
                steps.link(nc.vector.reciprocal(ln_r[:], ln_r[:]))
                nc.vector.tensor_tensor(cut(cT, c), cut(cT, c), ln_r[:].unsqueeze(1).broadcast_to([P, KT, TC]),
                                        ALU.mult).then_inc(ln_scaled, 1)
                dve.wait_ge(ln_tanh, c + 1)
                nc.vector.scalar_tensor_tensor(out=cut(cT, c), in0=ln_x[:], scalar=1.0, in1=cut(cT, c),
                                               op0=ALU.add, op1=ALU.mult).then_inc(ln_y, 1)
            steps.leave(3)

        def act_ln(act):
            for c in range(3):
                act.wait_ge(ln_y, c + 1)
                nc.scalar.copy(cut(A_hi, c), cut(cT, c)).then_inc(ln_hi, 1)

        def pool_ln(pool):
            pool.wait_ge(ln_hi, 2)
            nc.gpsimd.tensor_tensor(cut(A_lo, 1), cut(cT, 1), cut(A_hi, 1).bitcast(F32), ALU.subtract).then_inc(ln_lo, 1)

        def dve_ln(dve):
            for c in (0, 2):
                dve.wait_ge(ln_hi, c + 1)
                nc.vector.tensor_tensor(cut(A_lo, c), cut(cT, c), cut(A_hi, c).bitcast(F32), ALU.subtract).then_inc(ln_lo, 1)

        gate_loaded, part_stored = [sem("gate_loaded0"), sem("gate_loaded1")], [sem("part_stored0"), sem("part_stored1")]
        part_done, part_mul = sem("part_done"), sem("part_mul")
        prev_loaded = [sem("prev_loaded0"), sem("prev_loaded1")]
        ORDER = (CONV, MLSTM, XATT)

        def br_laps(eng, n, body):
            if n == 0:
                body(0)
            with eng.Fori(0 if n else 1, 2) as i:
                body(i)

        def sp_branch(sp, n, next_src):
            def lap(i, src):
                for s in range(RAW):
                    J = KT * n + RAW * i + s
                    load_w(sp, U_BR + J + RAW, s, src(s))
                    if J > 1:
                        sp.wait_ge(part_done, J - 1)
                        if RAW * i + s > 1:
                            sp.dma_start(part_d[RAW * i + s - 2], part_out[:, s % 2]).then_inc(part_stored[s % 2], 16)
                    sp.dma_start(gate_in[:, s % 2], proj_d[GT + KT * ORDER[n] + RAW * i + s]).then_inc(gate_loaded[s % 2], 16)
                    if n:
                        sp.dma_start(prev_in[:, s % 2], part_d[RAW * i + s]).then_inc(prev_loaded[s % 2], 16)
            lap(0, lambda s: w_br_v[ORDER[n]][:, :, (RAW + s) * P:(RAW + s + 1) * P])
            lap(1, next_src)
            for b in range(2):
                sp.wait_ge(part_done, KT * n + KT - 1 + b)
                sp.dma_start(part_d[KT - 2 + b], part_out[:, b]).then_inc(part_stored[b], 16)
            for b in range(2):
                sp.wait_ge(part_stored[b], 16 * 4 * (n + 1))

        def act_branch(act, n):
            with act.Fori(0, 2) as i:
                for s in range(RAW):
                    split_hi(act, U_BR + KT * n + RAW * i + s + SPLIT, U_BR // RAW + 2 * n + i + (s + SPLIT) // RAW, (s + SPLIT) % RAW)

        def pool_branch(pool, n):
            with pool.Fori(0, 2) as i:
                for s in range(RAW):
                    split_lo(pool, U_BR + KT * n + RAW * i + s + SPLIT, (s + SPLIT) % RAW)

        def pe_branch(pe, n, ready, count):
            pe.wait_ge(ready, count)

            def body(i):
                for s in range(RAW):
                    J = KT * n + RAW * i + s
                    if not isinstance(J, int) or J > 1:
                        pe.wait_ge(part_done, J - 1)
                    use_unit(pe, U_BR + J, s, banks(s % 2), a_hi, a_lo)
            br_laps(pe, n, body)

        def dve_branch(dve, n):
            def body(i):
                for s in range(RAW):
                    J = KT * n + RAW * i + s
                    lap = 2 * n + i
                    dve.wait_ge(w_used, U_BR + J + 1)
                    dve.wait_ge(gate_loaded[s % 2], 16 * (2 * lap + s // 2 + 1))
                    if not isinstance(J, int) or J > 1:
                        dve.wait_ge(part_stored[s % 2], 16 * (2 * lap + s // 2))
                    nc.vector.scalar_tensor_tensor(out=thirds(part_out[:, s % 2]), in0=thirds(gate_in[:, s % 2]), scalar=1.0,
                                                   in1=PS[:, 3 * (s % 2):3 * (s % 2) + 3, 0:TC], op0=ALU.add,
                                                   op1=ALU.mult).then_inc(part_mul if n else part_done, 1)
                    if n:
                        dve.wait_ge(part_mul, J - KT + 1)
                        dve.wait_ge(prev_loaded[s % 2], 16 * (2 * (lap - 2) + s // 2 + 1))
                        nc.vector.tensor_tensor(part_out[:, s % 2], part_out[:, s % 2], prev_in[:, s % 2], ALU.add).then_inc(part_done, 1)
            br_laps(dve, n, body)

        qk_loaded, vo_loaded = [sem("qk_loaded0"), sem("qk_loaded1")], sem("vo_loaded")
        (ml_M, ml_S, ml_turn, ml_D, ml_exp, ml_v1, ml_kw, ml_o, ml_sT, ml_intra, ml_U, ml_inter, ml_num, ml_rden, ml_sq,
         ml_var, ml_pow, ml_y, ml_upd, ml_state, ml_yT, ml_gain, ml_hi, ml_lo, ml_init) = (
            sem(n) for n in ("ml_M", "ml_S", "ml_turn", "ml_D", "ml_exp", "ml_v1", "ml_kw", "ml_o", "ml_sT", "ml_intra", "ml_U",
                             "ml_inter", "ml_num", "ml_rden", "ml_sq", "ml_var", "ml_pow", "ml_y", "ml_upd", "ml_state",
                             "ml_yT", "ml_gain", "ml_hi", "ml_lo", "ml_init"))
        n_loaded, cb_loaded, cb_stored = sem("n_loaded"), [sem(f"cb_loaded{s}") for s in range(4)], [sem("cb_stored0"), sem("cb_stored1")]
        sc_T, sc_CT, sc_own, sc_upd, sc_new, sc_qm, sc_n, fin_stored = (
            sem(n) for n in ("sc_T", "sc_CT", "sc_own", "sc_upd", "sc_new", "sc_qm", "sc_n", "fin_stored"))
        nf_turn, nf_copied, nu_done, nu_new, fc_turn, fc_copied = (
            sem(n) for n in ("nf_turn", "nf_copied", "nu_done", "nu_new", "fc_turn", "fc_copied"))
        SB = NPT
        cb_in = [x.rearrange("p (n z a) c -> p n z (a c)", n=2, z=2)[:, n] for x in (q_in[:, 1], o_in) for n in range(2)]
        cb_new = k_in[:, 1].rearrange("p (n z a) c -> p n z (a c)", n=2, z=2)
        nb_in = v_in[0:NB].rearrange("p k c -> p (k c)").rearrange("p (h d) -> p h d", h=H)

        def tok(t):
            return slice(P * t, P * (t + 1)) if isinstance(t, int) else bass.ds(P * t, P)

        def ml_tiles(eng, chunk, steps=None, per=0):
            chunk(0, 0, 0)
            with eng.Fori(0, (NPT - 2) // 2) as i:
                if steps:
                    steps.enter(i, 2 * per)
                chunk(2 * i + 1, 1, i)
                chunk(2 * i + 2, 0, i + 1)
            if steps:
                steps.leave((NPT - 2) // 2)
            chunk(NPT - 1, 1, (NPT - 1) // 2)

        def sp_mlstm(sp):
            def tiles(first, t):
                return proj_d[first:first + KT, :, tok(t)].rearrange("k p n -> p k n")

            def load(t, b):
                if not isinstance(t, int) or t > 0:
                    sp.wait_ge(ml_turn, 3 * t)
                sp.dma_start(v_in[:], tiles(VV, t)).then_inc(vo_loaded, 16)
                sp.dma_start(o_in[:], tiles(OO, t)).then_inc(vo_loaded, 16)
                if not isinstance(t, int) or t > 1:
                    sp.wait_ge(ml_inter, H * (t - 1))
                sp.dma_start(q_in[:, b], tiles(QQ, t)).then_inc(qk_loaded[b], 16)
                sp.dma_start(k_in[:, b], tiles(KK, t)).then_inc(qk_loaded[b], 16)
            sp.dma_start(n_in, a["state_mlstm_n"][0].rearrange("b h d -> (b h) d")).then_inc(n_loaded, 16)
            load(0, 0)
            load(1, 1)
            with sp.Fori(0, (NPT - 2) // 2) as i:
                load(2 * i + 2, 0)
                load(2 * i + 3, 1)
            load(SB, 0)
            sp.wait_ge(ml_turn, 3 * (SB + 1))
            sp.dma_start(nb_in, a["state_mlstm_n"][0]).then_inc(n_loaded, 16)
            sp.wait_ge(ml_inter, H * NPT)

            def c_dram(t, b, h):
                v = t[0, b].rearrange("h (z e) d -> h e z d", z=2)
                return v[h] if isinstance(h, int) else v[bass.ds(h, 1)].rearrange("h e z d -> (h e) z d")
            for b in range(4):
                sp.dma_start(cb_in[b], c_dram(a["state_mlstm_c"], b, 0)).then_inc(cb_loaded[b], 16)

            def head(h, last):
                for b in range(NB):
                    sp.wait_ge(sc_new, NB * h + b + 1)
                    sp.dma_start(c_dram(o["s_c"], b, h), cb_new[:, b % 2]).then_inc(cb_stored[b % 2], 16)
                    if b < NB - 4:
                        sp.dma_start(cb_in[b % 4], c_dram(a["state_mlstm_c"], b + 4, h)).then_inc(cb_loaded[b % 4], 16)
                    elif not last:
                        sp.dma_start(cb_in[b % 4], c_dram(a["state_mlstm_c"], b + 4 - NB, h + 1)).then_inc(cb_loaded[b % 4], 16)
            with sp.Fori(0, H - 1) as h:
                head(h, False)
            head(H - 1, True)
            sp.wait_ge(nu_new, 1)
            sp.dma_start(o["s_n"][0], nb_in).then_inc(fin_stored, 16)
            sp.wait_ge(nf_copied, 3)
            sp.dma_start(o["p_n"][0, 0].rearrange("h (z p) -> (h z) p", z=2), n_row).then_inc(fin_stored, 16)
            for h in range(H):
                sp.wait_ge(fc_copied, h + 1)
                sp.dma_start(c_dram(o["p_c"], 0, h), fc_out(h)).then_inc(fin_stored, 16)
            sp.wait_ge(fin_stored, 16 * (2 + H))
            for b in range(2):
                sp.wait_ge(cb_stored[b], 16 * NB * H // 2 + 16)

        def fc_out(h):
            return (q_in if h < 2 else k_in)[:, 0].rearrange("p (n z a) c -> p n z (a c)", n=2, z=2)[:, h % 2]

        def pe_mlstm(pe):
            def scores(t, b, uses):
                first = isinstance(t, int) and t == 0

                def state_read(banks):
                    if not first:
                        pe.wait_ge(ml_state, KT * (t - 1) + banks)
                state_read(2)
                for h in range(H):
                    last = nc.tensor.matmul(PS[:, 1, P * h:P * (h + 1)], sel[:, h], M_rows[:, tok(t)], start=True, stop=True)
                last.then_inc(ml_M, 1)
                pe.wait_ge(qk_loaded[b], 32 * (uses + 1))
                for h in range(H):
                    for z in range(2):
                        last = nc.tensor.matmul(PS[:, 0, P * h:P * (h + 1)], k_in[:, b, 2 * h + z], q_in[:, b, 2 * h + z],
                                                start=z == 0, stop=z == 1)
                last.then_inc(ml_S, 1)
                pe.wait_ge(vo_loaded, 32 * (t + 1))
                for n, src in enumerate((v_in, o_in, k_in[:, b])):
                    state_read(4 + 2 * n)
                    for k in range(KT):
                        last = nc.tensor.transpose(PS[:, 2 + 2 * n + k // 4, P * (k % 4):P * (k % 4 + 1)], src[:, k], ident[:])
                    last.then_inc(ml_turn, 1)
                pe.wait_ge(ml_v1, t + 1)
                if not first:
                    y_turn(t - 1, 1 - b)
                pe.wait_ge(ml_sT, t + 1)
                for h in range(H):
                    if h == 2 and not first:
                        pe.wait_ge(ml_gain, 2 * t)
                    nc.tensor.matmul(PS[:, h, 0:E1], sT[:, h], v1[:, h], start=True, stop=True).then_inc(ml_intra, 1)

            def y_turn(t, b):
                pe.wait_ge(ml_y, t + 1)
                for n in range(2):
                    for q in range(4):
                        k = 4 * n + q
                        last = nc.tensor.transpose(PS[:, 2 + n, P * q:P * (q + 1)], oy[:, b, k // 2, P * (k % 2):P * (k % 2 + 1)], ident[:])
                    last.then_inc(ml_yT, 1)

            def chunk(t, b, uses):
                scores(t, b, uses)
                pe.wait_ge(ml_o, t + 1)
                pe.wait_ge(ml_kw, t + 1)
                if isinstance(t, int) and t == 0:
                    pe.wait_ge(ml_init, 1)
                for h in range(H):
                    for z in range(2):
                        last = nc.tensor.matmul(PS[:, 4 + h, 0:E1], q_in[:, b, 2 * h + z], C_T[:, h, z], start=z == 0, stop=z == 1)
                    last.then_inc(ml_inter, 1)
                for h in range(H):
                    if h < 2:
                        pe.wait_ge(ml_U, H * t + 2 * (h + 1))
                    else:
                        pe.wait_ge(ml_num, H * t + 2 * (h - 1))
                    for z in range(2):
                        nc.tensor.matmul(PS[:, 2 * h + z, 0:E1], kw[:, h, P * z:P * (z + 1)], v1[:, h], start=True, stop=True).then_inc(ml_upd, 1)
            pe.wait_ge(n_loaded, 16)
            for z in range(2):
                last = nc.tensor.transpose(PS[:, 2, 32 * z:32 * (z + 1)], n_in[:, P * z:P * (z + 1)], ident[0:32, 0:32])
            nc.tensor.transpose(PS[0:NB, 2, 64:64 + H], keep_r[:, NPT:NSEG], ident[0:H, 0:H]).then_inc(nf_turn, 1)
            pe.wait_ge(nf_copied, 1)
            ml_tiles(pe, chunk)

            scores(SB, 0, SB // 2)
            pe.wait_ge(ml_o, SB + 1)
            pe.wait_ge(ml_kw, SB + 1)
            pe.wait_ge(ml_U, H * (SB + 1))
            with pe.Fori(0, H) as h:
                pe.wait_ge(ml_num, H * SB + h)
                pe.wait_ge(sc_qm, h + 1)
                def state_turn(b):
                    pe.wait_ge(cb_loaded[b % 4], 16 * (NB // 4 * h + b // 4 + 1))
                    pe.wait_ge(sc_CT, NB * h + b + 1)
                    for ze in range(2):
                        for zd in range(2):
                            last = nc.tensor.transpose(PS[:, b % 2, DH * zd + P * ze:DH * zd + P * (ze + 1)],
                                                       cb_in[b % 4][:, ze, P * zd:P * (zd + 1)], ident[:])
                    last.then_inc(sc_T, 1)
                state_turn(0)
                for b in range(NB):
                    r = NB * h + b
                    if b < NB - 1:
                        state_turn(b + 1)
                    pe.wait_ge(sc_own, r + 1)
                    if b > 1:
                        pe.wait_ge(sc_new, r - 1)
                    for z in range(2):
                        last = nc.tensor.matmul(PS[:, 2 + b % 2, DH * z:DH * (z + 1)], v_own[:, b % 2, P * z:P * (z + 1)],
                                                kw[:, bass.ds(h, 1)].rearrange("p h d -> p (h d)"), start=True, stop=True)
                    last.then_inc(sc_upd, 1)
                    pe.wait_ge(sc_CT, r + 3)
                    for z in range(2):
                        last = nc.tensor.matmul(PS[:, 4, 0:E1], qm[:, z, P * b:P * (b + 1)], Cb_T[:, b % 2, z],
                                                start=b == 0 and z == 0, stop=b == NB - 1 and z == 1)
                last.then_inc(ml_inter, 1)
            for h in range(H):
                last = nc.tensor.matmul(PS[0:NB, 6 + h // 2, DH * (h % 2):DH * (h % 2 + 1)], own[:], kw[:, h], start=True, stop=True)
            last.then_inc(nu_done, 1)
            pe.wait_ge(nf_copied, 2)
            nc.tensor.transpose(PS[0:KT, 5, 0:P], n_cols[:], ident[:]).then_inc(nf_turn, 1)

            def final_state(h):
                if h > 1:
                    pe.wait_ge(fc_copied, h - 1)
                for ze in range(2):
                    for zd in range(2):
                        last = nc.tensor.transpose(PS[:, h % 2, DH * ze + P * zd:DH * ze + P * (zd + 1)],
                                                   C_T[:, h, zd, P * ze:P * (ze + 1)], ident[:])
                last.then_inc(fc_turn, 1)
            final_state(0)
            final_state(1)
            y_turn(SB, 0)
            final_state(2)
            final_state(3)
            pe.wait_ge(fc_copied, H)

        def act_mlstm(act):
            def hi(t):
                for n in range(2):
                    act.wait_ge(ml_gain, 2 * t + n + 1)
                    act.wait_ge(gates_done, 1)
                    nc.scalar.copy(A_hi[:, 4 * n:4 * n + 4, tok(t)], y_T[:, n]).then_inc(ml_hi, 1)

            def front(t):
                act.wait_ge(ml_turn, 3 * t + 1)
                for n in range(2):
                    last = nc.scalar.copy(v1[:, 2 * n:2 * n + 2, 0:DH], PS[:, 2 + n].rearrange("p (h d) -> p h d", h=2))
                last.then_inc(ml_v1, 1)
                act.wait_ge(ml_D, t + 1)
                act.wait_ge(gates_done, 1)
                for h in range(H):
                    last = nc.scalar.activation(decay[:, h], decay[:, h], ACT.Exp, scale=-1.0, bias=gate_col(t, 0, h))
                last.then_inc(ml_exp, 1)
                act.wait_ge(ml_turn, 3 * t + 3)
                act.wait_ge(gates_done, 1)
                for h in range(H):
                    last = nc.scalar.activation(kw[:, h], PS[:, 6 + h // 2, DH * (h % 2):DH * (h % 2 + 1)], ACT.Copy, scale=gate_col(t, 3, h))
                last.then_inc(ml_kw, 1)
                if not isinstance(t, int) or t > 0:
                    hi(t - 1)
                    act.wait_ge(ml_y, t)
                for h in range(H):
                    act.wait_ge(ml_intra, H * t + h + 1)
                    nc.scalar.copy(num[:, h], PS[:, h, 0:E1]).then_inc(ml_U, 1)

            def back(t):
                act.wait_ge(ml_rden, t + 1)
                for h in range(H):
                    last = nc.scalar.activation(junk(h), num[:, h, 0:DH], ACT.Square, scale=rden[:, h:h + 1], accum_out=ssq[:, h:h + 1])
                last.then_inc(ml_sq, 1)

            def chunk(t, b, uses):
                front(t)
                back(t)
            ml_tiles(act, chunk)
            front(SB)
            with act.Fori(0, H) as h:
                for b in range(NB):
                    r = NB * h + b
                    act.wait_ge(sc_T, r + 1)
                    act.wait_ge(nf_copied, 1)
                    nc.scalar.copy(Cb_T[:, b % 2, :, 0:DH], PS[:, b % 2].rearrange("p (z e) -> p z e", z=2))
                    nc.scalar.copy(Cb_T[:, b % 2, :, DH:E1], n_T[:, :, bass.ds(H * b + h, 1)]).then_inc(sc_CT, 1)
            back(SB)
            for h in range(H):
                if h == 2:
                    hi(SB)
                act.wait_ge(fc_turn, h + 1)
                nc.scalar.copy(fc_out(h), PS[:, h % 2].rearrange("p (z d) -> p z d", z=2)).then_inc(fc_copied, 1)

        def junk(h):
            return (decay if h < 2 else sT)[:, 2 * (h % 2):2 * (h % 2) + 2].rearrange("p a b -> p (a b)")

        def gate_col(t, kind, h):
            if isinstance(t, int):
                return gate_cols[:, t, kind, h:h + 1]
            return gate_cols[:, bass.ds(t, 1), kind, h:h + 1].rearrange("p t h -> p (t h)")

        def keep_col(h, s):
            if isinstance(s, int) and isinstance(h, int):
                return keep_b[:, h, s:s + 1]
            if isinstance(h, int):
                return keep_b[:, h, bass.ds(s, 1)]
            return keep_b[:, bass.ds(h, 1), s:s + 1].rearrange("p h s -> p (h s)")

        def pool_mlstm(pool):
            def chunk(t, b=0, uses=0):
                pool.wait_ge(ml_var, t + 1)
                nc.gpsimd.tensor_tensor(hr[:], hr0[:], minus_half[:], ALU.pow).then_inc(ml_pow, 1)
                for n in range(2):
                    pool.wait_ge(ml_hi, 2 * t + n + 1)
                    pool.wait_ge(gates_done, 1)
                    nc.gpsimd.tensor_tensor(A_lo[:, 4 * n:4 * n + 4, tok(t)], y_T[:, n], A_hi[:, 4 * n:4 * n + 4, tok(t)].bitcast(F32),
                                            ALU.subtract).then_inc(ml_lo, 1)
            pool.sem_inc(ml_lo, 2)
            with pool.Fori(0, NPT) as t:
                chunk(t)
            chunk(SB)

        def dve_mlstm(dve):
            steps = st["dve"]

            def gain(t):
                for n in range(2):
                    dve.wait_ge(ml_yT, 2 * t + n + 1)
                    dve.wait_ge(ml_lo, 2 * t + n + 1)
                    nc.vector.tensor_tensor(y_T[:, n], PS[:, 2 + n].rearrange("p (k c) -> p k c", k=4),
                                            cols[:, V_HEAD, 4 * n:4 * n + 4].unsqueeze(2).broadcast_to([P, 4, P]),
                                            ALU.mult).then_inc(ml_gain, 1)

            def front(t, b, mask):
                dve.wait_ge(ml_M, t + 1)
                nc.vector.tensor_tensor(decay[:], PS[:, 1].rearrange("p (h j) -> p h j", h=H),
                                        later[:, mask].unsqueeze(1).broadcast_to([P, H, P]), ALU.add).then_inc(ml_D, 1)
                dve.wait_ge(ml_turn, 3 * t + 2)
                nc.vector.tensor_scalar(oy[:, b].rearrange("p (n h) d -> p n (h d)", n=2), PS[:, 4:6], 1.0, None, ALU.add).then_inc(ml_o, 1)
                dve.wait_ge(ml_S, t + 1)
                dve.wait_ge(ml_exp, t + 1)
                nc.vector.tensor_tensor(sT[:], decay[:], PS[:, 0].rearrange("p (h j) -> p h j", h=H), ALU.mult).then_inc(ml_sT, 1)
                if not isinstance(t, int) or t > 0:
                    gain(t - 1)

            def inter(t, h, bank, count, hh=None):
                dve.wait_ge(ml_U, count)
                dve.wait_ge(ml_inter, count)
                n = num[:, h] if isinstance(h, int) else num[:, bass.ds(h, 1)].rearrange("p h e -> p (h e)")
                w = gate_col(t, 1, h) if isinstance(h, int) else gate_cols[:, t, 1, bass.ds(h, 1)]
                nc.vector.scalar_tensor_tensor(out=n, in0=PS[:, bank, 0:E1], scalar=w, in1=n, op0=ALU.mult, op1=ALU.add).then_inc(ml_num, 1)

            def denominators(t):
                dve.wait_ge(ml_num, H * t + H)
                d = num[:, :, DH]
                em = gate_cols[:, t, 2] if isinstance(t, int) else gate_cols[:, bass.ds(t, 1), 2].rearrange("p t h -> p (t h)")
                steps.link(nc.vector.scalar_tensor_tensor(out=den[:], in0=d, scalar=-1.0, in1=d, op0=ALU.mult, op1=ALU.max))
                steps.link(nc.vector.tensor_tensor(den[:], den[:], em, ALU.max))
                nc.vector.reciprocal(rden[:], den[:]).then_inc(ml_rden, 1)

            def rows(t, b):
                dve.wait_ge(ml_sq, t + 1)
                nc.vector.tensor_scalar(hr0[:], ssq[:], 1.0 / DH, RMS_EPS, ALU.mult, ALU.add).then_inc(ml_var, 1)
                dve.wait_ge(ml_pow, t + 1)
                steps.link(nc.vector.tensor_tensor(hs[:], rden[:], hr[:], ALU.mult))
                for h in range(H):
                    last = nc.vector.scalar_tensor_tensor(out=oy[:, b, h], in0=num[:, h, 0:DH], scalar=hs[:, h:h + 1], in1=oy[:, b, h],
                                                          op0=ALU.mult, op1=ALU.mult)
                last.then_inc(ml_y, 1)

            def chunk(t, b, uses):
                front(t, b, 0)
                for h in range(H):
                    inter(t, h, 4 + h, H * t + h + 1)
                denominators(t)
                for h in range(H):
                    for z in range(2):
                        dve.wait_ge(ml_upd, KT * t + 2 * h + z + 1)
                        nc.vector.scalar_tensor_tensor(out=C_T[:, h, z], in0=C_T[:, h, z], scalar=keep_col(h, t), in1=PS[:, 2 * h + z, 0:E1],
                                                       op0=ALU.mult, op1=ALU.add).then_inc(ml_state, 1)
                rows(t, b)
            steps.mark(nc.vector.memset(C_T[:], 0.0))
            steps.mark(nc.vector.memset(v1[:, :, DH:E1], 1.0))
            steps.link(nc.vector.memset(qm[:], 0.0))
            dve.sem_inc(ml_init, 1)
            dve.wait_ge(nf_turn, 1)
            steps.mark(nc.vector.tensor_copy(n_T[:].rearrange("p z n -> p (z n)"), PS[:, 2, 0:2 * NB * H]))
            nc.vector.tensor_copy(keep8[:], PS[0:NB, 2, 64:64 + H]).then_inc(nf_copied, 1)
            ml_tiles(dve, chunk, steps, 3)

            dve.wait_ge(ml_state, KT * NPT)
            nc.vector.tensor_copy(n_cols[:].rearrange("p (h z) -> p h z", h=H), C_T[:, :, :, DH]).then_inc(nf_copied, 1)
            front(SB, 0, 1)
            dve.sem_inc(sc_CT, 2)
            for b in range(2):
                dve.sem_inc(cb_stored[b], 16)
            with dve.Fori(0, H) as h:
                for z in range(2):
                    last = nc.vector.tensor_copy(qm[:, z].rearrange("p (b r) -> p b r", b=NB)[:, :, 0:TS],
                                                 q_in[:, 0, bass.ds(2 * h + z, 1)].rearrange("p k (b r) -> p (k b) r", b=NB))
                last.then_inc(sc_qm, 1)
                for b in range(NB):
                    r = NB * h + b
                    if b > 1:
                        dve.wait_ge(sc_upd, r - 1)
                    nc.vector.tensor_scalar(v_own[:, b % 2], v1[:, bass.ds(h, 1), 0:DH].rearrange("p h d -> p (h d)"), own[:, b:b + 1], None,
                                            ALU.mult).then_inc(sc_own, 1)
                    if b:
                        new_state(dve, h, b - 1)
                new_state(dve, h, NB - 1)
                inter(SB, h, 4, H * SB + h + 1)
            dve.wait_ge(nu_done, 1)
            dve.wait_ge(n_loaded, 32)
            for h in range(H):
                last = nc.vector.scalar_tensor_tensor(out=nb_in[:, h], in0=nb_in[:, h], scalar=keep8[:, h:h + 1],
                                                      in1=PS[0:NB, 6 + h // 2, DH * (h % 2):DH * (h % 2 + 1)], op0=ALU.mult, op1=ALU.add)
            last.then_inc(nu_new, 1)
            dve.wait_ge(nf_turn, 2)
            dve.wait_ge(sc_new, NB * H)
            nc.vector.tensor_copy(n_row, PS[0:KT, 5, 0:P]).then_inc(nf_copied, 1)
            denominators(SB)
            rows(SB, 0)
            gain(SB)

        def new_state(dve, h, b):
            r = NB * h + b
            dve.wait_ge(sc_upd, r + 1)
            dve.wait_ge(cb_stored[b % 2], 16 * (NB // 2 * h + b // 2 + 1))
            nc.vector.scalar_tensor_tensor(out=cb_new[:, b % 2], in0=cb_in[b % 4], scalar=keep_col(h, NPT + b),
                                           in1=PS[:, 2 + b % 2].rearrange("p (z d) -> p z d", z=2), op0=ALU.mult, op1=ALU.add).then_inc(sc_new, 1)

        xq_loaded, mkv_loaded = [sem("xq_loaded0"), sem("xq_loaded1")], sem("mkv_loaded")
        (xa_S, xa_max, xa_exp, xa_p, xa_pT, xa_copied, xa_y, xa_half, xa_hi, xa_lo) = (
            sem(n) for n in ("xa_S", "xa_max", "xa_exp", "xa_p", "xa_pT", "xa_copied", "xa_y", "xa_half", "xa_hi", "xa_lo"))
        cache_loaded = [sem(f"cache_loaded{s}") for s in range(4)]
        ck_turn, ck_a, ck_d, ck_q, ck_used, cv_used = (sem(n) for n in ("ck_turn", "ck_a", "ck_d", "ck_q", "ck_used", "cv_used"))
        ck_T = (mk_T, mv[:].rearrange("p z c -> p (z c)").rearrange("p (k m) -> p k m", k=KT))

        def sp_xattn(sp):
            sp.dma_start(mk_T[:], kvT_d[0:KT].rearrange("k p m -> p k m")).then_inc(mkv_loaded, 16)
            sp.dma_start(mv[:], o["p_mem_v"][0, 0].rearrange("(z m) h d -> m z (h d)", m=P)).then_inc(mkv_loaded, 16)

            def load(t, b):
                if not isinstance(t, int) or t > 1:
                    sp.wait_ge(xa_S, t - 1)
                sp.dma_start(xq_in[:, b], proj_d[XQ:XQ + KT, :, tok(t)].rearrange("k p n -> p k n")).then_inc(xq_loaded[b], 16)

            def cache(name, b, slot):
                v = a[name][0].rearrange("b (z m) h d -> b m z (h d)", m=P)
                v = v[b] if isinstance(b, int) else v[bass.ds(b, 1)].rearrange("b m z c -> (b m) z c")
                sp.dma_start(cache_in[:, slot], v).then_inc(cache_loaded[slot], 16)
            load(0, 0)
            load(1, 1)
            with sp.Fori(1, NPT // 2) as i:
                load(2 * i, 0)
                load(2 * i + 1, 1)
            load(SB, 0)
            for b in range(4):
                cache("cache_mem_k", b, b)
            with sp.Fori(1, NB // 4) as i:
                for s in range(4):
                    sp.wait_ge(ck_turn, 2 * (4 * i + s - 3))
                    cache("cache_mem_k", 4 * i + s, s)
            for b in range(4):
                sp.wait_ge(ck_turn, 2 * (NB - 3 + b))
                cache("cache_mem_v", b, b)
            with sp.Fori(1, NB // 4) as i:
                for s in range(4):
                    sp.wait_ge(cv_used, 4 * i + s - 3)
                    cache("cache_mem_v", 4 * i + s, s)

        def pe_xattn(pe):
            def scores(t, b, lap):
                pe.wait_ge(xq_loaded[b], 16 * (lap + 1))
                if not isinstance(t, int) or t > 1:
                    pe.wait_ge(xa_exp, t - 1)
                for h in range(H):
                    for z in range(2):
                        last = nc.tensor.matmul(PS[:, 2 * b + h // 2, MEM * (h % 2):MEM * (h % 2 + 1)], xq_in[:, b, 2 * h + z],
                                                mk_T[:, 2 * h + z], start=z == 0, stop=z == 1)
                last.then_inc(xa_S, 1)

            def p_turn(t, b):
                pe.wait_ge(xa_p, t + 1)
                if not isinstance(t, int) or t > 0:
                    pe.wait_ge(xa_copied, t)
                for m in range(2):
                    for h in range(H):
                        last = nc.tensor.transpose(PS[:, 4 + m, P * h:P * (h + 1)], prob[:, b, h, P * m:P * (m + 1)], ident[:])
                last.then_inc(xa_pT, 1)

            def out(t, b):
                pe.wait_ge(xa_copied, t + 1)
                if not isinstance(t, int) or t > 0:
                    pe.wait_ge(xa_half, 2 * t)
                for k in range(KT):
                    for m in range(2):
                        last = nc.tensor.matmul(PS[:, 6 + k // 4, P * (k % 4):P * (k % 4 + 1)], mv[:, m, P * k:P * (k + 1)],
                                                prob_T[:, b, m, k // 2], start=m == 0, stop=m == 1)
                last.then_inc(xa_y, 1)
            pe.wait_ge(mkv_loaded, 32)
            scores(0, 0, 0)
            scores(1, 1, 0)
            p_turn(0, 0)
            scores(2, 0, 1)
            p_turn(1, 1)
            out(0, 0)
            scores(3, 1, 1)
            p_turn(2, 0)
            out(1, 1)
            with pe.Fori(2, NPT // 2) as i:
                for b in range(2):
                    t = 2 * i + b
                    scores(t, b, i)
                    p_turn(t - 1, 1 - b)
                    out(t - 2, b)
            p_turn(NPT - 1, 1)
            out(NPT - 2, 0)
            out(NPT - 1, 1)

            pe.wait_ge(xa_half, 2 * NPT)
            pe.wait_ge(xa_exp, NPT)

            def k_turn(b, s, lap):
                pe.wait_ge(cache_loaded[s], 16 * (lap + 1))
                for g in range(2):
                    if not isinstance(b, int) or b > 0:
                        pe.wait_ge((ck_a, ck_d)[g], b)
                    for q in range(4):
                        k = 4 * g + q
                        for m in range(2):
                            last = nc.tensor.transpose(PS[:, 4 + k // 2, MEM * (k % 2) + P * m:MEM * (k % 2) + P * (m + 1)],
                                                       cache_in[:, s, m, P * k:P * (k + 1)], ident[:])
                    last.then_inc(ck_turn, 1)

            def k_scores(b, s, first=False, end=False):
                pe.wait_ge(ck_a, b + 1)
                pe.wait_ge(ck_d, b + 1)
                pe.wait_ge(ck_q, b + 1)
                for k in range(KT):
                    h = k // 2
                    last = nc.tensor.matmul(PS[:, h // 2, MEM * (h % 2):MEM * (h % 2 + 1)], xqm[:, s, k], ck_T[s][:, k],
                                            start=first and k % 4 == 0, stop=end and k % 4 == 3, skip_group_check=True)
                last.then_inc(ck_used, 1)
            k_turn(0, 0, 0)
            for b in range(1, 4):
                k_turn(b, b, 0)
                k_scores(b - 1, 1 - b % 2, first=b == 1)
            with pe.Fori(1, NB // 4) as i:
                for s in range(4):
                    b = 4 * i + s
                    k_turn(b, s, i)
                    k_scores(b - 1, 1 - s % 2)
            k_scores(NB - 1, 1, end=True)
            p_turn(SB, 0)
            pe.wait_ge(xa_copied, SB + 1)
            with pe.Fori(0, NB // 4) as i:
                for s in range(4):
                    b = 4 * i + s
                    pe.wait_ge(cache_loaded[s], 16 * (NB // 4 + i + 1))
                    for k in range(KT):
                        for m in range(2):
                            last = nc.tensor.matmul(PS[:, 6 + k // 4, bass.ds(P * (k % 4) + TS * b, TS)], cache_in[:, s, m, P * k:P * (k + 1)],
                                                    prob_T[:, 0, m, k // 2, bass.ds(TS * b, TS)], start=m == 0, stop=m == 1)
                    last.then_inc(cv_used, 1)

        def act_xattn(act):
            def probs(t, b, ready):
                act.wait_ge(xa_max, t + 1)
                if not isinstance(t, int) or t > 1:
                    act.wait_ge(xa_pT, t - 1)
                for h in range(H):
                    last = nc.scalar.activation(prob[:, b, h], PS[:, 2 * b + h // 2, MEM * (h % 2):MEM * (h % 2 + 1)], ACT.Exp,
                                                bias=smax[:, b, h:h + 1], accum_out=ssum[:, b, h:h + 1])
                last.then_inc(xa_exp, 1)

            def turned(t, b):
                act.wait_ge(xa_pT, t + 1)
                if not isinstance(t, int) or t > 1:
                    act.wait_ge(xa_y, t - 1)
                nc.scalar.copy(prob_T[:, b].rearrange("p m h j -> p m (h j)"), PS[:, 4:6]).then_inc(xa_copied, 1)

            def hi(t):
                for n in range(2):
                    act.wait_ge(xa_half, 2 * t + n + 1)
                    act.wait_ge(gates_done, 1)
                    nc.scalar.copy(A_hi[:, 4 * n:4 * n + 4, tok(t)], xa_T[:, n]).then_inc(xa_hi, 1)
            probs(0, 0, 0)
            probs(1, 1, 0)
            turned(0, 0)
            for t in (2, 3):
                probs(t, t % 2, 0)
                turned(t - 1, 1 - t % 2)
                hi(t - 2)
            with act.Fori(2, NPT // 2) as i:
                for b in range(2):
                    t = 2 * i + b
                    probs(t, b, 0)
                    turned(t - 1, 1 - b)
                    hi(t - 2)
            turned(NPT - 1, 1)
            hi(NPT - 2)
            hi(NPT - 1)

            def keys(b, s):
                act.wait_ge(ck_turn, 2 * b + 1)
                if not isinstance(b, int) or b > 1:
                    act.wait_ge(ck_used, b - 1)
                nc.scalar.copy(ck_T[s][:, 0:4].rearrange("p (a k) m -> p a (k m)", a=2), PS[:, 4:6]).then_inc(ck_a, 1)
            keys(0, 0)
            keys(1, 1)
            with act.Fori(1, NB // 2) as i:
                for s in range(2):
                    keys(2 * i + s, s)
            act.wait_ge(ck_used, NB)
            probs(SB, 0, 0)
            turned(SB, 0)
            hi(SB)

        def pool_xattn(pool):
            def lo(t):
                for n in range(2):
                    pool.wait_ge(xa_hi, 2 * t + n + 1)
                    pool.wait_ge(gates_done, 1)
                    nc.gpsimd.tensor_tensor(A_lo[:, 4 * n:4 * n + 4, tok(t)], xa_T[:, n], A_hi[:, 4 * n:4 * n + 4, tok(t)].bitcast(F32),
                                            ALU.subtract).then_inc(xa_lo, 1)
            with pool.Fori(0, NPT) as t:
                lo(t)
            lo(SB)

        def dve_xattn(dve):
            steps = st["dve"]

            def maxima(t, b, sem_, count):
                dve.wait_ge(sem_, count)
                nc.vector.tensor_reduce(smax[:, b], PS[:, 2 * b:2 * b + 2].rearrange("p n (h m) -> p (n h) m", h=2), AX_X, ALU.max,
                                        negate=True).then_inc(xa_max, 1)

            def norm(t, b):
                dve.wait_ge(xa_exp, t + 1)
                steps.link(nc.vector.reciprocal(rsum[:, b], ssum[:, b]))
                for h in range(H):
                    last = nc.vector.tensor_scalar(prob[:, b, h], prob[:, b, h], rsum[:, b, h:h + 1], None, ALU.mult)
                last.then_inc(xa_p, 1)

            def half(t, sem_, count):
                dve.wait_ge(sem_, count)
                for n in range(2):
                    if not isinstance(t, int) or t > 0:
                        dve.wait_ge(xa_lo, 2 * t + n - 1)
                    nc.vector.tensor_scalar(xa_T[:, n].rearrange("p k c -> p (k c)"), PS[:, 6 + n], 0.5, None, ALU.mult).then_inc(xa_half, 1)
            maxima(0, 0, xa_S, 1)
            norm(0, 0)
            maxima(1, 1, xa_S, 2)
            norm(1, 1)
            for t in (2, 3):
                maxima(t, t % 2, xa_S, t + 1)
                norm(t, t % 2)
                half(t - 2, xa_y, t - 1)
            with dve.Fori(2, NPT // 2) as i:
                steps.enter(i - 2, 2)
                for b in range(2):
                    t = 2 * i + b
                    maxima(t, b, xa_S, t + 1)
                    norm(t, b)
                    half(t - 2, xa_y, t - 1)
            steps.leave(NPT // 2 - 2)
            half(NPT - 2, xa_y, NPT - 1)
            half(NPT - 1, xa_y, NPT)

            def own_queries(b, s):
                if not isinstance(b, int) or b > 1:
                    dve.wait_ge(ck_used, b - 1)
                steps.link(nc.vector.memset(xqm[:, s], 0.0))
                c = slice(TS * b, TS * (b + 1)) if isinstance(b, int) else bass.ds(TS * b, TS)
                nc.vector.tensor_copy(xqm[:, s, :, c], xq_in[:, 0, :, c]).then_inc(ck_q, 1)

            def keys(b, s):
                dve.wait_ge(ck_turn, 2 * b + 2)
                nc.vector.tensor_copy(ck_T[s][:, 4:8].rearrange("p (a k) m -> p a (k m)", a=2), PS[:, 6:8]).then_inc(ck_d, 1)
            dve.wait_ge(xq_loaded[0], 16 * (NPT // 2 + 1))
            for b in range(2):
                own_queries(b, b)
                keys(b, b)
            with dve.Fori(1, NB // 2) as i:
                steps.enter(i - 1, 2)
                for s in range(2):
                    own_queries(2 * i + s, s)
                    keys(2 * i + s, s)
            steps.leave(NB // 2 - 1)
            maxima(SB, 0, ck_used, NB)
            norm(SB, 0)
            half(SB, cv_used, NB)

        early_sems.close()
        x2_loaded, post_loaded, mix_loaded, y_stored = sem("x2_loaded"), sem("post_loaded"), [sem(f"mix_loaded{r}") for r in range(4)], sem("y_stored")
        mix_hi, mix_lo = sem("mix_hi"), sem("mix_lo")
        f_copied, f_turned, f_nat = sem("f_copied"), sem("f_turned"), sem("f_nat")
        n_sq, n_var, n_pow, n_post, n_x2, n_xs, n_turned, n_gain, n_hi, n_lo, n_y = (
            sem(n) for n in ("n_sq", "n_var", "n_pow", "n_post", "n_x2", "n_xs", "n_turned", "n_gain", "n_hi", "n_lo", "n_y"))
        f_th, f_v, f_g, f_hi, f_lo = sem("f_th"), sem("f_v"), sem("f_g"), sem("f_hi"), sem("f_lo")
        G_hi, G_lo = (t[:].rearrange("p k n -> p (k n)")[:, 0:FT * TC].rearrange("p (f n) -> p f n", n=TC) for t in (A_hi, A_lo))
        IN_LAPS, OUT_LAPS = 2 * FT // RAW, 2 * KT // RAW
        UNITS = TH_UNITS
        TILES, NORMS, HALVES = 2 * KT, 9, 6

        def unit(third, n):
            return U_TH + UNITS * third + n

        def lap_of(third, n):
            return U_TH // RAW + UNITS // RAW * third + n // RAW

        def sp_ffn(sp):
            for g, name in enumerate(("norm_mix_post", "norm_ffn_post")):
                sp.dma_start(post[:, g], a[name][0].partition_broadcast(P)).then_inc(post_loaded, 16)

            def token_tile(prompt, sample, t):
                return prompt[0].rearrange("(t p) d -> t p d", p=P)[t] if t < NPT else sample.rearrange("b t d -> (b t) d")

            def mix_round(third, r):
                if third:
                    sp.wait_ge(mix_lo, 4 * third)
                sp.dma_start(mix_in[:, 2 * r:2 * r + 2], part_d[2 * r:2 * r + 2, :, TC * third:TC * (third + 1)].rearrange("k p n -> p k n")
                             ).then_inc(mix_loaded[r], 16)

            def load_x2(third):
                for n in range(3):
                    sp.dma_start(x2[:, n], token_tile(a["x_prompt"], a["x_sample"], 3 * third + n)).then_inc(x2_loaded, 16)

            def store_y(third):
                for n in range(3):
                    sp.wait_ge(n_y, 3 * third + n + 2)
                    sp.dma_start(token_tile(o["y_prompt"], o["y_sample"], 3 * third + n), x2[:, n]).then_inc(y_stored, 16)
                sp.wait_ge(y_stored, 48 * (third + 1))

            def ffn_in_src(i, s):
                return w_fi_v[:, :, bass.ds(DFF * (s % 2) + P * (2 * i + s // 2), P)]

            def ffn_out_src(i, s):
                return w_fo_v[s % 2][:, :, bass.ds(P * (2 * i + s // 2), P)]
            load_x2(0)
            for r in range(4):
                mix_round(0, r)
            for third in range(3):
                for s in range(RAW):
                    load_w(sp, unit(third, RAW + s), s, w_out_v[:, :, (RAW + s) * P:(RAW + s + 1) * P])
                if third:
                    store_y(third - 1)
                    load_x2(third)
                for s in range(RAW):
                    load_w(sp, unit(third, KT + s), s, ffn_in_src(0, s))
                with sp.Fori(1, IN_LAPS) as i:
                    for s in range(RAW):
                        load_w(sp, unit(third, KT + s) + RAW * i, s, ffn_in_src(i, s))
                for s in range(RAW):
                    load_w(sp, unit(third, KT + 2 * FT + s), s, ffn_out_src(0, s), FK)
                for i in range(OUT_LAPS):
                    if third < 2:
                        mix_round(third + 1, i)
                    for s in range(RAW):
                        if i < OUT_LAPS - 1:
                            load_w(sp, unit(third, KT + 2 * FT + RAW * (i + 1) + s), s, ffn_out_src(i + 1, s), FK)
                        elif third < 2:
                            load_w(sp, unit(third + 1, s), s, w_out_v[:, :, s * P:(s + 1) * P])
            store_y(2)

        def thirds_of(eng, body):
            with eng.Fori(0, 2) as third:
                body(third, False)
            body(2, True)

        def pe_ffn(pe):
            def turn(third, c, b):
                O = TILES * third + c
                pe.wait_ge(f_copied, O + 3)
                pe.wait_ge(f_nat, O + 1)
                for n in range(3):
                    last = nc.tensor.transpose(PS[:, 6 + b, P * n:P * (n + 1)], oT[:, b, P * n:P * (n + 1)], ident[:])
                last.then_inc(f_turned, 1)

            def third_of(third, last):
                pe.wait_ge(mix_lo, 4 * third + 4)
                for j in range(KT):
                    pe.wait_ge(f_copied, TILES * third + j + 1)
                    use_unit(pe, unit(third, j), j % RAW, [PS[:, 4 + j % 2, 0:TC]], lambda k, c: m_hi[:, k], lambda k, c: m_lo[:, k])
                    if j:
                        turn(third, j - 1, (j - 1) % 2)
                turn(third, KT - 1, 1)
                for n in range(3):
                    pe.wait_ge(n_xs, 3 * third + n + 1)
                    for h in range(2):
                        if n == 2:
                            pe.wait_ge(n_gain, HALVES * third + h + 1)
                        for q in range(4):
                            k = 4 * h + q
                            t = nc.tensor.transpose(PS[:, 2 * (n % 2) + h, P * q:P * (q + 1)], nat[:, n, P * k:P * (k + 1)], ident[:])
                        t.then_inc(n_turned, 1)
                with pe.Fori(0, IN_LAPS) as i:
                    pe.wait_ge(n_lo, HALVES * third + HALVES + 2)
                    for s in range(RAW):
                        if s % 2 == 0:
                            pe.wait_ge(f_g, FT * third + 2 * i + s // 2 + 1)
                        use_unit(pe, unit(third, KT + s) + RAW * i, s, [PS[:, s, 0:TC]], lambda k, c: m_hi[:, k], lambda k, c: m_lo[:, k])
                pe.wait_ge(f_lo, FT * third + FT + 2)

                def out_lap(i, first):
                    for s in range(RAW):
                        c, z = 2 * i + s // 2, s % 2
                        if z == 0:
                            pe.wait_ge(f_copied, TILES * third + KT + c + 1)
                        use_unit(pe, unit(third, KT + 2 * FT + s) + RAW * i, s, [PS[:, 4 + s // 2, 0:TC]],
                                 lambda k, c, z=z: G_hi[:, FK * z + k], lambda k, c, z=z: G_lo[:, FK * z + k], FK, z == 0, z == 1)
                        if z and not (first and s == 1):
                            turn(third, KT + c - 1, 1 - s // 2)
                out_lap(0, True)
                with pe.Fori(1, OUT_LAPS) as i:
                    out_lap(i, False)
                turn(third, TILES - 1, 1)
            thirds_of(pe, third_of)

        def act_ffn(act):
            def evac(third, c, b):
                O = TILES * third + c
                act.wait_ge(f_turned, O + 1)
                nc.scalar.copy(oT[:, b], PS[:, 4 + b, 0:TC]).then_inc(f_copied, 1)

            def mix_round(third, r):
                act.wait_ge(mix_loaded[r], 16 * (third + 1))
                nc.scalar.copy(m_hi[:, 2 * r:2 * r + 2], mix_in[:, 2 * r:2 * r + 2]).then_inc(mix_hi, 1)

            def square(third, n, src):
                if not (isinstance(third, int) and third == 0 and n == 0):
                    act.wait_ge(n_sq, NORMS * third + n + 1)
                nc.scalar.activation(n_junk, src, ACT.Square, accum_out=n_ss[:, n:n + 1]).then_inc(n_sq, 1)

            def gate(third, p, b):
                act.wait_ge(f_lo, FT * third + p + 1)
                nc.scalar.activation(th[:, b], PS[:, 2 * b, 0:TC], ACT.Tanh, scale=0.5).then_inc(f_th, 1)

            def hi(third, p, b):
                act.wait_ge(f_g, FT * third + p + 3)
                act.wait_ge(gates_done, 1)
                d = G_hi[:, p] if isinstance(p, int) else G_hi[:, bass.ds(p, 1)].rearrange("p f n -> p (f n)")
                nc.scalar.copy(d, th[:, b]).then_inc(f_hi, 1)

            def third_of(third, last):
                act.wait_ge(n_sq, NORMS * third + 1)
                for j in range(KT):
                    split_hi(act, unit(third, j + SPLIT), lap_of(third, j + SPLIT), (j + SPLIT) % RAW)
                    act.wait_ge(w_used, unit(third, j) + 1)
                    evac(third, j, j % 2)
                act.wait_ge(f_nat, TILES * third + KT + 2)
                for n in range(3):
                    square(third, n, nat[:, n])
                for n in range(3):
                    act.wait_ge(n_x2, 3 * third + n + 1)
                    square(third, 3 + n, x2[:, n])
                for n in range(3):
                    for h in range(2):
                        act.wait_ge(n_gain, HALVES * third + 2 * n + h + 1)
                        nc.scalar.copy(m_hi[:, 4 * h:4 * h + 4, P * n:P * (n + 1)], nT[:, h]).then_inc(n_hi, 1)

                def in_lap(i, first, end):
                    for s in range(RAW):
                        u = KT + RAW * i + s
                        split_hi(act, unit(third, SPLIT) + u, lap_of(third, KT) + i + (s + SPLIT) // RAW, (s + SPLIT) % RAW,
                                 FK if end and s > 1 else KT)
                        p = 2 * i + s // 2
                        act.wait_ge(w_used, unit(third, 0) + u + 1)
                        if s % 2 == 0:
                            gate(third, p, s // 2)
                            if not (first and s == 0):
                                hi(third, p - 1, 1 - s // 2)
                in_lap(0, True, False)
                act.wait_ge(gates_done, 1)
                with act.Fori(1, IN_LAPS - 1) as i:
                    in_lap(i, False, False)
                in_lap(IN_LAPS - 1, False, True)
                hi(third, FT - 1, 1)

                def out_lap(i, end):
                    if not last:
                        mix_round(third + 1, i)
                    for s in range(RAW):
                        u = KT + 2 * FT + RAW * i + s
                        if not (last and end and s > 1):
                            split_hi(act, unit(third, SPLIT) + u, lap_of(third, KT + 2 * FT) + i + (s + SPLIT) // RAW, (s + SPLIT) % RAW,
                                     KT if end and s > 1 else FK)
                        act.wait_ge(w_used, unit(third, 0) + u + 1)
                        if s % 2:
                            evac(third, KT + 2 * i + s // 2, s // 2)

                for i in range(OUT_LAPS):
                    out_lap(i, i == OUT_LAPS - 1)
                act.wait_ge(f_nat, TILES * third + TILES + 2)
                for n in range(3):
                    square(third, 6 + n, nat[:, n])
            act.sem_inc(n_sq, 1)
            for r in range(4):
                mix_round(0, r)
            thirds_of(act, third_of)

        def pool_ffn(pool):
            def mix_round(third, r):
                pool.wait_ge(mix_hi, 4 * third + r + 1)
                nc.gpsimd.tensor_tensor(m_lo[:, 2 * r:2 * r + 2], mix_in[:, 2 * r:2 * r + 2], m_hi[:, 2 * r:2 * r + 2].bitcast(F32), ALU.subtract).then_inc(mix_lo, 1)

            def power(third, n):
                pool.wait_ge(n_var, NORMS * third + n + 1)
                nc.gpsimd.tensor_tensor(n_r[:, n:n + 1], n_v[:, n:n + 1], minus_half[:, 0:1], ALU.pow).then_inc(n_pow, 1)

            def lo(third, p, b):
                pool.wait_ge(f_hi, FT * third + p + 1)
                pool.wait_ge(gates_done, 1)
                h, l = (t[:, p] if isinstance(p, int) else t[:, bass.ds(p, 1)].rearrange("p f n -> p (f n)") for t in (G_hi, G_lo))
                nc.gpsimd.tensor_tensor(l, th[:, b], h.bitcast(F32), ALU.subtract).then_inc(f_lo, 1)

            def third_of(third, last):
                for j in range(KT):
                    split_lo(pool, unit(third, j + SPLIT), (j + SPLIT) % RAW)
                for n in range(6):
                    power(third, n)
                for n in range(3):
                    for h in range(2):
                        pool.wait_ge(n_hi, HALVES * third + 2 * n + h + 1)
                        m = (slice(None), slice(4 * h, 4 * h + 4), slice(P * n, P * (n + 1)))
                        nc.gpsimd.tensor_tensor(m_lo[m], nT[:, h], m_hi[m].bitcast(F32), ALU.subtract).then_inc(n_lo, 1)

                def in_lap(i, first, end):
                    for s in range(RAW):
                        split_lo(pool, unit(third, KT + SPLIT + s) + RAW * i, (s + SPLIT) % RAW, FK if end and s > 1 else KT)
                        if s % 2 == 0 and not (first and s == 0):
                            lo(third, 2 * i + s // 2 - 1, 1 - s // 2)
                in_lap(0, True, False)
                with pool.Fori(1, IN_LAPS - 1) as i:
                    in_lap(i, False, False)
                in_lap(IN_LAPS - 1, False, True)
                lo(third, FT - 1, 1)
                for i in range(OUT_LAPS):
                    if not last:
                        mix_round(third + 1, i)
                    for s in range(RAW):
                        end = i == OUT_LAPS - 1 and s > 1
                        if not (last and end):
                            split_lo(pool, unit(third, KT + 2 * FT + SPLIT + s + RAW * i), (s + SPLIT) % RAW, KT if end else FK)
                for n in range(6, 9):
                    power(third, n)
            pool.sem_inc(n_lo, 2)
            pool.sem_inc(f_lo, 2)
            for r in (0, 2):
                mix_round(0, r)
            thirds_of(pool, third_of)

        def dve_ffn(dve):
            def evac(third, c, b):
                O = TILES * third + c
                dve.wait_ge(f_turned, O + 3)
                col = c % KT if isinstance(c, int) else c - KT
                d = nat[:, :, P * col:P * (col + 1)] if isinstance(c, int) else nat[:, :, bass.ds(P * col, P)]
                nc.vector.tensor_scalar(d, PS[:, 6 + b, 0:TC].rearrange("p (n c) -> p n c", n=3), 1.0, None, ALU.mult).then_inc(f_nat, 1)

            def variance(third, n):
                dve.wait_ge(n_sq, NORMS * third + n + 2)
                nc.vector.tensor_scalar(n_v[:, n:n + 1], n_ss[:, n:n + 1], 1.0 / D, RMS_EPS, ALU.mult, ALU.add).then_inc(n_var, 1)

            def add_post(third, n, g):
                dve.wait_ge(n_pow, NORMS * third + 6 * g + n + 1)
                nc.vector.scalar_tensor_tensor(out=nat[:, n], in0=nat[:, n], scalar=n_r[:, 6 * g + n:6 * g + n + 1], in1=post[:, g],
                                               op0=ALU.mult, op1=ALU.mult).then_inc(n_post, 1)
                dve.wait_ge(n_post, 6 * third + 3 * g + n + 1)
                nc.vector.tensor_tensor(x2[:, n], x2[:, n], nat[:, n], ALU.add).then_inc(n_y if g else n_x2, 1)

            def swiglu(third, p, b):
                G = FT * third + p
                dve.wait_ge(f_th, G + 1)
                nc.vector.scalar_tensor_tensor(out=th[:, b], in0=th[:, b], scalar=1.0, in1=PS[:, 2 * b, 0:TC], op0=ALU.add, op1=ALU.mult).then_inc(f_v, 1)
                dve.wait_ge(f_v, G + 1)
                dve.wait_ge(w_used, unit(third, KT + 2) + 2 * p)
                nc.vector.scalar_tensor_tensor(out=th[:, b], in0=th[:, b], scalar=0.5, in1=PS[:, 2 * b + 1, 0:TC], op0=ALU.mult, op1=ALU.mult).then_inc(f_g, 1)

            def third_of(third, last):
                dve.wait_ge(n_y, 3 * third + 1)
                for j in range(KT):
                    evac(third, j, j % 2)
                for n in range(3):
                    variance(third, n)
                dve.wait_ge(x2_loaded, 48 * (third + 1))
                dve.wait_ge(post_loaded, 32)
                for n in range(3):
                    add_post(third, n, 0)
                for n in range(3):
                    variance(third, 3 + n)
                for n in range(3):
                    dve.wait_ge(n_pow, NORMS * third + 3 + n + 1)
                    nc.vector.tensor_scalar(nat[:, n], x2[:, n], n_r[:, 3 + n:4 + n], None, ALU.mult).then_inc(n_xs, 1)
                for n in range(3):
                    for h in range(2):
                        dve.wait_ge(n_turned, HALVES * third + 2 * n + h + 1)
                        dve.wait_ge(n_lo, HALVES * third + 2 * n + h + 1)
                        nc.vector.tensor_tensor(nT[:, h], PS[:, 2 * (n % 2) + h].rearrange("p (k c) -> p k c", k=4),
                                                cols[:, V_FFN, 4 * h:4 * h + 4].unsqueeze(2).broadcast_to([P, 4, P]), ALU.mult).then_inc(n_gain, 1)
                with dve.Fori(0, FT // 2) as i:
                    for b in range(2):
                        swiglu(third, 2 * i + b, b)
                for i in range(OUT_LAPS):
                    for c in (2 * i - 1, 2 * i):
                        if c >= 0:
                            evac(third, KT + c, c % 2)
                evac(third, TILES - 1, 1)
                for n in range(6, 9):
                    variance(third, n)
                for n in range(3):
                    add_post(third, n, 1)
            for x in (f_copied, f_turned, f_nat, f_g):
                dve.sem_inc(x, 2)
            dve.sem_inc(n_y, 1)
            for r in (1, 3):
                dve.wait_ge(mix_hi, r + 1)
                nc.vector.tensor_tensor(m_lo[:, 2 * r:2 * r + 2], mix_in[:, 2 * r:2 * r + 2], m_hi[:, 2 * r:2 * r + 2].bitcast(F32),
                                        ALU.subtract).then_inc(mix_lo, 1)
            thirds_of(dve, third_of)


        block = ctx.enter_context(nc.Block())

        @block.sync
        def _(sp):
            sp_norm(sp)
            end_phase(sp, 1)
            sp_memkv(sp)
            end_phase(sp, 2)
            sp_proj(sp)
            end_phase(sp, 3)
            sp_branch(sp, 0, lambda s: w_br_v[ORDER[1]][:, :, s * P:(s + 1) * P])
            end_phase(sp, 4)
            sp_mlstm(sp)
            sp_branch(sp, 1, lambda s: w_br_v[ORDER[2]][:, :, s * P:(s + 1) * P])
            end_phase(sp, 5)
            sp_xattn(sp)
            sp_branch(sp, 2, lambda s: w_out_v[:, :, s * P:(s + 1) * P])
            end_phase(sp, 6)
            sp_ffn(sp)

        @block.scalar
        def _(act):
            act_norm(act)
            end_phase(act, 1)
            act_memkv(act)
            end_phase(act, 2)
            act_proj(act)
            end_phase(act, 3)
            act_ln(act)
            act_branch(act, 0)
            end_phase(act, 4)
            act_mlstm(act)
            act_branch(act, 1)
            end_phase(act, 5)
            act_xattn(act)
            act_branch(act, 2)
            end_phase(act, 6)
            act_ffn(act)

        @block.gpsimd
        def _(pool):
            pool_norm(pool)
            end_phase(pool, 1)
            pool_memkv(pool)
            end_phase(pool, 2)
            pool_proj(pool)
            end_phase(pool, 3)
            clear_early(pool)
            pool_ln(pool)
            pool_branch(pool, 0)
            end_phase(pool, 4)
            pool_mlstm(pool)
            pool_branch(pool, 1)
            end_phase(pool, 5)
            pool_xattn(pool)
            pool_branch(pool, 2)
            end_phase(pool, 6)
            pool_ffn(pool)

        @block.vector
        def _(dve):
            dve_norm(dve)
            end_phase(dve, 1)
            dve_memkv(dve)
            end_phase(dve, 2)
            dve_proj(dve)
            end_phase(dve, 3)
            dve_ln(dve)
            dve_branch(dve, 0)
            end_phase(dve, 4)
            dve_mlstm(dve)
            dve_branch(dve, 1)
            end_phase(dve, 5)
            dve_xattn(dve)
            dve_branch(dve, 2)
            end_phase(dve, 6)
            dve_ffn(dve)

        @block.tensor
        def _(pe):
            pe_norm(pe)
            end_phase(pe, 1)
            pe_memkv(pe)
            end_phase(pe, 2)
            pe_proj(pe)
            end_phase(pe, 3)
            pe_branch(pe, 0, ln_lo, 3)
            end_phase(pe, 4)
            pe_mlstm(pe)
            pe_branch(pe, 1, ml_lo, 2 * NT + 2)
            end_phase(pe, 5)
            pe_xattn(pe)
            pe_branch(pe, 2, xa_lo, 2 * NT)
            end_phase(pe, 6)
            pe_ffn(pe)


_INS = ["x_prompt", "x_sample", "mem_prompt", "state_mlstm_c", "state_mlstm_n", "state_mlstm_m", "state_conv",
        "cache_mem_k", "cache_mem_v", "norm_mix_pre", "norm_mix_post", "norm_ffn_pre", "norm_ffn_post", "w_in",
        "b_gate", "mlstm_head_norm", "conv_w", "conv_b", "conv_ln_g", "conv_ln_b", "mem_norm", "w_mem_kv",
        "w_branch", "w_out", "w_ffn_in", "w_ffn_out"]
_OUTS = [("y_prompt", (1, SEQ, D)), ("y_sample", (NB, TS, D)), ("p_c", (1, 1, H, DH, DH)), ("p_n", (1, 1, H, DH)),
         ("p_m", (1, 1, H)), ("p_conv", (1, 1, CB, D)), ("p_mem_k", (1, 1, MEM, H, DH)),
         ("p_mem_v", (1, 1, MEM, H, DH)), ("s_c", (1, NB, H, DH, DH)), ("s_n", (1, NB, H, DH)), ("s_m", (1, NB, H)),
         ("s_conv", (1, NB, CB, D))]


def kernel(**inputs):
    import numpy as _np
    import concourse.bacc as _bacc
    from concourse.bass_utils import run_bass_kernel_spmd as _run

    nc = _bacc.Bacc("TRN2", target_bir_lowering=False, num_devices=1)
    arrays, ins, outs = {}, {}, {}
    for name in _INS:
        x = _np.ascontiguousarray(inputs[name])
        arrays[f"in_{name}"] = x
        ins[name] = nc.dram_tensor(f"in_{name}", x.shape, mybir.dt.from_np(x.dtype), kind="ExternalInput").ap()
    for name, shape in _OUTS:
        outs[name] = nc.dram_tensor(f"out_{name}", shape, F32, kind="ExternalOutput").ap()
    hybrid_step(nc, ins, outs)
    r = _run(nc, [arrays], core_ids=[0])
    return tuple(r.results[0][f"out_{name}"] for name, _ in _OUTS)
```

```python
from contextlib import ExitStack

import concourse.bass as bass
from concourse import mybir

F32 = mybir.dt.float32
F32R = mybir.dt.float32r
ACT = mybir.ActivationFunctionType
ALU = mybir.AluOpType
AX_X = mybir.AxisListType.X

P = 128
D = 1024
KT = D // P
SEQ = 1024
NB, TS = 8, 16
NTOK = SEQ + NB * TS
NT = NTOK // P
NPT = SEQ // P
TC = NTOK // 3
H, DH = 4, 256
MEM = 256
CW = 31
CB = CW - 1
DFF = 2816
FT = DFF // P
FK = FT // 2
RMS_EPS, LN_EPS = 1e-6, 1e-5
BIG = 1e30
NSEG = NPT + NB

RAW, SPLIT = 4, 2
GA, GB, QQ, KK, VV, OO, XQ, GT = 0, 8, 16, 24, 32, 40, 48, 56
NPROJ = 80
COLS = ((0, 16, 4104), (16, 32, 0), (48, 32, 6152))
IF_COL = 4096
V_MIX, V_FFN, V_MEM, V_HEAD, V_CB, V_LG, V_LB = range(7)
U_PROJ = 2 * KT
U_BR = U_PROJ + NPROJ
U_TH = U_BR + 3 * KT
TH_UNITS = KT + 2 * FT + 2 * KT
CONV, MLSTM, XATT = 1, 0, 2


class Steps:

    def __init__(self, eng, sem):
        self.eng, self.sem, self.base, self.n = eng, sem, 0, 0

    def mark(self, ins):
        ins.then_inc(self.sem, 1)
        self.n += 1

    def wait(self, back=0):
        self.eng.wait_ge(self.sem, self.base + self.n - back)

    def link(self, ins):
        self.mark(ins)
        self.wait()

    def enter(self, i, per):
        self.saved = (self.base, self.n, per)
        self.base, self.n = self.base + self.n + per * i, 0

    def leave(self, trips):
        base, n, per = self.saved
        assert self.n == per, (self.n, per)
        self.base, self.n = base, n + per * trips


def hybrid_step(nc, a, o):
    ctx = ExitStack()
    with ctx:
        def sb(name, shape, dt=F32, scope=ctx):
            return scope.enter_context(nc.sbuf_tensor(name, shape, dt))

        def sem(name):
            return ctx.enter_context(nc.semaphore(name))

        A_hi, A_lo = sb("A_hi", [P, KT, NTOK], F32R), sb("A_lo", [P, KT, NTOK], F32R)
        w_raw = sb("w_raw", [P, RAW, FK, P])
        w_hi, w_lo = sb("w_hi", [P, SPLIT, FK, P], F32R), sb("w_lo", [P, SPLIT, FK, P], F32R)
        ident = sb("ident", [P, P])
        mean_mat = sb("mean_mat", [P, P])
        sel = sb("sel", [H, H, P])
        later = sb("later", [P, 2, P])
        minus_half = sb("minus_half", [P, H])
        ln_eps = sb("ln_eps", [P, 1])
        own = sb("own", [P, NB])
        cols = sb("cols", [P, 7, KT])
        taps = sb("taps", [P, CW, KT])
        gate_cols = sb("gate_cols", [P, NT, 4, H])
        keep_b = sb("keep_b", [P, H, NSEG])
        M_rows = sb("M_rows", [H, NTOK])
        keep_r = sb("keep_r", [H, NSEG])
        PS = ctx.enter_context(nc.psum_tensor("PS", [P, 8, 512], F32))

        u_tail = sb("u_tail", [P, KT, CB + P])

        s_early = ExitStack()
        stage = sb("stage", [P, 2, NTOK], F32, s_early)
        hist_T = sb("hist_T", [P, KT, NB, CB], F32, s_early)
        wif = sb("wif", [P, KT, P], F32, s_early)
        wif_hi, wif_lo = sb("wif_hi", [P, KT, P], F32R, s_early), sb("wif_lo", [P, KT, P], F32R, s_early)
        s_norm = ExitStack()
        x_in = sb("x_in", [P, 2, D], F32, s_norm)
        sq = sb("sq", [P, D], F32, s_norm)
        x_s = sb("x_s", [P, 2, D], F32, s_norm)
        x_ss = sb("x_ss", [P, 2], F32, s_norm)
        x_r0 = sb("x_r0", [P, 2], F32, s_norm)
        x_r = sb("x_r", [P, 2], F32, s_norm)
        x_T = sb("x_T", [P, 2, 4, P], F32, s_norm)
        vec_in = sb("vec_in", [7 * KT, P], F32, s_norm)
        tap_in = sb("tap_in", [124, 2, P], F32, s_norm)
        hist_in = stage[0:4 * CB, :, 0:D]
        mem_hi, mem_lo = sb("mem_hi", [P, KT, MEM], F32R, s_norm), sb("mem_lo", [P, KT, MEM], F32R, s_norm)
        kv_T = sb("kv_T", [P, 2, MEM], F32, s_norm)
        kv_nat = sb("kv_nat", [P, 2, 2, P], F32, s_norm)
        s_norm.close()
        s_gate = ExitStack()
        g_i = sb("g_i", [H, NTOK], F32, s_gate)
        g_f = sb("g_f", [H, NTOK], F32, s_gate)
        g_a = sb("g_a", [H, NTOK], F32, s_gate)
        g_b = sb("g_b", [H, NTOK], F32, s_gate)
        restart_mul = sb("restart_mul", [H, NTOK], F32, s_gate)
        restart_add = sb("restart_add", [H, NTOK], F32, s_gate)
        g_rows = sb("g_rows", [P, NTOK], F32, s_gate)
        g_bias = sb("g_bias", [P, 2], F32, s_gate)
        m_prev = sb("m_prev", [H, NSEG], F32, s_gate)
        m_new = sb("m_new", [H, NSEG], F32, s_gate)
        b_last = sb("b_last", [H, NSEG], F32, s_gate)
        M_last = sb("M_last", [H, NSEG], F32, s_gate)
        s_gate.close()
        s_conv = ExitStack()
        glu = sb("glu", [P, 2, 2, NTOK], F32, s_conv)
        EXT = CB + SEQ + NB * (CB + TS)
        ext = sb("ext", [P, 2, EXT], F32, s_conv)
        c_out = sb("c_out", [P, 2, NTOK], F32, s_conv)
        s_conv.close()
        s_early.close()
        s_ml = ExitStack()
        E1 = DH + 1
        v1 = sb("v1", [P, H, E1], F32, s_ml)
        oy = sb("oy", [P, 2, H, DH], F32, s_ml)
        kw = sb("kw", [P, H, DH], F32, s_ml)
        decay = sb("decay", [P, H, P], F32, s_ml)
        sT = sb("sT", [P, H, P], F32, s_ml)
        num = sb("num", [P, H, E1], F32, s_ml)
        C_T = sb("C_T", [P, H, 2, E1], F32, s_ml)
        q_in, k_in = sb("q_in", [P, 2, KT, P], F32, s_ml), sb("k_in", [P, 2, KT, P], F32, s_ml)
        v_in, o_in = sb("v_in", [P, KT, P], F32, s_ml), sb("o_in", [P, KT, P], F32, s_ml)
        y_T = sb("y_T", [P, 2, 4, P], F32, s_ml)
        den, rden, ssq, hr0, hr, hs = (sb(n, [P, H], F32, s_ml) for n in ("den", "rden", "ssq", "hr0", "hr", "hs"))
        qm = sb("qm", [P, 2, NB * (P + TS)], F32, s_ml)
        Cb_T = sb("Cb_T", [P, 2, 2, E1], F32, s_ml)
        v_own = sb("v_own", [P, 2, DH], F32, s_ml)
        n_in = y_T[0:NB * H, 0, 0:2].rearrange("p k c -> p (k c)")
        n_T = sb("n_T", [P, 2, NB * H], F32, s_ml)
        n_cols = sb("n_cols", [P, KT], F32, s_ml)
        n_row = o_in[0:KT, 0]
        keep8 = sb("keep8", [NB, H], F32, s_ml)
        s_ml.close()
        s_ff = ExitStack()
        x2 = sb("x2", [P, 3, D], F32, s_ff)
        nat = sb("nat", [P, 3, D], F32, s_ff)
        post = sb("post", [P, 2, D], F32, s_ff)
        m_hi, m_lo = sb("m_hi", [P, KT, TC], F32R, s_ff), sb("m_lo", [P, KT, TC], F32R, s_ff)
        mix_in = sb("mix_in", [P, KT, TC], F32, s_ff)
        ff_tmp = sb("ff_tmp", [P, 4, TC], F32, s_ff)
        n_ss, n_v, n_r = (sb(n, [P, 9], F32, s_ff) for n in ("n_ss", "n_v", "n_r"))
        oT, th = ff_tmp[:, 0:2], ff_tmp[:, 2:4]
        n_junk = ff_tmp[:].rearrange("p a n -> p (a n)")[:, 0:D]
        nT = u_tail[:].rearrange("p k n -> p (k n)")[:, 0:D].rearrange("p (n k c) -> p n k c", n=2, k=4)
        s_ff.close()
        s_xa = ExitStack()
        prob = sb("prob", [P, 2, H, MEM], F32, s_xa)
        prob_T = sb("prob_T", [P, 2, 2, H, P], F32, s_xa)
        xa_T = sb("xa_T", [P, 2, 4, P], F32, s_xa)
        cache_in = sb("cache_in", [P, 4, 2, D], F32, s_xa)
        xqm = prob_T[:].rearrange("p b m h j -> p b (m h) j")
        smax, ssum, rsum = (sb(n, [P, 2, H], F32, s_xa) for n in ("smax", "ssum", "rsum"))
        xq_in = sb("xq_in", [P, 2, KT, P], F32, s_xa)
        mk_T, mv = sb("mk_T", [P, KT, MEM], F32, s_xa), sb("mv", [P, 2, D], F32, s_xa)
        s_xa.close()
        s_br = ExitStack()
        gate_in = sb("gate_in", [P, 2, NTOK], F32, s_br)
        part_out = sb("part_out", [P, 2, NTOK], F32, s_br)
        s_ln = ExitStack()
        cT = sb("cT", [P, KT, NTOK], F32, s_ln)
        ln_x = sb("ln_x", [P, KT, TC], F32, s_ln)
        ln_r = sb("ln_r", [P, TC], F32, s_ln)
        ln_sum = sb("ln_sum", [P, TC], F32, s_ln)
        s_ln.close()
        prev_in = sb("prev_in", [P, 2, NTOK], F32, s_br)
        s_br.close()

        proj_d = nc.dram_tensor("proj_d", (NPROJ, P, NTOK), F32, kind="Internal").ap()
        conv_d = nc.dram_tensor("conv_d", (KT, P, NTOK), F32, kind="Internal").ap()
        kvT_d = nc.dram_tensor("kvT_d", (2 * KT, P, MEM), F32, kind="Internal").ap()
        part_d = nc.dram_tensor("part_d", (KT, P, NTOK), F32, kind="Internal").ap()


        early_sems = ExitStack()
        early = []

        def early_sem(name):
            early.append(early_sems.enter_context(nc.semaphore(name)))
            return early[-1]

        def clear_early(eng):
            eng.sem_clear(range(min(x.num for x in early), max(x.num for x in early) + 1))

        w_loaded = [sem(f"w_loaded{s}") for s in range(RAW)]
        w_hi_done, w_lo_done, w_used = sem("w_hi_done"), sem("w_lo_done"), sem("w_used")
        phase_done = sem("phase_done")
        act_steps, dve_steps, pool_steps = sem("act_steps"), sem("dve_steps"), sem("pool_steps")
        st = {}

        w_in_v = a["w_in"][0].rearrange("(k p) c -> p k c", p=P)
        w_kv_v = a["w_mem_kv"][0].rearrange("(k p) c -> p k c", p=P)
        w_br_v = a["w_branch"][0].rearrange("b (k p) c -> b p k c", p=P)
        w_out_v = a["w_out"][0].rearrange("(k p) c -> p k c", p=P)
        w_fi_v = a["w_ffn_in"][0].rearrange("(k p) c -> p k c", p=P)
        w_fo_v = a["w_ffn_out"][0].rearrange("(z k p) c -> z p k c", p=P, k=FK)

        def load_w(sp, u, s, src, kt=KT):
            if not isinstance(u, int) or u >= RAW:
                sp.wait_ge(w_lo_done, u - RAW + 1)
            sp.dma_start(w_raw[:, s, 0:kt], src).then_inc(w_loaded[s], 16)

        def split_hi(act, u, lap, s, kt=KT):
            act.wait_ge(w_loaded[s], 16 * (lap + 1))
            if not isinstance(u, int) or u >= SPLIT:
                act.wait_ge(w_used, u - SPLIT + 1)
            nc.scalar.copy(w_hi[:, s % SPLIT, 0:kt], w_raw[:, s, 0:kt]).then_inc(w_hi_done, 1)

        def split_lo(pool, u, s, kt=KT):
            pool.wait_ge(w_hi_done, u + 1)
            nc.gpsimd.tensor_tensor(w_lo[:, s % SPLIT, 0:kt], w_raw[:, s, 0:kt],
                                    w_hi[:, s % SPLIT, 0:kt].bitcast(F32), ALU.subtract).then_inc(w_lo_done, 1)

        def product(outs, wh, wl, mh, ml, kt, start=True, stop=True):
            for k in range(kt):
                for n, (w, m) in enumerate(((wh, mh), (wh, ml), (wl, mh))):
                    for c, out in enumerate(outs):
                        last = nc.tensor.matmul(out, w[:, k], m(k, c), start=start and k == 0 and n == 0,
                                                stop=stop and k == kt - 1 and n == 2)
            return last

        def use_unit(pe, u, s, outs, mh, ml, kt=KT, start=True, stop=True):
            pe.wait_ge(w_lo_done, u + 1)
            product(outs, w_hi[:, s % SPLIT], w_lo[:, s % SPLIT], mh, ml, kt, start, stop).then_inc(w_used, 1)

        def end_phase(eng, n):
            eng.drain().then_inc(phase_done, 1)
            eng.wait_ge(phase_done, 5 * n)

        wif_lo_done = sem("wif_lo_done")

        vec_loaded, tap_loaded, hist_loaded, wif_loaded = (early_sem(n) for n in ("vec_loaded", "tap_loaded", "hist_loaded", "wif_loaded"))
        consts_ready, vec_T, vec_copied, hist_Tr = (early_sem(n) for n in ("consts_ready", "vec_T", "vec_copied", "hist_Tr"))
        wif_zero, wif_hi_done = early_sem("wif_zero"), early_sem("wif_hi_done")
        x_loaded = [early_sem("x_loaded0"), early_sem("x_loaded1")]
        x_sq, x_scaled, x_turned, x_gained, x_hi, x_lo = (early_sem(n) for n in ("x_sq", "x_scaled", "x_turned", "x_gained", "x_hi", "x_lo"))
        x_var, x_rstd, x_lo0 = early_sem("x_var"), early_sem("x_rstd"), early_sem("x_lo0")
        kv_copied, kv_turned, kv_nat_ready = early_sem("kv_copied"), early_sem("kv_turned"), early_sem("kv_nat_ready")
        kvT_stored = [early_sem("kvT_stored0"), early_sem("kvT_stored1")]
        kv_stored = [early_sem("kv_stored0"), early_sem("kv_stored1")]
        NKV = 2 * KT
        N_IN = NT + MEM // P
        FIRST = MEM // P + 1

        def kv_steps(eng, body):
            for s in range(RAW):
                body(s, 0, s)
            with eng.Fori(1, NKV // RAW) as i:
                for s in range(RAW):
                    body(RAW * i + s, i, s)

        def norm_tile(lap, s):
            return 2 * lap + FIRST + s // 2, (FIRST + s // 2) % 2
        x_src = a["x_prompt"][0].rearrange("(t p) d -> t p d", p=P)
        s_src = a["x_sample"].rearrange("b t d -> (b t) d")
        m_src = a["mem_prompt"][0].rearrange("(t p) d -> t p d", p=P)

        def sp_norm(sp):
            for s in range(RAW):
                load_w(sp, s, s, w_kv_v[:, :, s * P:(s + 1) * P])
            for t in range(2):
                sp.dma_start(x_in[:, t], m_src[t]).then_inc(x_loaded[t], 16)
            for v, name in enumerate(("norm_mix_pre", "norm_ffn_pre", "mem_norm", "mlstm_head_norm",
                                      "conv_b", "conv_ln_g", "conv_ln_b")):
                sp.dma_start(vec_in[v * KT:(v + 1) * KT, :], a[name][0].rearrange("(k p) -> k p", p=P)).then_inc(vec_loaded, 16)
            sp.dma_start(tap_in[:], a["conv_w"][0].rearrange("w (k p) -> (w k) p", p=P)
                         .rearrange("(g r) p -> r g p", g=2)).then_inc(tap_loaded, 16)
            sp.dma_start(hist_in, a["state_conv"][0].rearrange("(g b) r c -> (b r) g c", g=2)).then_inc(hist_loaded, 16)
            sp.wait_ge(wif_zero, 1)
            for g in range(2):
                sp.dma_start(wif[:, :, 32 * g:32 * g + H], w_in_v[:, :, IF_COL + H * g:IF_COL + H * (g + 1)]).then_inc(wif_loaded, 16)

            def load_x(t, b, src):
                sp.wait_ge(x_scaled, t - 1)
                sp.dma_start(x_in[:, b], src).then_inc(x_loaded[b], 16)
            load_x(2, 0, s_src)
            load_x(3, 1, x_src[0])
            mk, mv = (o[n][0, 0].rearrange("(z m) h d -> m z (h d)", m=P) for n in ("p_mem_k", "p_mem_v"))

            def store_kv(e):
                sp.wait_ge(kv_nat_ready, e + 1)
                sp.dma_start((mk, mv)[e // KT][:, :, P * (e % KT):P * (e % KT + 1)], kv_nat[:, e % 2]).then_inc(kv_stored[e % 2], 16)
            for j in range(NKV):
                u = j + RAW
                src = (w_kv_v[:, :, u * P:(u + 1) * P] if u < NKV else
                       w_in_v[:, :, COLS[0][2] + (u - NKV) * P:COLS[0][2] + (u - NKV + 1) * P])
                load_w(sp, u, u % RAW, src)
                t = FIRST + j // 2 + 1
                if j % 2 == 0 and t < N_IN:
                    load_x(t, t % 2, x_src[t - FIRST])
                if j:
                    store_kv(j - 1)
            store_kv(NKV - 1)
            for b in range(2):
                sp.wait_ge(kv_stored[b], 16 * NKV // 2)

        def pool_norm(pool):
            steps = st["pool"] = Steps(pool, pool_steps)
            pool.sem_inc(x_lo, 1)
            steps.mark(nc.gpsimd.memset(wif[:], 0.0))
            pool.wait_ge(pool_steps, 1)
            pool.sem_inc(wif_zero, 1)
            for t, v in ((ident[:], 0.0), (sel[:], 0.0), (later[:], 0.0), (own[:], 1.0), (minus_half[:], -0.5), (ln_eps[:], LN_EPS)):
                steps.mark(nc.gpsimd.memset(t, v))
            steps.wait()
            steps.mark(nc.gpsimd.affine_select(out=ident[:], in_=ident[:], compare_op=ALU.not_equal, fill=1.0, base=0,
                                               pattern=[[-1, P]], channel_multiplier=1))
            steps.mark(nc.gpsimd.affine_select(out=sel[:], in_=sel[:], compare_op=ALU.not_equal, fill=1.0, base=0,
                                               pattern=[[-1, H], [0, P]], channel_multiplier=1))
            for g in range(2):
                steps.mark(nc.gpsimd.affine_select(out=later[:, g], in_=later[:, g], compare_op=ALU.is_ge, fill=BIG, base=0,
                                                   pattern=[[1, P]], channel_multiplier=-1))
            steps.mark(nc.gpsimd.affine_select(out=own[:], in_=own[:], compare_op=ALU.is_ge, fill=0.0, base=0,
                                               pattern=[[-TS, NB]], channel_multiplier=1))
            steps.wait()
            v = later[:, 1].rearrange("p (b r) -> p b r", b=NB)
            steps.mark(nc.gpsimd.affine_select(out=v, in_=v, compare_op=ALU.is_ge, fill=BIG, base=0,
                                               pattern=[[-TS, NB], [0, TS]], channel_multiplier=1))
            steps.mark(nc.gpsimd.affine_select(out=own[:], in_=own[:], compare_op=ALU.is_ge, fill=0.0, base=TS - 1,
                                               pattern=[[TS, NB]], channel_multiplier=-1))
            steps.wait()
            pool.sem_inc(consts_ready, 1)
            for s in range(SPLIT):
                split_lo(pool, s, s)
            pool.wait_ge(wif_hi_done, 1)
            nc.gpsimd.tensor_tensor(wif_lo[:], wif[:], wif_hi[:].bitcast(F32), ALU.subtract).then_inc(wif_lo_done, 1)

            def lo(t, dst):
                pool.wait_ge(x_hi, 2 * t + 2)
                d_hi, d_lo = dst(1)
                pool.wait_ge(consts_ready, 1)
                nc.gpsimd.tensor_tensor(d_lo, x_T[:, 1], d_hi.bitcast(F32), ALU.subtract).then_inc(x_lo, 1)

            def rstd(t, b):
                pool.wait_ge(x_var, t + 1)
                nc.gpsimd.tensor_tensor(x_r[:, b:b + 1], x_r0[:, b:b + 1], minus_half[:, 0:1], ALU.pow).then_inc(x_rstd, 1)
            rstd(0, 0)
            for t in range(1, FIRST):
                rstd(t, t % 2)
                lo(t - 1, lambda h: norm_dst(t - 1, h))

            def body(j, lap, s):
                if s % 2 == 0:
                    t, b = norm_tile(lap, s)
                    rstd(t, b)
                    lo(t - 1, lambda h: norm_dst(t - 1, h))
                split_lo(pool, j + SPLIT, (s + SPLIT) % RAW)
            kv_steps(pool, body)
            lo(N_IN - 1, lambda h: norm_dst(N_IN - 1, h))

        def norm_dst(t, h):
            ks = slice(4 * h, 4 * h + 4)
            if isinstance(t, int) and t < FIRST - 1:
                return mem_hi[:, ks, P * t:P * (t + 1)], mem_lo[:, ks, P * t:P * (t + 1)]
            if isinstance(t, int) and t == FIRST - 1:
                return A_hi[:, ks, SEQ:NTOK], A_lo[:, ks, SEQ:NTOK]
            c = P * (t - FIRST)
            c = slice(c, c + P) if isinstance(t, int) else bass.ds(c, P)
            return A_hi[:, ks, c], A_lo[:, ks, c]

        def act_norm(act):
            st["act"] = Steps(act, act_steps)
            split_hi(act, 0, 0, 0)
            split_hi(act, 1, 0, 1)
            act.wait_ge(wif_loaded, 32)
            nc.scalar.copy(wif_hi[:], wif[:]).then_inc(wif_hi_done, 1)

            def square(t, b, lap):
                act.wait_ge(x_loaded[b], 16 * (lap + 1))
                if not isinstance(t, int) or t:
                    act.wait_ge(x_sq, t)
                if not isinstance(t, int) or t > 1:
                    act.wait_ge(x_scaled, t - 1)
                act.wait_ge(wif_hi_done, 1)
                nc.scalar.activation(sq[:], x_in[:, b], ACT.Square, accum_out=x_ss[:, b:b + 1]).then_inc(x_sq, 1)

            def hi(t, dst):
                for h in range(2):
                    act.wait_ge(x_gained, 2 * t + h + 1)
                    act.wait_ge(wif_hi_done, 1)
                    nc.scalar.copy(dst(h), x_T[:, h]).then_inc(x_hi, 1)
            square(0, 0, 0)
            for t in range(1, FIRST):
                square(t, t % 2, t // 2)
                hi(t - 1, lambda h: norm_dst(t - 1, h)[0])

            def body(j, lap, s):
                if s % 2 == 0:
                    t, b = norm_tile(lap, s)
                    square(t, b, lap + (FIRST + s // 2) // 2)
                    hi(t - 1, lambda h: norm_dst(t - 1, h)[0])
                split_hi(act, j + SPLIT, lap + (s + SPLIT) // RAW, (s + SPLIT) % RAW)
                act.wait_ge(w_used, j + 1)
                if not isinstance(j, int) or j > 1:
                    act.wait_ge(kv_turned, j - 1)
                    act.wait_ge(kvT_stored[s % 2], 16 * (2 * lap + s // 2))
                nc.scalar.copy(kv_T[:, s % 2], PS[:, 4 + s % 2, 0:MEM]).then_inc(kv_copied, 1)
                act.wait_ge(kv_copied, j + 1)
                dst = kvT_d[j] if isinstance(j, int) else kvT_d[bass.ds(j, 1)].rearrange("a p m -> (a p) m")
                act.dma_start(dst, kv_T[:, s % 2]).then_inc(kvT_stored[s % 2], 16)
            kv_steps(act, body)
            hi(N_IN - 1, lambda h: norm_dst(N_IN - 1, h)[0])
            for b in range(2):
                act.wait_ge(kvT_stored[b], 16 * NKV // 2)

        def pe_norm(pe):
            pe.wait_ge(consts_ready, 1)
            pe.wait_ge(vec_loaded, 7 * 16)
            nc.tensor.transpose(PS[:, 5, 0:7 * KT], vec_in[:], ident[0:7 * KT, 0:7 * KT])
            pe.wait_ge(tap_loaded, 16)
            for g in range(2):
                last = nc.tensor.transpose(PS[:, 5, 64 + 124 * g:188 + 124 * g], tap_in[:, g], ident[0:124, 0:124])
            last.then_inc(vec_T, 1)
            pe.wait_ge(hist_loaded, 16)
            for n, bank in enumerate((6, 7, 4, 5)):
                if bank == 5:
                    pe.wait_ge(vec_copied, 1)
                for q in range(4):
                    k = 4 * (n % 2) + q
                    last = nc.tensor.transpose(PS[:, bank, 120 * q:120 * (q + 1)], hist_in[:, n // 2, k * P:(k + 1) * P], ident[0:120, 0:120])
                last.then_inc(hist_Tr, 1)

            def turn(t, b):
                pe.wait_ge(x_scaled, t + 1)
                for h in range(2):
                    if not isinstance(t, int) or t > 1:
                        pe.wait_ge(x_gained, 2 * (t - 2) + h + 1)
                    for q in range(4):
                        last = nc.tensor.transpose(PS[:, 2 * b + h, P * q:P * (q + 1)], x_s[:, b, P * (4 * h + q):P * (4 * h + q + 1)], ident[:])
                    last.then_inc(x_turned, 1)
            turn(0, 0)
            turn(1, 1)

            def kv_turn(j, b):
                pe.wait_ge(kv_copied, j + 1)
                if not isinstance(j, int) or j > 1:
                    pe.wait_ge(kv_nat_ready, j - 1)
                for z in range(2):
                    last = nc.tensor.transpose(PS[:, 6 + b, P * z:P * (z + 1)], kv_T[:, b, P * z:P * (z + 1)], ident[:])
                last.then_inc(kv_turned, 1)

            def body(j, lap, s):
                if s % 2 == 0:
                    t, b = norm_tile(lap, s)
                    turn(t - 1, 1 - b)
                if not isinstance(j, int) or j > 1:
                    pe.wait_ge(kv_copied, j - 1)
                use_unit(pe, j, s, [PS[:, 4 + s % 2, 0:MEM]], lambda k, c: mem_hi[:, k], lambda k, c: mem_lo[:, k])
                if not isinstance(j, int) or j > 0:
                    kv_turn(j - 1, (s + 1) % 2)
            pe.wait_ge(x_lo0, FIRST)
            pe.wait_ge(x_lo, FIRST)
            kv_steps(pe, body)
            kv_turn(NKV - 1, 1)
            turn(N_IN - 1, (N_IN - 1) % 2)

        def dve_norm(dve):
            steps = st["dve"] = Steps(dve, dve_steps)
            steps.mark(nc.vector.memset(mean_mat[:], 1.0 / D))
            dve.wait_ge(vec_T, 1)
            steps.mark(nc.vector.tensor_copy(cols[:].rearrange("p v k -> p (v k)"), PS[:, 5, 0:7 * KT]))
            nc.vector.tensor_copy(taps[:].rearrange("p w k -> p (w k)"), PS[:, 5, 64:64 + CW * KT]).then_inc(vec_copied, 1)
            dve.wait_ge(vec_copied, 1)
            steps.mark(nc.vector.tensor_scalar(cols[:, V_HEAD], cols[:, V_HEAD], 0.25, None, ALU.mult))
            steps.mark(nc.vector.tensor_scalar(cols[:, V_LG:V_LB + 1], cols[:, V_LG:V_LB + 1], 0.25, None, ALU.mult))
            for n, bank in enumerate((6, 7, 4, 5)):
                dve.wait_ge(hist_Tr, n + 1)
                g, k = n // 2, 4 * (n % 2)
                steps.mark(nc.vector.tensor_copy(hist_T[:, k:k + 4, 4 * g:4 * g + 4].rearrange("p k b r -> p k (b r)"),
                                                 PS[:, bank, 0:480].rearrange("p (k r) -> p k r", k=4)))

            def scale(t, b):
                dve.wait_ge(x_sq, t + 1)
                nc.vector.tensor_scalar(x_r0[:, b:b + 1], x_ss[:, b:b + 1], 1.0 / D, RMS_EPS, ALU.mult, ALU.add).then_inc(x_var, 1)
                dve.wait_ge(x_rstd, t + 1)
                if not isinstance(t, int) or t > 1:
                    dve.wait_ge(x_turned, 2 * (t - 1))
                nc.vector.tensor_scalar(x_s[:, b], x_in[:, b], x_r[:, b:b + 1], None, ALU.mult).then_inc(x_scaled, 1)

            def gain(t, b, v):
                for h in range(2):
                    dve.wait_ge(x_turned, 2 * t + h + 1)
                    dve.wait_ge(x_lo if h else x_lo0, t + 1)
                    nc.vector.tensor_tensor(x_T[:, h], PS[:, 2 * b + h].rearrange("p (k c) -> p k c", k=4),
                                            cols[:, v, 4 * h:4 * h + 4].unsqueeze(2).broadcast_to([P, 4, P]),
                                            ALU.mult).then_inc(x_gained, 1)

            def lo(t, d_hi, d_lo):
                dve.wait_ge(x_hi, 2 * t + 1)
                nc.vector.tensor_tensor(d_lo, x_T[:, 0], d_hi.bitcast(F32), ALU.subtract).then_inc(x_lo0, 1)
            dve.sem_inc(x_lo0, 1)
            scale(0, 0)
            for t in range(1, FIRST):
                scale(t, t % 2)
                gain(t - 1, (t - 1) % 2, V_MEM)
                lo(t - 1, *norm_dst(t - 1, 0))

            def kv_out(e, b, before):
                dve.wait_ge(kv_turned, e + 1)
                if not isinstance(e, int) or e > 1:
                    dve.wait_ge(kv_stored[b], 16 * before)
                nc.vector.tensor_copy(kv_nat[:, b].rearrange("p z c -> p (z c)"), PS[:, 6 + b, 0:MEM]).then_inc(kv_nat_ready, 1)

            def body(j, lap, s):
                if s % 2 == 0:
                    t, b = norm_tile(lap, s)
                    scale(t, b)
                    gain(t - 1, 1 - b, V_MIX)
                    lo(t - 1, *norm_dst(t - 1, 0))
                if not isinstance(j, int) or j > 0:
                    kv_out(j - 1, (s + 1) % 2, 2 * lap + (s - 1) // 2)
            kv_steps(dve, body)
            kv_out(NKV - 1, 1, NKV // 2 - 1)
            gain(N_IN - 1, (N_IN - 1) % 2, V_MIX)
            lo(N_IN - 1, *norm_dst(N_IN - 1, 0))

        state_m_loaded, wif_used, gate_read = sem("state_m_loaded"), sem("wif_used"), sem("gate_read")
        g_dve, g_act, gate_turned, gates_done, m_stored = sem("g_dve"), sem("g_act"), sem("gate_turned"), sem("gates_done"), sem("m_stored")
        p_copied = sem("p_copied")
        stage_stored = [sem("stage_stored0"), sem("stage_stored1")]
        glu_loaded, c_stored = [sem("glu_loaded0"), sem("glu_loaded1")], [sem("c_stored0"), sem("c_stored1")]
        conv_done = sem("conv_done")
        cT_loaded, tail_turned, tail_read, tail_stored, hist_moved = sem("cT_loaded"), sem("tail_turned"), sem("tail_read"), sem("tail_stored"), sem("hist_moved")
        ln_mean, ln_centred, ln_sq, ln_var, ln_std, ln_scaled, ln_z, ln_tanh, ln_y, ln_hi, ln_lo = (
            sem(n) for n in ("ln_mean", "ln_centred", "ln_sq", "ln_var", "ln_std", "ln_scaled", "ln_z", "ln_tanh", "ln_y", "ln_hi", "ln_lo"))
        tail_p, tail_s = part_out[0:CB, 0, 0:D], part_out[:, 1, 0:D]
        ln_summed, ln_lo_pool = sem("ln_summed"), sem("ln_lo_pool")
        LN_LAP = NPROJ // RAW - 6

        def cut(t, c):
            return t[:, :, TC * c:TC * (c + 1)] if isinstance(c, int) else t[:, :, bass.ds(TC * c, TC)]

        LAPS = NPROJ // RAW

        def dtile(t, j):
            return t[j] if isinstance(j, int) else t[bass.ds(j, 1)].rearrange("a p n -> (a p) n")

        def thirds(t):
            return t.rearrange("p (c n) -> p c n", c=3)

        def seg(t, n):
            return (t[:, 0:SEQ].rearrange("h (s r) -> h s r", r=P) if n == 0 else
                    t[:, SEQ:NTOK].rearrange("h (s r) -> h s r", r=TS))

        def seg_of(t, n):
            v = t[:, 0:NPT] if n == 0 else t[:, NPT:NSEG]
            return v.unsqueeze(2).broadcast_to([H, 8, P if n == 0 else TS])

        def sp_proj(sp):
            sp.dma_start(g_bias[0:H, 0:1], a["b_gate"][0, 0:H].unsqueeze(1)).then_inc(state_m_loaded, 16)
            sp.dma_start(g_bias[32:32 + H, 0:1], a["b_gate"][0, H:2 * H].unsqueeze(1)).then_inc(state_m_loaded, 16)
            with nc.allow_non_contiguous_dma(reason="32 values"):
                sp.dma_start(m_prev[:, NPT:NSEG], a["state_mlstm_m"][0].rearrange("b h -> h b")).then_inc(state_m_loaded, 16)

            def lap(i, col):
                for s in range(RAW):
                    load_w(sp, U_PROJ + RAW * (i + 1) + s, s, w_in_v[:, :, bass.ds(col + P * s, P)])

            def load_glu(k, b):
                for g, t in enumerate((GA, GB)):
                    sp.dma_start(glu[:, b, g], dtile(proj_d, t + k)).then_inc(glu_loaded[b], 16)

            def store_c(k, b):
                sp.wait_ge(conv_done, k + 1)
                sp.dma_start(dtile(conv_d, k), c_out[:, b]).then_inc(c_stored[b], 16)

            def col(i):
                t = RAW * (i + 1)
                return COLS[1][2] + P * (t - COLS[1][0])
            with sp.Fori(0, 3) as i:
                lap(i, COLS[0][2] + P * RAW * (i + 1))
            lap(3, col(3))
            sp.wait_ge(g_dve, 8)
            with nc.allow_non_contiguous_dma(reason="36 values"):
                sp.dma_start(o["p_m"][0].rearrange("b h -> h b"), m_new[:, NPT - 1:NPT]).then_inc(m_stored, 16)
                sp.dma_start(o["s_m"][0].rearrange("b h -> h b"), m_new[:, NPT:NSEG]).then_inc(m_stored, 16)
            sp.wait_ge(m_stored, 32)
            for b in range(2):
                sp.wait_ge(stage_stored[b], 16 * 8)
            sp.wait_ge(gates_done, 1)
            load_glu(0, 0)
            lap(4, col(4))
            load_glu(1, 1)
            with sp.Fori(0, 3) as i:
                for b in range(2):
                    k = 2 * i + b + 2
                    lap(k + 3, COLS[1][2] + P * (RAW * (k + 4) - COLS[1][0]))
                    store_c(k - 2, b)
                    load_glu(k, b)
            with sp.Fori(0, 3) as i:
                lap(i + 11, COLS[2][2] + P * RAW * i)
            for b in range(2):
                store_c(KT - 2 + b, b)
            for b in range(2):
                sp.wait_ge(c_stored[b], 16 * KT // 2 + 16)
            sp.dma_start(cT[:], conv_d.rearrange("k p n -> p k n")).then_inc(cT_loaded, 16)
            sp.dma_start(o["s_conv"][0][:, 0:CB - TS, :], a["state_conv"][0][:, TS:CB, :]).then_inc(hist_moved, 16)
            with sp.Fori(3, 8) as i:
                lap(i + 11, COLS[2][2] + P * RAW * i)
            sp.wait_ge(tail_read, 4)
            sp.dma_start(o["p_conv"][0, 0], tail_p).then_inc(tail_stored, 16)
            for b in range(NB):
                sp.dma_start(o["s_conv"][0, b, CB - TS:CB, :], tail_s[TS * b:TS * (b + 1), :]).then_inc(tail_stored, 16)
            for s in range(RAW):
                load_w(sp, U_BR + s, s, w_br_v[CONV][:, :, s * P:(s + 1) * P])
            sp.wait_ge(tail_stored, 16 * (NB + 1))
            sp.wait_ge(hist_moved, 16)

        def act_proj(act):
            def lap(i, func, scale, between=()):
                for s in range(RAW):
                    j = RAW * i + s
                    u = U_PROJ + j
                    split_hi(act, u + SPLIT, U_PROJ // RAW + i + (s + SPLIT) // RAW, (s + SPLIT) % RAW)
                    act.wait_ge(w_used, u + 1)
                    if not isinstance(j, int) or j > 1:
                        act.wait_ge(stage_stored[s % 2], 16 * (2 * i + s // 2))
                    nc.scalar.activation(thirds(stage[:, s % 2]), PS[:, 3 * (s % 2):3 * (s % 2) + 3, 0:TC], func,
                                         scale=scale).then_inc(p_copied, 1)
                    act.wait_ge(p_copied, j + 1)
                    act.dma_start(dtile(proj_d, j), stage[:, s % 2]).then_inc(stage_stored[s % 2], 16)
                    if s < len(between):
                        between[s](act)

            def soft_exp(act):
                act.wait_ge(g_dve, 1)
                nc.scalar.activation(g_b[:], g_a[:], ACT.Exp).then_inc(g_act, 1)

            def soft_ln(act):
                act.wait_ge(g_act, 1)
                nc.scalar.activation(g_a[:], g_b[:], ACT.Ln, bias=1.0).then_inc(g_act, 1)

            def exps(act):
                act.wait_ge(g_dve, 9)
                nc.scalar.activation(g_rows[32:32 + H, :], g_f[:], ACT.Exp)
                nc.scalar.activation(g_rows[64:64 + H, :], g_a[:], ACT.Exp, scale=-1.0)
                nc.scalar.activation(keep_r[:], keep_r[:], ACT.Exp)
                nc.scalar.activation(g_rows[96:96 + H, :], g_b[:], ACT.Exp).then_inc(g_act, 1)
            lap(0, ACT.Copy, 0.5, (soft_exp, soft_ln))
            lap(1, ACT.Copy, 0.5, (exps,))
            for lo, hi, func, scale in ((2, 4, ACT.Tanh, 0.5), (4, 6, ACT.Copy, 1.0), (6, 8, ACT.Copy, DH ** -0.5),
                                        (8, 10, ACT.Copy, 1.0), (10, 12, ACT.Tanh, 0.5),
                                        (12, 14, ACT.Copy, DH ** -0.5)):
                with act.Fori(lo, hi) as i:
                    lap(i, func, scale)

            def square(c):
                act.wait_ge(ln_centred, c + 1)
                nc.scalar.activation(ln_x[:], cut(cT, c), ACT.Square).then_inc(ln_sq, 1)

            def std(c):
                act.wait_ge(ln_var, c + 1)
                nc.scalar.activation(ln_r[:], PS[:, 7, 0:TC], ACT.Sqrt, bias=ln_eps[:, 0:1]).then_inc(ln_std, 1)

            def affine(c):
                act.wait_ge(ln_scaled, c + 1)
                for k in range(KT):
                    v = cT[:, k, TC * c:TC * (c + 1)]
                    last = nc.scalar.activation(v, v, ACT.Identity, scale=cols[:, V_LG, k:k + 1], bias=cols[:, V_LB, k:k + 1])
                last.then_inc(ln_z, 1)

            def half_tanh(c):
                act.wait_ge(ln_z, c + 1)
                nc.scalar.activation(ln_x[:], cut(cT, c), ACT.Tanh, scale=2.0).then_inc(ln_tanh, 1)

            def none(c):
                pass
            for c in range(3):
                for h, steps_ in enumerate(((none, square, none, std), (affine, half_tanh, none, none))):
                    lap(2 * c + (LN_LAP + h), ACT.Tanh, 0.5, [lambda eng, f=f, c=c: f(c) for f in steps_])

        def pool_proj(pool):
            with pool.Fori(0, LAPS) as i:
                for s in range(RAW):
                    split_lo(pool, U_PROJ + RAW * i + s + SPLIT, (s + SPLIT) % RAW)

        def a_hi(k, c):
            return A_hi[:, k, TC * c:TC * (c + 1)]

        def a_lo(k, c):
            return A_lo[:, k, TC * c:TC * (c + 1)]

        def banks(b):
            return [PS[:, 3 * b + c, 0:TC] for c in range(3)]

        def pe_proj(pe):
            pe.wait_ge(wif_lo_done, 1)
            product(banks(1), wif_hi, wif_lo, a_hi, a_lo, KT).then_inc(wif_used, 1)

            def lap(i, between=None):
                for s in range(RAW):
                    j = RAW * i + s
                    if isinstance(j, int) and j == 1:
                        pe.wait_ge(gate_read, 1)
                    if not isinstance(j, int) or j > 1:
                        pe.wait_ge(p_copied, j - 1)
                    use_unit(pe, U_PROJ + j, s, banks(s % 2), a_hi, a_lo)
                    if between and s in between:
                        between[s]()
            lap(0)
            lap(1)
            lap(2)
            pe.wait_ge(g_act, 3)
            pe.wait_ge(g_dve, 9)
            for n in range(2):
                for q in range(4):
                    t = 4 * n + q
                    last = nc.tensor.transpose(PS[:, 6 + n, P * q:P * (q + 1)], g_rows[:, P * t:P * (t + 1)], ident[:])
                last.then_inc(gate_turned, 1)
            pe.wait_ge(gate_read, 2)
            nc.tensor.transpose(PS[:, 6, 0:P], g_rows[:, P * NPT:NTOK], ident[:])
            for h in range(H):
                last = nc.tensor.matmul(PS[:, 6, P + NSEG * h:P + NSEG * (h + 1)], sel[:, h], keep_r[:], start=True, stop=True)
            last.then_inc(gate_turned, 1)
            with pe.Fori(3, LN_LAP) as i:
                lap(i)
            pe.wait_ge(conv_done, KT)
            for g in range(2):
                for h in range(2):
                    if g:
                        pe.wait_ge(tail_read, h + 1)
                    for q in range(4):
                        k = 4 * h + q
                        out = PS[0:CB, 6 + h, P * q:P * (q + 1)] if g == 0 else PS[:, 6 + h, P * q:P * (q + 1)]
                        last = nc.tensor.transpose(out, u_tail[:, k, 0:CB] if g == 0 else u_tail[:, k, CB:CB + P], ident[:])
                    last.then_inc(tail_turned, 1)
            pe.wait_ge(cT_loaded, 16)
            pe.wait_ge(tail_read, 4)

            def average(bank, count, done):
                pe.wait_ge(ln_summed, count)
                nc.tensor.matmul(PS[:, bank, 0:TC], mean_mat[:], ln_sum[:], start=True, stop=True).then_inc(done, 1)

            with pe.Fori(0, 3) as c:
                def mean():
                    average(6, 2 * c + 1, ln_mean)

                def variance():
                    average(7, 2 * c + 2, ln_var)
                lap(2 * c + LN_LAP, {0: mean, 2: variance})
                lap(2 * c + (LN_LAP + 1))

        def dve_proj(dve):
            steps = st["dve"]
            dve.sem_inc(c_stored[0], 16)
            dve.sem_inc(c_stored[1], 16)
            for t, v, w in ((restart_mul, 1.0, 0.0), (restart_add, 0.0, -BIG)):
                steps.link(nc.vector.memset(t[:], v))
                for n in range(2):
                    steps.mark(nc.vector.memset(seg(t, n)[:, :, 0:1], w))
            steps.mark(nc.vector.memset(g_rows[:], 0.0))
            steps.mark(nc.vector.memset(m_prev[:, 0:1], 0.0))
            steps.wait()
            dve.wait_ge(state_m_loaded, 48)
            dve.wait_ge(wif_used, 1)
            steps.mark(nc.vector.tensor_scalar(thirds(g_i[:]), PS[0:H, 3:6, 0:TC], g_bias[0:H, 0:1], None, ALU.add))
            nc.vector.tensor_scalar(thirds(g_f[:]), PS[32:32 + H, 3:6, 0:TC], g_bias[32:32 + H, 0:1], None, ALU.add).then_inc(gate_read, 1)
            dve.wait_ge(gate_read, 1)
            nc.vector.scalar_tensor_tensor(out=g_a[:], in0=g_f[:], scalar=-1.0, in1=g_f[:], op0=ALU.mult, op1=ALU.min).then_inc(g_dve, 1)
            dve.wait_ge(g_act, 2)
            nc.vector.scalar_tensor_tensor(out=g_f[:], in0=g_f[:], scalar=0.0, in1=g_a[:], op0=ALU.min, op1=ALU.subtract).then_inc(g_dve, 1)
            dve.wait_ge(g_dve, 2)
            nc.vector.tensor_tensor_scan(g_b[:], restart_mul[:], g_f[:], 0.0, ALU.mult, ALU.add).then_inc(g_dve, 1)
            dve.wait_ge(g_dve, 3)
            nc.vector.tensor_tensor(g_i[:], g_i[:], g_b[:], ALU.subtract).then_inc(g_dve, 1)
            dve.wait_ge(g_dve, 4)
            nc.vector.tensor_tensor_scan(g_a[:], restart_add[:], g_i[:], -BIG, ALU.add, ALU.max).then_inc(g_dve, 1)
            dve.wait_ge(g_dve, 5)
            for n, r in ((0, P), (1, TS)):
                lo = NPT * n
                steps.mark(nc.vector.tensor_copy(b_last[:, lo:lo + 8], seg(g_b, n)[:, :, r - 1]))
                steps.mark(nc.vector.tensor_copy(M_last[:, lo:lo + 8], seg(g_a, n)[:, :, r - 1]))
            steps.wait()
            steps.link(nc.vector.tensor_tensor_scan(m_new[:, 0:NPT], M_last[:, 0:NPT], b_last[:, 0:NPT], 0.0, ALU.max, ALU.add))
            steps.link(nc.vector.tensor_copy(m_prev[:, 1:NPT], m_new[:, 0:NPT - 1]))
            nc.vector.tensor_tensor(M_last[:], M_last[:], m_prev[:], ALU.max).then_inc(g_dve, 1)
            for n in range(2):
                steps.mark(nc.vector.tensor_tensor(seg(M_rows, n), seg(g_a, n), seg_of(m_prev, n), ALU.max))
            dve.wait_ge(g_dve, 6)
            steps.mark(nc.vector.tensor_tensor(keep_r[:], m_prev[:], M_last[:], ALU.subtract))
            nc.vector.tensor_tensor(m_new[:, NPT:NSEG], M_last[:, NPT:NSEG], b_last[:, NPT:NSEG], ALU.add).then_inc(g_dve, 1)
            steps.wait()
            nc.vector.tensor_tensor(g_a[:], g_b[:], M_rows[:], ALU.add).then_inc(g_dve, 1)
            dve.wait_ge(g_dve, 8)
            for n in range(2):
                steps.mark(nc.vector.tensor_tensor(seg(g_f, n), seg_of(m_prev, n), seg(M_rows, n), ALU.subtract))
                steps.mark(nc.vector.tensor_tensor(seg(g_b, n), seg(g_i, n), seg_of(M_last, n), ALU.subtract))
            steps.wait()
            nc.vector.tensor_copy(g_rows[0:H, :], g_i[:]).then_inc(g_dve, 1)
            for n in range(2):
                dve.wait_ge(gate_turned, n + 1)
                nc.vector.tensor_copy(gate_cols[:, 4 * n:4 * n + 4], PS[:, 6 + n].rearrange("p (t q c) -> p t q c", t=4, q=4)[:, :, :, 0:H]).then_inc(gate_read, 1)
            dve.wait_ge(gate_turned, 3)
            steps.mark(nc.vector.tensor_copy(gate_cols[:, NPT], PS[:, 6, 0:P].rearrange("p (q c) -> p q c", q=4)[:, :, 0:H]))
            steps.link(nc.vector.tensor_copy(keep_b[:].rearrange("p h s -> p (h s)"), PS[:, 6, P:P + H * NSEG]))
            dve.sem_inc(gates_done, 1)

            dve.wait_ge(m_stored, 32)
            steps.mark(nc.vector.memset(ext[:, 0, 0:CB], 0.0))
            steps.link(nc.vector.memset(ext[:, 1, 0:CB], 0.0))

            def tap_scalar(w, k):
                return taps[:, w, k:k + 1] if isinstance(k, int) else taps[:, w, bass.ds(k, 1)]
            with dve.Fori(0, KT // 2) as i:
                steps.enter(i, 2 * (4 + 2 * CW))
                for b in range(2):
                    k = 2 * i + b
                    ep, es = ext[:, b, 0:CB + SEQ], ext[:, b, CB + SEQ:EXT].rearrange("p (s r) -> p s r", s=NB)
                    cp, cs = c_out[:, b, 0:SEQ], c_out[:, b, SEQ:NTOK].rearrange("p (s r) -> p s r", s=NB)
                    dve.wait_ge(glu_loaded[b], 32 * (i + 1))
                    steps.mark(nc.vector.scalar_tensor_tensor(out=ep[:, CB:CB + SEQ], in0=glu[:, b, 1, 0:SEQ], scalar=1.0,
                                                              in1=glu[:, b, 0, 0:SEQ], op0=ALU.add, op1=ALU.mult))
                    steps.mark(nc.vector.scalar_tensor_tensor(out=es[:, :, CB:CB + TS], in0=glu[:, b, 1, SEQ:NTOK].rearrange("p (s r) -> p s r", s=NB),
                                                              scalar=1.0, in1=glu[:, b, 0, SEQ:NTOK].rearrange("p (s r) -> p s r", s=NB),
                                                              op0=ALU.add, op1=ALU.mult))
                    steps.link(nc.vector.tensor_copy(es[:, :, 0:CB], hist_T[:, bass.ds(k, 1)].rearrange("p k b r -> p (k b) r")))
                    dve.wait_ge(c_stored[b], 16 * (i + 1))
                    for e, c, n in ((ep, cp, SEQ), (es, cs, TS)):
                        src = e[:, 0:n] if n == SEQ else e[:, :, 0:n]
                        steps.mark(nc.vector.tensor_scalar(c, src, tap_scalar(0, k), cols[:, V_CB, bass.ds(k, 1)], ALU.mult, ALU.add))
                    for w in range(1, CW):
                        for e, c, n in ((ep, cp, SEQ), (es, cs, TS)):
                            src = e[:, w:w + n] if n == SEQ else e[:, :, w:w + n]
                            steps.wait(1)
                            steps.mark(nc.vector.scalar_tensor_tensor(out=c, in0=src, scalar=tap_scalar(w, k), in1=c,
                                                                      op0=ALU.mult, op1=ALU.add))
                    ut = u_tail[:, bass.ds(k, 1)].rearrange("p k n -> p (k n)")
                    steps.mark(nc.vector.tensor_copy(ut[:, 0:CB], ep[:, SEQ:SEQ + CB]))
                    steps.wait(1)
                    nc.vector.tensor_copy(ut[:, CB:CB + P].rearrange("p (s r) -> p s r", s=NB), es[:, :, CB:CB + TS]).then_inc(conv_done, 1)
                steps.leave(KT // 2)
            for g in range(2):
                for h in range(2):
                    dve.wait_ge(tail_turned, 2 * g + h + 1)
                    dst, src = (tail_p, PS[0:CB, 6 + h]) if g == 0 else (tail_s, PS[:, 6 + h])
                    nc.vector.tensor_copy(dst[:, 512 * h:512 * (h + 1)], src).then_inc(tail_read, 1)
            dve.wait_ge(cT_loaded, 16)
            with dve.Fori(0, 3) as c:
                steps.enter(c, 1)
                nc.vector.tensor_reduce(ln_sum[:], cut(cT, c).rearrange("p k n -> p n k"), AX_X, ALU.add).then_inc(ln_summed, 1)
                dve.wait_ge(ln_mean, c + 1)
                nc.vector.tensor_tensor(cut(cT, c), cut(cT, c), PS[:, 6, 0:TC].unsqueeze(1).broadcast_to([P, KT, TC]),
                                        ALU.subtract).then_inc(ln_centred, 1)
                dve.wait_ge(ln_sq, c + 1)
                nc.vector.tensor_reduce(ln_sum[:], ln_x[:].rearrange("p k n -> p n k"), AX_X, ALU.add).then_inc(ln_summed, 1)
                dve.wait_ge(ln_std, c + 1)
                steps.link(nc.vector.reciprocal(ln_r[:], ln_r[:]))
                nc.vector.tensor_tensor(cut(cT, c), cut(cT, c), ln_r[:].unsqueeze(1).broadcast_to([P, KT, TC]),
                                        ALU.mult).then_inc(ln_scaled, 1)
                dve.wait_ge(ln_tanh, c + 1)
                nc.vector.scalar_tensor_tensor(out=cut(cT, c), in0=ln_x[:], scalar=1.0, in1=cut(cT, c),
                                               op0=ALU.add, op1=ALU.mult).then_inc(ln_y, 1)
            steps.leave(3)

        def act_ln(act):
            for c in range(3):
                act.wait_ge(ln_y, c + 1)
                nc.scalar.copy(cut(A_hi, c), cut(cT, c)).then_inc(ln_hi, 1)

        def pool_ln(pool):
            pool.wait_ge(ln_hi, 2)
            nc.gpsimd.tensor_tensor(cut(A_lo, 1), cut(cT, 1), cut(A_hi, 1).bitcast(F32), ALU.subtract).then_inc(ln_lo_pool, 1)

        def dve_ln(dve):
            for c in (0, 2):
                dve.wait_ge(ln_hi, c + 1)
                nc.vector.tensor_tensor(cut(A_lo, c), cut(cT, c), cut(A_hi, c).bitcast(F32), ALU.subtract).then_inc(ln_lo, 1)

        gate_loaded, part_stored = [sem("gate_loaded0"), sem("gate_loaded1")], [sem("part_stored0"), sem("part_stored1")]
        part_done, part_mul = sem("part_done"), sem("part_mul")
        prev_loaded = [sem("prev_loaded0"), sem("prev_loaded1")]
        ORDER = (CONV, MLSTM, XATT)

        def br_laps(eng, n, body):
            if n == 0:
                body(0)
            with eng.Fori(0 if n else 1, 2) as i:
                body(i)

        def sp_branch(sp, n, next_src, ahead=None):
            def lap(i, src):
                for s in range(RAW):
                    J = KT * n + RAW * i + s
                    load_w(sp, U_BR + J + RAW, s, src(s))
                    if J > 1:
                        sp.wait_ge(part_done, J - 1)
                        if RAW * i + s > 1:
                            sp.dma_start(part_d[RAW * i + s - 2], part_out[:, s % 2]).then_inc(part_stored[s % 2], 16)
                    sp.dma_start(gate_in[:, s % 2], proj_d[GT + KT * ORDER[n] + RAW * i + s]).then_inc(gate_loaded[s % 2], 16)
                    if RAW * i + s == 5 and ahead:
                        ahead(sp)
                    if n:
                        sp.dma_start(prev_in[:, s % 2], part_d[RAW * i + s]).then_inc(prev_loaded[s % 2], 16)
            lap(0, lambda s: w_br_v[ORDER[n]][:, :, (RAW + s) * P:(RAW + s + 1) * P])
            lap(1, next_src)
            if n == 2:
                sp_mix_ahead(sp)
            for b in range(2):
                sp.wait_ge(part_done, KT * n + KT - 1 + b)
                sp.dma_start(part_d[KT - 2 + b], part_out[:, b]).then_inc(part_stored[b], 16)
            for b in range(2):
                sp.wait_ge(part_stored[b], 16 * 4 * (n + 1))

        def act_branch(act, n):
            with act.Fori(0, 2) as i:
                for s in range(RAW):
                    split_hi(act, U_BR + KT * n + RAW * i + s + SPLIT, U_BR // RAW + 2 * n + i + (s + SPLIT) // RAW, (s + SPLIT) % RAW)

        def pool_branch(pool, n):
            with pool.Fori(0, 2) as i:
                for s in range(RAW):
                    split_lo(pool, U_BR + KT * n + RAW * i + s + SPLIT, (s + SPLIT) % RAW)

        def pe_branch(pe, n, ready, count):
            if n:
                pe.wait_ge(ready, count)

            def body(i):
                for s in range(RAW):
                    J = KT * n + RAW * i + s
                    if not isinstance(J, int) or J > 1:
                        pe.wait_ge(part_done, J - 1)
                    if isinstance(J, int) and J == 0:
                        for c in range(3):
                            pe.wait_ge((ln_lo, ln_lo_pool, ln_lo)[c], (1, 1, 2)[c])
                            if c < 2:
                                pe.wait_ge(w_lo_done, U_BR + 1)
                                product([banks(0)[c]], w_hi[:, 0], w_lo[:, 0], lambda k, _: a_hi(k, c), lambda k, _: a_lo(k, c), KT)
                            else:
                                use_unit(pe, U_BR, 0, [banks(0)[c]], lambda k, _: a_hi(k, c), lambda k, _: a_lo(k, c))
                    else:
                        use_unit(pe, U_BR + J, s, banks(s % 2), a_hi, a_lo)
            br_laps(pe, n, body)

        def dve_branch(dve, n):
            def body(i):
                for s in range(RAW):
                    J = KT * n + RAW * i + s
                    lap = 2 * n + i
                    dve.wait_ge(w_used, U_BR + J + 1)
                    dve.wait_ge(gate_loaded[s % 2], 16 * (2 * lap + s // 2 + 1))
                    if not isinstance(J, int) or J > 1:
                        dve.wait_ge(part_stored[s % 2], 16 * (2 * lap + s // 2))
                    nc.vector.scalar_tensor_tensor(out=thirds(part_out[:, s % 2]), in0=thirds(gate_in[:, s % 2]), scalar=1.0,
                                                   in1=PS[:, 3 * (s % 2):3 * (s % 2) + 3, 0:TC], op0=ALU.add,
                                                   op1=ALU.mult).then_inc(part_mul if n else part_done, 1)
                    if n:
                        dve.wait_ge(part_mul, J - KT + 1)
                        dve.wait_ge(prev_loaded[s % 2], 16 * (2 * (lap - 2) + s // 2 + 1))
                        nc.vector.tensor_tensor(part_out[:, s % 2], part_out[:, s % 2], prev_in[:, s % 2], ALU.add).then_inc(part_done, 1)
            br_laps(dve, n, body)

        qk_loaded, vo_loaded = [sem("qk_loaded0"), sem("qk_loaded1")], sem("vo_loaded")
        (ml_M, ml_S, ml_turn, ml_D, ml_exp, ml_v1, ml_kw, ml_o, ml_sT, ml_intra, ml_U, ml_inter, ml_num, ml_rden, ml_sq,
         ml_var, ml_pow, ml_y, ml_upd, ml_state, ml_yT, ml_gain, ml_hi, ml_lo, ml_init) = (
            sem(n) for n in ("ml_M", "ml_S", "ml_turn", "ml_D", "ml_exp", "ml_v1", "ml_kw", "ml_o", "ml_sT", "ml_intra", "ml_U",
                             "ml_inter", "ml_num", "ml_rden", "ml_sq", "ml_var", "ml_pow", "ml_y", "ml_upd", "ml_state",
                             "ml_yT", "ml_gain", "ml_hi", "ml_lo", "ml_init"))
        n_loaded, cb_loaded, cb_stored = sem("n_loaded"), [sem(f"cb_loaded{s}") for s in range(4)], [sem("cb_stored0"), sem("cb_stored1")]
        sc_T, sc_CT, sc_own, sc_upd, sc_new, sc_qm, fin_stored = (
            sem(n) for n in ("sc_T", "sc_CT", "sc_own", "sc_upd", "sc_new", "sc_qm", "fin_stored"))
        nf_turn, nf_copied, nu_done, nu_new, fc_turn, fc_copied = (
            sem(n) for n in ("nf_turn", "nf_copied", "nu_done", "nu_new", "fc_turn", "fc_copied"))
        SB = NPT
        cb_in = [x.rearrange("p (n z a) c -> p n z (a c)", n=2, z=2)[:, n] for x in (q_in[:, 1], o_in) for n in range(2)]
        cb_new = k_in[:, 1].rearrange("p (n z a) c -> p n z (a c)", n=2, z=2)
        nb_in = v_in[0:NB].rearrange("p k c -> p (k c)").rearrange("p (h d) -> p h d", h=H)

        def tok(t):
            return slice(P * t, P * (t + 1)) if isinstance(t, int) else bass.ds(P * t, P)

        def ml_tiles(eng, chunk, steps=None, per=0):
            chunk(0, 0, 0)
            with eng.Fori(0, (NPT - 2) // 2) as i:
                if steps:
                    steps.enter(i, 2 * per)
                chunk(2 * i + 1, 1, i)
                chunk(2 * i + 2, 0, i + 1)
            if steps:
                steps.leave((NPT - 2) // 2)
            chunk(NPT - 1, 1, (NPT - 1) // 2)

        def proj_tiles(first, t):
            return proj_d[first:first + KT, :, tok(t)].rearrange("k p n -> p k n")

        def sp_mlstm_ahead(sp):
            for dst, first, done in ((q_in[:, 0], QQ, qk_loaded[0]), (k_in[:, 0], KK, qk_loaded[0]), (v_in[:], VV, vo_loaded),
                                     (o_in[:], OO, vo_loaded), (q_in[:, 1], QQ, qk_loaded[1]), (k_in[:, 1], KK, qk_loaded[1])):
                sp.dma_start(dst, proj_tiles(first, 1 if done is qk_loaded[1] else 0)).then_inc(done, 16)
            sp.dma_start(n_in, a["state_mlstm_n"][0].rearrange("b h d -> (b h) d")).then_inc(n_loaded, 16)

        def sp_mlstm(sp):
            def load(t, b):
                sp.wait_ge(ml_turn, 3 * t)
                sp.dma_start(v_in[:], proj_tiles(VV, t)).then_inc(vo_loaded, 16)
                sp.dma_start(o_in[:], proj_tiles(OO, t)).then_inc(vo_loaded, 16)
                if not isinstance(t, int) or t > 1:
                    sp.wait_ge(ml_inter, H * (t - 1))
                    sp.dma_start(q_in[:, b], proj_tiles(QQ, t)).then_inc(qk_loaded[b], 16)
                    sp.dma_start(k_in[:, b], proj_tiles(KK, t)).then_inc(qk_loaded[b], 16)
            load(1, 1)
            with sp.Fori(0, (NPT - 2) // 2) as i:
                load(2 * i + 2, 0)
                load(2 * i + 3, 1)
            load(SB, 0)
            sp.wait_ge(ml_turn, 3 * (SB + 1))
            sp.dma_start(nb_in, a["state_mlstm_n"][0]).then_inc(n_loaded, 16)
            sp.wait_ge(ml_inter, H * NPT)

            def c_dram(t, b, h):
                v = t[0, b].rearrange("h (z e) d -> h e z d", z=2)
                return v[h] if isinstance(h, int) else v[bass.ds(h, 1)].rearrange("h e z d -> (h e) z d")
            for b in range(4):
                sp.dma_start(cb_in[b], c_dram(a["state_mlstm_c"], b, 0)).then_inc(cb_loaded[b], 16)

            def head(h, last):
                for b in range(NB):
                    sp.wait_ge(sc_new, NB * h + b + 1)
                    sp.dma_start(c_dram(o["s_c"], b, h), cb_new[:, b % 2]).then_inc(cb_stored[b % 2], 16)
                    if b < NB - 4:
                        sp.dma_start(cb_in[b % 4], c_dram(a["state_mlstm_c"], b + 4, h)).then_inc(cb_loaded[b % 4], 16)
                    elif not last:
                        sp.dma_start(cb_in[b % 4], c_dram(a["state_mlstm_c"], b + 4 - NB, h + 1)).then_inc(cb_loaded[b % 4], 16)
            with sp.Fori(0, H - 1) as h:
                head(h, False)
            head(H - 1, True)
            sp.wait_ge(nu_new, 1)
            sp.dma_start(o["s_n"][0], nb_in).then_inc(fin_stored, 16)
            sp.wait_ge(nf_copied, 3)
            sp.dma_start(o["p_n"][0, 0].rearrange("h (z p) -> (h z) p", z=2), n_row).then_inc(fin_stored, 16)
            for h in range(H):
                sp.wait_ge(fc_copied, h + 1)
                sp.dma_start(c_dram(o["p_c"], 0, h), fc_out(h)).then_inc(fin_stored, 16)
            sp.wait_ge(fin_stored, 16 * (2 + H))
            for b in range(2):
                sp.wait_ge(cb_stored[b], 16 * NB * H // 2 + 16)

        def fc_out(h):
            return (q_in if h < 2 else k_in)[:, 0].rearrange("p (n z a) c -> p n z (a c)", n=2, z=2)[:, h % 2]

        def pe_mlstm(pe):
            def scores(t, b, uses):
                first = isinstance(t, int) and t == 0

                def state_read(banks):
                    if not first:
                        pe.wait_ge(ml_state, KT * (t - 1) + banks)
                state_read(2)
                for h in range(H):
                    last = nc.tensor.matmul(PS[:, 1, P * h:P * (h + 1)], sel[:, h], M_rows[:, tok(t)], start=True, stop=True)
                last.then_inc(ml_M, 1)
                pe.wait_ge(qk_loaded[b], 32 * (uses + 1))
                for h in range(H):
                    for z in range(2):
                        last = nc.tensor.matmul(PS[:, 0, P * h:P * (h + 1)], k_in[:, b, 2 * h + z], q_in[:, b, 2 * h + z],
                                                start=z == 0, stop=z == 1)
                last.then_inc(ml_S, 1)
                pe.wait_ge(vo_loaded, 32 * (t + 1))
                for n, src in enumerate((v_in, o_in, k_in[:, b])):
                    state_read(4 + 2 * n)
                    for k in range(KT):
                        last = nc.tensor.transpose(PS[:, 2 + 2 * n + k // 4, P * (k % 4):P * (k % 4 + 1)], src[:, k], ident[:])
                    last.then_inc(ml_turn, 1)
                pe.wait_ge(ml_v1, t + 1)
                if not first:
                    y_turn(t - 1, 1 - b)
                pe.wait_ge(ml_sT, t + 1)
                for h in range(H):
                    if h == 2 and not first:
                        pe.wait_ge(ml_gain, 2 * t)
                    nc.tensor.matmul(PS[:, h, 0:E1], sT[:, h], v1[:, h], start=True, stop=True).then_inc(ml_intra, 1)

            def y_turn(t, b):
                pe.wait_ge(ml_y, t + 1)
                for n in range(2):
                    for q in range(4):
                        k = 4 * n + q
                        last = nc.tensor.transpose(PS[:, 2 + n, P * q:P * (q + 1)], oy[:, b, k // 2, P * (k % 2):P * (k % 2 + 1)], ident[:])
                    last.then_inc(ml_yT, 1)

            def chunk(t, b, uses):
                scores(t, b, uses)
                pe.wait_ge(ml_o, t + 1)
                pe.wait_ge(ml_kw, t + 1)
                if isinstance(t, int) and t == 0:
                    pe.wait_ge(ml_init, 1)
                for h in range(H):
                    for z in range(2):
                        last = nc.tensor.matmul(PS[:, 4 + h, 0:E1], q_in[:, b, 2 * h + z], C_T[:, h, z], start=z == 0, stop=z == 1)
                    last.then_inc(ml_inter, 1)
                for h in range(H):
                    if h < 2:
                        pe.wait_ge(ml_U, H * t + 2 * (h + 1))
                    else:
                        pe.wait_ge(ml_num, H * t + 2 * (h - 1))
                    for z in range(2):
                        nc.tensor.matmul(PS[:, 2 * h + z, 0:E1], kw[:, h, P * z:P * (z + 1)], v1[:, h], start=True, stop=True).then_inc(ml_upd, 1)
            pe.wait_ge(n_loaded, 16)
            for z in range(2):
                last = nc.tensor.transpose(PS[:, 2, 32 * z:32 * (z + 1)], n_in[:, P * z:P * (z + 1)], ident[0:32, 0:32])
            nc.tensor.transpose(PS[0:NB, 2, 64:64 + H], keep_r[:, NPT:NSEG], ident[0:H, 0:H]).then_inc(nf_turn, 1)
            pe.wait_ge(nf_copied, 1)
            ml_tiles(pe, chunk)

            scores(SB, 0, SB // 2)
            pe.wait_ge(ml_o, SB + 1)
            pe.wait_ge(ml_kw, SB + 1)
            pe.wait_ge(ml_U, H * (SB + 1))
            with pe.Fori(0, H) as h:
                pe.wait_ge(ml_num, H * SB + h)
                pe.wait_ge(sc_qm, h + 1)
                def state_turn(b):
                    pe.wait_ge(cb_loaded[b % 4], 16 * (NB // 4 * h + b // 4 + 1))
                    pe.wait_ge(sc_CT, NB * h + b + 1)
                    for ze in range(2):
                        for zd in range(2):
                            last = nc.tensor.transpose(PS[:, b % 2, DH * zd + P * ze:DH * zd + P * (ze + 1)],
                                                       cb_in[b % 4][:, ze, P * zd:P * (zd + 1)], ident[:])
                    last.then_inc(sc_T, 1)
                state_turn(0)
                for b in range(NB):
                    r = NB * h + b
                    if b < NB - 1:
                        state_turn(b + 1)
                    pe.wait_ge(sc_own, r + 1)
                    if b > 1:
                        pe.wait_ge(sc_new, r - 1)
                    for z in range(2):
                        last = nc.tensor.matmul(PS[:, 2 + b % 2, DH * z:DH * (z + 1)], v_own[:, b % 2, P * z:P * (z + 1)],
                                                kw[:, bass.ds(h, 1)].rearrange("p h d -> p (h d)"), start=True, stop=True)
                    last.then_inc(sc_upd, 1)
                    pe.wait_ge(sc_CT, r + 3)
                    for z in range(2):
                        last = nc.tensor.matmul(PS[:, 4, 0:E1], qm[:, z, P * b:P * (b + 1)], Cb_T[:, b % 2, z],
                                                start=b == 0 and z == 0, stop=b == NB - 1 and z == 1)
                last.then_inc(ml_inter, 1)
            for h in range(H):
                last = nc.tensor.matmul(PS[0:NB, 6 + h // 2, DH * (h % 2):DH * (h % 2 + 1)], own[:], kw[:, h], start=True, stop=True)
            last.then_inc(nu_done, 1)
            pe.wait_ge(nf_copied, 2)
            nc.tensor.transpose(PS[0:KT, 5, 0:P], n_cols[:], ident[:]).then_inc(nf_turn, 1)

            def final_state(h):
                if h > 1:
                    pe.wait_ge(fc_copied, h - 1)
                for ze in range(2):
                    for zd in range(2):
                        last = nc.tensor.transpose(PS[:, h % 2, DH * ze + P * zd:DH * ze + P * (zd + 1)],
                                                   C_T[:, h, zd, P * ze:P * (ze + 1)], ident[:])
                last.then_inc(fc_turn, 1)
            final_state(0)
            final_state(1)
            y_turn(SB, 0)
            final_state(2)
            final_state(3)
            pe.wait_ge(fc_copied, H)

        def act_mlstm(act):
            def hi(t):
                for n in range(2):
                    act.wait_ge(ml_gain, 2 * t + n + 1)
                    act.wait_ge(gates_done, 1)
                    nc.scalar.copy(A_hi[:, 4 * n:4 * n + 4, tok(t)], y_T[:, n]).then_inc(ml_hi, 1)

            def front(t):
                act.wait_ge(ml_turn, 3 * t + 1)
                for n in range(2):
                    last = nc.scalar.copy(v1[:, 2 * n:2 * n + 2, 0:DH], PS[:, 2 + n].rearrange("p (h d) -> p h d", h=2))
                last.then_inc(ml_v1, 1)
                act.wait_ge(ml_D, t + 1)
                act.wait_ge(gates_done, 1)
                for h in range(H):
                    last = nc.scalar.activation(decay[:, h], decay[:, h], ACT.Exp, scale=-1.0, bias=gate_col(t, 0, h))
                last.then_inc(ml_exp, 1)
                act.wait_ge(ml_turn, 3 * t + 3)
                act.wait_ge(gates_done, 1)
                for h in range(H):
                    last = nc.scalar.activation(kw[:, h], PS[:, 6 + h // 2, DH * (h % 2):DH * (h % 2 + 1)], ACT.Copy, scale=gate_col(t, 3, h))
                last.then_inc(ml_kw, 1)
                if not isinstance(t, int) or t > 0:
                    hi(t - 1)
                    act.wait_ge(ml_y, t)
                for h in range(H):
                    act.wait_ge(ml_intra, H * t + h + 1)
                    nc.scalar.copy(num[:, h], PS[:, h, 0:E1]).then_inc(ml_U, 1)

            def back(t):
                act.wait_ge(ml_rden, t + 1)
                for h in range(H):
                    last = nc.scalar.activation(junk(h), num[:, h, 0:DH], ACT.Square, scale=rden[:, h:h + 1], accum_out=ssq[:, h:h + 1])
                last.then_inc(ml_sq, 1)

            def chunk(t, b, uses):
                front(t)
                back(t)
            ml_tiles(act, chunk)
            front(SB)
            with act.Fori(0, H) as h:
                for b in range(NB):
                    r = NB * h + b
                    act.wait_ge(sc_T, r + 1)
                    act.wait_ge(nf_copied, 1)
                    nc.scalar.copy(Cb_T[:, b % 2, :, 0:DH], PS[:, b % 2].rearrange("p (z e) -> p z e", z=2))
                    nc.scalar.copy(Cb_T[:, b % 2, :, DH:E1], n_T[:, :, bass.ds(H * b + h, 1)]).then_inc(sc_CT, 1)
            back(SB)
            for h in range(H):
                if h == 2:
                    hi(SB)
                act.wait_ge(fc_turn, h + 1)
                nc.scalar.copy(fc_out(h), PS[:, h % 2].rearrange("p (z d) -> p z d", z=2)).then_inc(fc_copied, 1)

        def junk(h):
            return (decay if h < 2 else sT)[:, 2 * (h % 2):2 * (h % 2) + 2].rearrange("p a b -> p (a b)")

        def gate_col(t, kind, h):
            if isinstance(t, int):
                return gate_cols[:, t, kind, h:h + 1]
            return gate_cols[:, bass.ds(t, 1), kind, h:h + 1].rearrange("p t h -> p (t h)")

        def keep_col(h, s):
            if isinstance(s, int) and isinstance(h, int):
                return keep_b[:, h, s:s + 1]
            if isinstance(h, int):
                return keep_b[:, h, bass.ds(s, 1)]
            return keep_b[:, bass.ds(h, 1), s:s + 1].rearrange("p h s -> p (h s)")

        def pool_mlstm(pool):
            def chunk(t, b=0, uses=0):
                pool.wait_ge(ml_var, t + 1)
                nc.gpsimd.tensor_tensor(hr[:], hr0[:], minus_half[:], ALU.pow).then_inc(ml_pow, 1)
                for n in range(2):
                    pool.wait_ge(ml_hi, 2 * t + n + 1)
                    pool.wait_ge(gates_done, 1)
                    nc.gpsimd.tensor_tensor(A_lo[:, 4 * n:4 * n + 4, tok(t)], y_T[:, n], A_hi[:, 4 * n:4 * n + 4, tok(t)].bitcast(F32),
                                            ALU.subtract).then_inc(ml_lo, 1)
            pool.sem_inc(ml_lo, 2)
            nc.gpsimd.memset(C_T[:], 0.0).then_inc(ml_init, 1)
            nc.gpsimd.memset(qm[:], 0.0).then_inc(ml_init, 1)
            with pool.Fori(0, NPT) as t:
                chunk(t)
            chunk(SB)

        def dve_mlstm(dve):
            steps = st["dve"]

            def gain(t):
                for n in range(2):
                    dve.wait_ge(ml_yT, 2 * t + n + 1)
                    dve.wait_ge(ml_lo, 2 * t + n + 1)
                    nc.vector.tensor_tensor(y_T[:, n], PS[:, 2 + n].rearrange("p (k c) -> p k c", k=4),
                                            cols[:, V_HEAD, 4 * n:4 * n + 4].unsqueeze(2).broadcast_to([P, 4, P]),
                                            ALU.mult).then_inc(ml_gain, 1)

            def front(t, b, mask):
                dve.wait_ge(ml_M, t + 1)
                nc.vector.tensor_tensor(decay[:], PS[:, 1].rearrange("p (h j) -> p h j", h=H),
                                        later[:, mask].unsqueeze(1).broadcast_to([P, H, P]), ALU.add).then_inc(ml_D, 1)
                dve.wait_ge(ml_turn, 3 * t + 2)
                nc.vector.tensor_scalar(oy[:, b].rearrange("p (n h) d -> p n (h d)", n=2), PS[:, 4:6], 1.0, None, ALU.add).then_inc(ml_o, 1)
                dve.wait_ge(ml_S, t + 1)
                dve.wait_ge(ml_exp, t + 1)
                nc.vector.tensor_tensor(sT[:], decay[:], PS[:, 0].rearrange("p (h j) -> p h j", h=H), ALU.mult).then_inc(ml_sT, 1)
                if not isinstance(t, int) or t > 0:
                    gain(t - 1)

            def inter(t, h, bank, count, hh=None):
                dve.wait_ge(ml_U, count)
                dve.wait_ge(ml_inter, count)
                n = num[:, h] if isinstance(h, int) else num[:, bass.ds(h, 1)].rearrange("p h e -> p (h e)")
                w = gate_col(t, 1, h) if isinstance(h, int) else gate_cols[:, t, 1, bass.ds(h, 1)]
                nc.vector.scalar_tensor_tensor(out=n, in0=PS[:, bank, 0:E1], scalar=w, in1=n, op0=ALU.mult, op1=ALU.add).then_inc(ml_num, 1)

            def denominators(t):
                dve.wait_ge(ml_num, H * t + H)
                d = num[:, :, DH]
                em = gate_cols[:, t, 2] if isinstance(t, int) else gate_cols[:, bass.ds(t, 1), 2].rearrange("p t h -> p (t h)")
                steps.link(nc.vector.scalar_tensor_tensor(out=den[:], in0=d, scalar=-1.0, in1=d, op0=ALU.mult, op1=ALU.max))
                steps.link(nc.vector.tensor_tensor(den[:], den[:], em, ALU.max))
                nc.vector.reciprocal(rden[:], den[:]).then_inc(ml_rden, 1)

            def rows(t, b):
                dve.wait_ge(ml_sq, t + 1)
                nc.vector.tensor_scalar(hr0[:], ssq[:], 1.0 / DH, RMS_EPS, ALU.mult, ALU.add).then_inc(ml_var, 1)
                dve.wait_ge(ml_pow, t + 1)
                steps.link(nc.vector.tensor_tensor(hs[:], rden[:], hr[:], ALU.mult))
                for h in range(H):
                    last = nc.vector.scalar_tensor_tensor(out=oy[:, b, h], in0=num[:, h, 0:DH], scalar=hs[:, h:h + 1], in1=oy[:, b, h],
                                                          op0=ALU.mult, op1=ALU.mult)
                last.then_inc(ml_y, 1)

            def chunk(t, b, uses):
                front(t, b, 0)
                for h in range(H):
                    inter(t, h, 4 + h, H * t + h + 1)
                denominators(t)
                for h in range(H):
                    for z in range(2):
                        dve.wait_ge(ml_upd, KT * t + 2 * h + z + 1)
                        nc.vector.scalar_tensor_tensor(out=C_T[:, h, z], in0=C_T[:, h, z], scalar=keep_col(h, t), in1=PS[:, 2 * h + z, 0:E1],
                                                       op0=ALU.mult, op1=ALU.add).then_inc(ml_state, 1)
                rows(t, b)
            steps.link(nc.vector.memset(v1[:, :, DH:E1], 1.0))
            dve.wait_ge(nf_turn, 1)
            steps.mark(nc.vector.tensor_copy(n_T[:].rearrange("p z n -> p (z n)"), PS[:, 2, 0:2 * NB * H]))
            nc.vector.tensor_copy(keep8[:], PS[0:NB, 2, 64:64 + H]).then_inc(nf_copied, 1)
            ml_tiles(dve, chunk, steps, 3)

            dve.wait_ge(ml_state, KT * NPT)
            nc.vector.tensor_copy(n_cols[:].rearrange("p (h z) -> p h z", h=H), C_T[:, :, :, DH]).then_inc(nf_copied, 1)
            front(SB, 0, 1)
            dve.wait_ge(ml_init, 2)
            dve.sem_inc(sc_CT, 2)
            for b in range(2):
                dve.sem_inc(cb_stored[b], 16)
            with dve.Fori(0, H) as h:
                for z in range(2):
                    last = nc.vector.tensor_copy(qm[:, z].rearrange("p (b r) -> p b r", b=NB)[:, :, 0:TS],
                                                 q_in[:, 0, bass.ds(2 * h + z, 1)].rearrange("p k (b r) -> p (k b) r", b=NB))
                last.then_inc(sc_qm, 1)
                for b in range(NB):
                    r = NB * h + b
                    if b > 1:
                        dve.wait_ge(sc_upd, r - 1)
                    nc.vector.tensor_scalar(v_own[:, b % 2], v1[:, bass.ds(h, 1), 0:DH].rearrange("p h d -> p (h d)"), own[:, b:b + 1], None,
                                            ALU.mult).then_inc(sc_own, 1)
                    if b:
                        new_state(dve, h, b - 1)
                new_state(dve, h, NB - 1)
                inter(SB, h, 4, H * SB + h + 1)
            dve.wait_ge(nu_done, 1)
            dve.wait_ge(n_loaded, 32)
            for h in range(H):
                last = nc.vector.scalar_tensor_tensor(out=nb_in[:, h], in0=nb_in[:, h], scalar=keep8[:, h:h + 1],
                                                      in1=PS[0:NB, 6 + h // 2, DH * (h % 2):DH * (h % 2 + 1)], op0=ALU.mult, op1=ALU.add)
            last.then_inc(nu_new, 1)
            dve.wait_ge(nf_turn, 2)
            dve.wait_ge(sc_new, NB * H)
            nc.vector.tensor_copy(n_row, PS[0:KT, 5, 0:P]).then_inc(nf_copied, 1)
            denominators(SB)
            rows(SB, 0)
            gain(SB)

        def new_state(dve, h, b):
            r = NB * h + b
            dve.wait_ge(sc_upd, r + 1)
            dve.wait_ge(cb_stored[b % 2], 16 * (NB // 2 * h + b // 2 + 1))
            nc.vector.scalar_tensor_tensor(out=cb_new[:, b % 2], in0=cb_in[b % 4], scalar=keep_col(h, NPT + b),
                                           in1=PS[:, 2 + b % 2].rearrange("p (z d) -> p z d", z=2), op0=ALU.mult, op1=ALU.add).then_inc(sc_new, 1)

        xq_loaded, mkv_loaded = [sem("xq_loaded0"), sem("xq_loaded1")], sem("mkv_loaded")
        (xa_S, xa_max, xa_exp, xa_p, xa_pT, xa_copied, xa_y, xa_half, xa_hi, xa_lo) = (
            sem(n) for n in ("xa_S", "xa_max", "xa_exp", "xa_p", "xa_pT", "xa_copied", "xa_y", "xa_half", "xa_hi", "xa_lo"))
        cache_loaded = [sem(f"cache_loaded{s}") for s in range(4)]
        ck_turn, ck_a, ck_d, ck_q, ck_used, cv_own, cv_used, cv_nat, cv_turned = (
            sem(n) for n in ("ck_turn", "ck_a", "ck_d", "ck_q", "ck_used", "cv_own", "cv_used", "cv_nat", "cv_turned"))
        prob_own = prob[:].rearrange("p b h m -> p b (h m)").rearrange("p b (m h j) -> p b m h j", m=2, h=H)
        xa_nat = prob_T[:, 1].rearrange("p m h j -> p (m h j)")
        ck_T = (mk_T, mv[:].rearrange("p z c -> p (z c)").rearrange("p (k m) -> p k m", k=KT))

        def cache(eng, name, b, slot):
            v = a[name][0].rearrange("b (z m) h d -> b m z (h d)", m=P)
            v = v[b] if isinstance(b, int) else v[bass.ds(b, 1)].rearrange("b m z c -> (b m) z c")
            eng.dma_start(cache_in[:, slot], v).then_inc(cache_loaded[slot], 16)

        def values(eng, b):
            if b < 4:
                eng.wait_ge(ck_turn, 2 * (NB - 3 + b))
            else:
                eng.wait_ge(cv_used, b - 3)
            cache(eng, "cache_mem_v", b, b % 4)

        def load_xq(sp, t, b):
            if not isinstance(t, int) or t > 1:
                sp.wait_ge(xa_S, t - 1)
            sp.dma_start(xq_in[:, b], proj_d[XQ:XQ + KT, :, tok(t)].rearrange("k p n -> p k n")).then_inc(xq_loaded[b], 16)

        def sp_xattn_ahead(sp):
            load_xq(sp, 0, 0)
            sp.dma_start(mk_T[:], kvT_d[0:KT].rearrange("k p m -> p k m")).then_inc(mkv_loaded, 16)
            sp.dma_start(mv[:], o["p_mem_v"][0, 0].rearrange("(z m) h d -> m z (h d)", m=P)).then_inc(mkv_loaded, 16)
            load_xq(sp, 1, 1)

        def sp_xattn(sp):
            def load(t, b):
                load_xq(sp, t, b)
            with sp.Fori(1, NPT // 2) as i:
                load(2 * i, 0)
                load(2 * i + 1, 1)
            load(SB, 0)
            for b in range(4):
                cache(sp, "cache_mem_k", b, b)
            with sp.Fori(1, NB // 4) as i:
                for s in range(4):
                    sp.wait_ge(ck_turn, 2 * (4 * i + s - 3))
                    cache(sp, "cache_mem_k", 4 * i + s, s)
            for b in (0, 2):
                values(sp, b)
            for b in (4, 6):
                values(sp, b)

        def pe_xattn(pe):
            def scores(t, b, lap):
                pe.wait_ge(xq_loaded[b], 16 * (lap + 1))
                if not isinstance(t, int) or t > 1:
                    pe.wait_ge(xa_exp, t - 1)
                for h in range(H):
                    for z in range(2):
                        last = nc.tensor.matmul(PS[:, 2 * b + h // 2, MEM * (h % 2):MEM * (h % 2 + 1)], xq_in[:, b, 2 * h + z],
                                                mk_T[:, 2 * h + z], start=z == 0, stop=z == 1)
                last.then_inc(xa_S, 1)

            def p_turn(t, b):
                pe.wait_ge(xa_p, t + 1)
                if not isinstance(t, int) or t > 0:
                    pe.wait_ge(xa_copied, t)
                for m in range(2):
                    for h in range(H):
                        last = nc.tensor.transpose(PS[:, 4 + m, P * h:P * (h + 1)], prob[:, b, h, P * m:P * (m + 1)], ident[:])
                last.then_inc(xa_pT, 1)

            def out(t, b):
                pe.wait_ge(xa_copied, t + 1)
                if not isinstance(t, int) or t > 0:
                    pe.wait_ge(xa_half, 2 * t)
                for k in range(KT):
                    for m in range(2):
                        last = nc.tensor.matmul(PS[:, 6 + k // 4, P * (k % 4):P * (k % 4 + 1)], mv[:, m, P * k:P * (k + 1)],
                                                prob_T[:, b, m, k // 2], start=m == 0, stop=m == 1)
                last.then_inc(xa_y, 1)
            pe.wait_ge(mkv_loaded, 32)
            scores(0, 0, 0)
            scores(1, 1, 0)
            p_turn(0, 0)
            scores(2, 0, 1)
            p_turn(1, 1)
            out(0, 0)
            scores(3, 1, 1)
            p_turn(2, 0)
            out(1, 1)
            with pe.Fori(2, NPT // 2) as i:
                for b in range(2):
                    t = 2 * i + b
                    scores(t, b, i)
                    p_turn(t - 1, 1 - b)
                    out(t - 2, b)
            p_turn(NPT - 1, 1)
            out(NPT - 2, 0)
            out(NPT - 1, 1)

            pe.wait_ge(xa_half, 2 * NPT)
            pe.wait_ge(xa_exp, NPT)

            def k_turn(b, s, lap):
                pe.wait_ge(cache_loaded[s], 16 * (lap + 1))
                for g in range(2):
                    if not isinstance(b, int) or b > 0:
                        pe.wait_ge((ck_a, ck_d)[g], b)
                    for q in range(4):
                        k = 4 * g + q
                        for m in range(2):
                            last = nc.tensor.transpose(PS[:, 4 + k // 2, MEM * (k % 2) + P * m:MEM * (k % 2) + P * (m + 1)],
                                                       cache_in[:, s, m, P * k:P * (k + 1)], ident[:])
                    last.then_inc(ck_turn, 1)

            def k_scores(b, s, first=False, end=False):
                pe.wait_ge(ck_a, b + 1)
                pe.wait_ge(ck_d, b + 1)
                pe.wait_ge(ck_q, b + 1)
                for k in range(KT):
                    h = k // 2
                    last = nc.tensor.matmul(PS[:, h // 2, MEM * (h % 2):MEM * (h % 2 + 1)], xqm[:, s, k], ck_T[s][:, k],
                                            start=first and k % 4 == 0, stop=end and k % 4 == 3, skip_group_check=True)
                last.then_inc(ck_used, 1)
            k_turn(0, 0, 0)
            for b in range(1, 4):
                k_turn(b, b, 0)
                k_scores(b - 1, 1 - b % 2, first=b == 1)
            with pe.Fori(1, NB // 4) as i:
                for s in range(4):
                    b = 4 * i + s
                    k_turn(b, s, i)
                    k_scores(b - 1, 1 - s % 2)
            k_scores(NB - 1, 1, end=True)
            p_turn(SB, 0)
            pe.wait_ge(xa_copied, SB + 1)
            for b in range(NB):
                pe.wait_ge(cv_own, b + 1)
                pe.wait_ge(cache_loaded[b % 4], 16 * (NB // 4 + b // 4 + 1))
                for h in range(H):
                    for m in range(2):
                        last = nc.tensor.matmul(PS[:, 6 + h // 2, DH * (h % 2):DH * (h % 2 + 1)], prob_own[:, b % 2, m, h],
                                                cache_in[:, b % 4, m, DH * h:DH * (h + 1)], start=b == 0 and m == 0 and h % 2 == 0,
                                                stop=b == NB - 1 and m == 1 and h % 2 == 1, skip_group_check=True)
                last.then_inc(cv_used, 1)
            pe.wait_ge(cv_nat, 1)
            for k in range(KT):
                last = nc.tensor.transpose(PS[:, 6 + k // 4, P * (k % 4):P * (k % 4 + 1)], xa_nat[:, P * k:P * (k + 1)], ident[:])
            last.then_inc(cv_turned, 1)

        def act_xattn(act):
            def probs(t, b, ready):
                act.wait_ge(xa_max, t + 1)
                if not isinstance(t, int) or t > 1:
                    act.wait_ge(xa_pT, t - 1)
                for h in range(H):
                    last = nc.scalar.activation(prob[:, b, h], PS[:, 2 * b + h // 2, MEM * (h % 2):MEM * (h % 2 + 1)], ACT.Exp,
                                                bias=smax[:, b, h:h + 1], accum_out=ssum[:, b, h:h + 1])
                last.then_inc(xa_exp, 1)

            def turned(t, b):
                act.wait_ge(xa_pT, t + 1)
                if not isinstance(t, int) or t > 1:
                    act.wait_ge(xa_y, t - 1)
                nc.scalar.copy(prob_T[:, b].rearrange("p m h j -> p m (h j)"), PS[:, 4:6]).then_inc(xa_copied, 1)

            def hi(t):
                for n in range(2):
                    act.wait_ge(xa_half, 2 * t + n + 1)
                    act.wait_ge(gates_done, 1)
                    nc.scalar.copy(A_hi[:, 4 * n:4 * n + 4, tok(t)], xa_T[:, n]).then_inc(xa_hi, 1)
            probs(0, 0, 0)
            probs(1, 1, 0)
            turned(0, 0)
            for t in (2, 3):
                probs(t, t % 2, 0)
                turned(t - 1, 1 - t % 2)
                hi(t - 2)
            with act.Fori(2, NPT // 2) as i:
                for b in range(2):
                    t = 2 * i + b
                    probs(t, b, 0)
                    turned(t - 1, 1 - b)
                    hi(t - 2)
            turned(NPT - 1, 1)
            hi(NPT - 2)
            hi(NPT - 1)

            def keys(b, s):
                act.wait_ge(ck_turn, 2 * b + 1)
                if not isinstance(b, int) or b > 1:
                    act.wait_ge(ck_used, b - 1)
                nc.scalar.copy(ck_T[s][:, 0:4].rearrange("p (a k) m -> p a (k m)", a=2), PS[:, 4:6]).then_inc(ck_a, 1)
            keys(0, 0)
            keys(1, 1)
            with act.Fori(1, NB // 2) as i:
                for s in range(2):
                    keys(2 * i + s, s)
            for b in (1, 3):
                values(act, b)
            act.wait_ge(ck_used, NB)
            probs(SB, 0, 0)
            turned(SB, 0)
            for b in (5, 7):
                values(act, b)
            act.wait_ge(cv_used, NB)
            nc.scalar.copy(xa_nat, PS[:, 6:8].rearrange("p n c -> p (n c)")).then_inc(cv_nat, 1)
            hi(SB)

        def pool_xattn(pool):
            def lo(t):
                for n in range(2):
                    pool.wait_ge(xa_hi, 2 * t + n + 1)
                    pool.wait_ge(gates_done, 1)
                    nc.gpsimd.tensor_tensor(A_lo[:, 4 * n:4 * n + 4, tok(t)], xa_T[:, n], A_hi[:, 4 * n:4 * n + 4, tok(t)].bitcast(F32),
                                            ALU.subtract).then_inc(xa_lo, 1)
            with pool.Fori(0, NPT) as t:
                lo(t)
            lo(SB)

        def dve_xattn(dve):
            steps = st["dve"]

            def maxima(t, b, sem_, count):
                dve.wait_ge(sem_, count)
                nc.vector.tensor_reduce(smax[:, b], PS[:, 2 * b:2 * b + 2].rearrange("p n (h m) -> p (n h) m", h=2), AX_X, ALU.max,
                                        negate=True).then_inc(xa_max, 1)

            def norm(t, b):
                dve.wait_ge(xa_exp, t + 1)
                steps.link(nc.vector.reciprocal(rsum[:, b], ssum[:, b]))
                for h in range(H):
                    last = nc.vector.tensor_scalar(prob[:, b, h], prob[:, b, h], rsum[:, b, h:h + 1], None, ALU.mult)
                last.then_inc(xa_p, 1)

            def half(t, sem_, count):
                dve.wait_ge(sem_, count)
                for n in range(2):
                    if not isinstance(t, int) or t > 0:
                        dve.wait_ge(xa_lo, 2 * t + n - 1)
                    nc.vector.tensor_scalar(xa_T[:, n].rearrange("p k c -> p (k c)"), PS[:, 6 + n], 0.5, None, ALU.mult).then_inc(xa_half, 1)
            maxima(0, 0, xa_S, 1)
            norm(0, 0)
            maxima(1, 1, xa_S, 2)
            norm(1, 1)
            for t in (2, 3):
                maxima(t, t % 2, xa_S, t + 1)
                norm(t, t % 2)
                half(t - 2, xa_y, t - 1)
            with dve.Fori(2, NPT // 2) as i:
                steps.enter(i - 2, 2)
                for b in range(2):
                    t = 2 * i + b
                    maxima(t, b, xa_S, t + 1)
                    norm(t, b)
                    half(t - 2, xa_y, t - 1)
            steps.leave(NPT // 2 - 2)
            half(NPT - 2, xa_y, NPT - 1)
            half(NPT - 1, xa_y, NPT)

            def own_queries(b, s):
                if not isinstance(b, int) or b > 1:
                    dve.wait_ge(ck_used, b - 1)
                steps.link(nc.vector.memset(xqm[:, s], 0.0))
                c = slice(TS * b, TS * (b + 1)) if isinstance(b, int) else bass.ds(TS * b, TS)
                nc.vector.tensor_copy(xqm[:, s, :, c], xq_in[:, 0, :, c]).then_inc(ck_q, 1)

            def keys(b, s):
                dve.wait_ge(ck_turn, 2 * b + 2)
                nc.vector.tensor_copy(ck_T[s][:, 4:8].rearrange("p (a k) m -> p a (k m)", a=2), PS[:, 6:8]).then_inc(ck_d, 1)
            dve.wait_ge(xq_loaded[0], 16 * (NPT // 2 + 1))
            for b in range(2):
                own_queries(b, b)
                keys(b, b)
            with dve.Fori(1, NB // 2) as i:
                steps.enter(i - 1, 2)
                for s in range(2):
                    own_queries(2 * i + s, s)
                    keys(2 * i + s, s)
            steps.leave(NB // 2 - 1)
            maxima(SB, 0, ck_used, NB)
            norm(SB, 0)
            dve.wait_ge(xa_copied, SB + 1)
            for b in range(NB):
                s = b % 2
                if b > 1:
                    dve.wait_ge(cv_used, b - 1)
                    steps.link(nc.vector.memset(prob_own[:, s, :, :, TS * (b - 2):TS * (b - 1)], 0.0))
                else:
                    steps.link(nc.vector.memset(prob_own[:, s], 0.0))
                nc.vector.tensor_copy(prob_own[:, s, :, :, TS * b:TS * (b + 1)], prob_T[:, 0, :, :, TS * b:TS * (b + 1)]).then_inc(cv_own, 1)
            half(SB, cv_turned, 1)

        early_sems.close()
        x2_loaded, post_loaded, mix_loaded, y_stored = sem("x2_loaded"), sem("post_loaded"), [sem(f"mix_loaded{r}") for r in range(4)], sem("y_stored")
        mix_hi, mix_lo = sem("mix_hi"), sem("mix_lo")
        f_copied, f_turned, f_nat = sem("f_copied"), sem("f_turned"), sem("f_nat")
        n_sq, n_var, n_pow, n_post, n_x2, n_xs, n_turned, n_gain, n_hi, n_lo, n_y = (
            sem(n) for n in ("n_sq", "n_var", "n_pow", "n_post", "n_x2", "n_xs", "n_turned", "n_gain", "n_hi", "n_lo", "n_y"))
        n_lo0 = sem("n_lo0")
        f_th, f_v, f_g, f_hi, f_lo = sem("f_th"), sem("f_v"), sem("f_g"), sem("f_hi"), sem("f_lo")
        G_hi, G_lo = (t[:].rearrange("p k n -> p (k n)")[:, 0:FT * TC].rearrange("p (f n) -> p f n", n=TC) for t in (A_hi, A_lo))
        IN_LAPS, OUT_LAPS = 2 * FT // RAW, 2 * KT // RAW
        UNITS = TH_UNITS
        TILES, NORMS, HALVES = 2 * KT, 9, 6

        def unit(third, n):
            return U_TH + UNITS * third + n

        def lap_of(third, n):
            return U_TH // RAW + UNITS // RAW * third + n // RAW

        def load_mix(sp, third, r):
            if third:
                sp.wait_ge(mix_lo, 4 * third)
            sp.dma_start(mix_in[:, 2 * r:2 * r + 2], part_d[2 * r:2 * r + 2, :, TC * third:TC * (third + 1)].rearrange("k p n -> p k n")
                         ).then_inc(mix_loaded[r], 16)

        def split_mix_hi(act, third, r):
            act.wait_ge(mix_loaded[r], 16 * (third + 1))
            nc.scalar.copy(m_hi[:, 2 * r:2 * r + 2], mix_in[:, 2 * r:2 * r + 2]).then_inc(mix_hi, 1)

        def split_mix_lo(eng, third, r):
            eng.wait_ge(mix_hi, 4 * third + r + 1)
            eng.tensor_tensor(m_lo[:, 2 * r:2 * r + 2], mix_in[:, 2 * r:2 * r + 2], m_hi[:, 2 * r:2 * r + 2].bitcast(F32), ALU.subtract).then_inc(mix_lo, 1)

        def sp_mix_ahead(sp):
            for b in range(2):
                sp.wait_ge(part_stored[b], 16 * (4 * 2 + 3))
            for r in range(3):
                load_mix(sp, 0, r)

        def sp_ffn(sp):
            load_mix(sp, 0, 3)
            for g, name in enumerate(("norm_mix_post", "norm_ffn_post")):
                sp.dma_start(post[:, g], a[name][0].partition_broadcast(P)).then_inc(post_loaded, 16)

            def token_tile(prompt, sample, t):
                return prompt[0].rearrange("(t p) d -> t p d", p=P)[t] if t < NPT else sample.rearrange("b t d -> (b t) d")

            def load_x2(third):
                for n in range(3):
                    sp.dma_start(x2[:, n], token_tile(a["x_prompt"], a["x_sample"], 3 * third + n)).then_inc(x2_loaded, 16)

            def store_y(third):
                for n in range(3):
                    sp.wait_ge(n_y, 3 * third + n + 2)
                    sp.dma_start(token_tile(o["y_prompt"], o["y_sample"], 3 * third + n), x2[:, n]).then_inc(y_stored, 16)
                sp.wait_ge(y_stored, 48 * (third + 1))

            def ffn_in_src(i, s):
                return w_fi_v[:, :, bass.ds(DFF * (s % 2) + P * (2 * i + s // 2), P)]

            def ffn_out_src(i, s):
                return w_fo_v[s % 2][:, :, bass.ds(P * (2 * i + s // 2), P)]
            load_x2(0)
            for third in range(3):
                for s in range(RAW):
                    load_w(sp, unit(third, RAW + s), s, w_out_v[:, :, (RAW + s) * P:(RAW + s + 1) * P])
                if third:
                    store_y(third - 1)
                    load_x2(third)
                for s in range(RAW):
                    load_w(sp, unit(third, KT + s), s, ffn_in_src(0, s))
                with sp.Fori(1, IN_LAPS) as i:
                    for s in range(RAW):
                        load_w(sp, unit(third, KT + s) + RAW * i, s, ffn_in_src(i, s))
                for s in range(RAW):
                    load_w(sp, unit(third, KT + 2 * FT + s), s, ffn_out_src(0, s), FK)
                for i in range(OUT_LAPS):
                    if third < 2:
                        load_mix(sp, third + 1, i)
                    for s in range(RAW):
                        if i < OUT_LAPS - 1:
                            load_w(sp, unit(third, KT + 2 * FT + RAW * (i + 1) + s), s, ffn_out_src(i + 1, s), FK)
                        elif third < 2:
                            load_w(sp, unit(third + 1, s), s, w_out_v[:, :, s * P:(s + 1) * P])
            store_y(2)

        def thirds_of(eng, body):
            with eng.Fori(0, 2) as third:
                body(third, False)
            body(2, True)

        def pe_ffn(pe):
            def turn(third, c, b):
                O = TILES * third + c
                pe.wait_ge(f_copied, O + 3)
                pe.wait_ge(f_nat, O + 1)
                for n in range(3):
                    last = nc.tensor.transpose(PS[:, 6 + b, P * n:P * (n + 1)], oT[:, b, P * n:P * (n + 1)], ident[:])
                last.then_inc(f_turned, 1)

            def third_of(third, last):
                pe.wait_ge(mix_lo, 4 * third + 4)
                for j in range(KT):
                    pe.wait_ge(f_copied, TILES * third + j + 1)
                    use_unit(pe, unit(third, j), j % RAW, [PS[:, 4 + j % 2, 0:TC]], lambda k, c: m_hi[:, k], lambda k, c: m_lo[:, k])
                    if j:
                        turn(third, j - 1, (j - 1) % 2)
                turn(third, KT - 1, 1)
                for n in range(3):
                    pe.wait_ge(n_xs, 3 * third + n + 1)
                    for h in range(2):
                        if n == 2:
                            pe.wait_ge(n_gain, HALVES * third + h + 1)
                        for q in range(4):
                            k = 4 * h + q
                            t = nc.tensor.transpose(PS[:, 2 * (n % 2) + h, P * q:P * (q + 1)], nat[:, n, P * k:P * (k + 1)], ident[:])
                        t.then_inc(n_turned, 1)
                with pe.Fori(0, IN_LAPS) as i:
                    pe.wait_ge(n_lo, 3 * third + 4)
                    pe.wait_ge(n_lo0, 3 * third + 4)
                    for s in range(RAW):
                        if s % 2 == 0:
                            pe.wait_ge(f_g, FT * third + 2 * i + s // 2 + 1)
                        use_unit(pe, unit(third, KT + s) + RAW * i, s, [PS[:, s, 0:TC]], lambda k, c: m_hi[:, k], lambda k, c: m_lo[:, k])

                def out_lap(i, first):
                    for s in range(RAW):
                        c, z = 2 * i + s // 2, s % 2
                        if first and s < 2:
                            pe.wait_ge(f_lo, FT * third + FK * (z + 1) + 2)
                        if z == 0:
                            pe.wait_ge(f_copied, TILES * third + KT + c + 1)
                        use_unit(pe, unit(third, KT + 2 * FT + s) + RAW * i, s, [PS[:, 4 + s // 2, 0:TC]],
                                 lambda k, c, z=z: G_hi[:, FK * z + k], lambda k, c, z=z: G_lo[:, FK * z + k], FK, z == 0, z == 1)
                        if z and not (first and s == 1):
                            turn(third, KT + c - 1, 1 - s // 2)
                out_lap(0, True)
                with pe.Fori(1, OUT_LAPS) as i:
                    out_lap(i, False)
                turn(third, TILES - 1, 1)
            thirds_of(pe, third_of)

        def act_ffn(act):
            def evac(third, c, b):
                O = TILES * third + c
                act.wait_ge(f_turned, O + 1)
                nc.scalar.copy(oT[:, b], PS[:, 4 + b, 0:TC]).then_inc(f_copied, 1)

            def square(third, n, src):
                if not (isinstance(third, int) and third == 0 and n == 0):
                    act.wait_ge(n_sq, NORMS * third + n + 1)
                nc.scalar.activation(n_junk, src, ACT.Square, accum_out=n_ss[:, n:n + 1]).then_inc(n_sq, 1)

            def gate(third, p, b):
                act.wait_ge(f_lo, FT * third + p + 1)
                nc.scalar.activation(th[:, b], PS[:, 2 * b, 0:TC], ACT.Tanh, scale=0.5).then_inc(f_th, 1)

            def hi(third, p, b):
                act.wait_ge(f_g, FT * third + p + 3)
                act.wait_ge(gates_done, 1)
                d = G_hi[:, p] if isinstance(p, int) else G_hi[:, bass.ds(p, 1)].rearrange("p f n -> p (f n)")
                nc.scalar.copy(d, th[:, b]).then_inc(f_hi, 1)

            def third_of(third, last):
                act.wait_ge(n_sq, NORMS * third + 1)
                for j in range(KT):
                    split_hi(act, unit(third, j + SPLIT), lap_of(third, j + SPLIT), (j + SPLIT) % RAW)
                    act.wait_ge(w_used, unit(third, j) + 1)
                    evac(third, j, j % 2)
                act.wait_ge(f_nat, TILES * third + KT + 2)
                for n in range(3):
                    square(third, n, nat[:, n])
                for n in range(3):
                    act.wait_ge(n_x2, 3 * third + n + 1)
                    square(third, 3 + n, x2[:, n])
                for n in range(3):
                    for h in range(2):
                        act.wait_ge(n_gain, HALVES * third + 2 * n + h + 1)
                        nc.scalar.copy(m_hi[:, 4 * h:4 * h + 4, P * n:P * (n + 1)], nT[:, h]).then_inc(n_hi, 1)

                def in_lap(i, first, end):
                    for s in range(RAW):
                        u = KT + RAW * i + s
                        split_hi(act, unit(third, SPLIT) + u, lap_of(third, KT) + i + (s + SPLIT) // RAW, (s + SPLIT) % RAW,
                                 FK if end and s > 1 else KT)
                        p = 2 * i + s // 2
                        act.wait_ge(w_used, unit(third, 0) + u + 1)
                        if s % 2 == 0:
                            gate(third, p, s // 2)
                            if not (first and s == 0):
                                hi(third, p - 1, 1 - s // 2)
                in_lap(0, True, False)
                act.wait_ge(gates_done, 1)
                with act.Fori(1, IN_LAPS - 1) as i:
                    in_lap(i, False, False)
                in_lap(IN_LAPS - 1, False, True)
                hi(third, FT - 1, 1)

                def out_lap(i, end):
                    if not last:
                        split_mix_hi(act, third + 1, i)
                    for s in range(RAW):
                        u = KT + 2 * FT + RAW * i + s
                        if not (last and end and s > 1):
                            split_hi(act, unit(third, SPLIT) + u, lap_of(third, KT + 2 * FT) + i + (s + SPLIT) // RAW, (s + SPLIT) % RAW,
                                     KT if end and s > 1 else FK)
                        act.wait_ge(w_used, unit(third, 0) + u + 1)
                        if s % 2:
                            evac(third, KT + 2 * i + s // 2, s // 2)

                for i in range(OUT_LAPS):
                    out_lap(i, i == OUT_LAPS - 1)
                act.wait_ge(f_nat, TILES * third + TILES + 2)
                for n in range(3):
                    square(third, 6 + n, nat[:, n])
            act.sem_inc(n_sq, 1)
            split_mix_hi(act, 0, 3)
            thirds_of(act, third_of)

        def pool_ffn(pool):
            def power(third, n):
                pool.wait_ge(n_var, NORMS * third + n + 1)
                nc.gpsimd.tensor_tensor(n_r[:, n:n + 1], n_v[:, n:n + 1], minus_half[:, 0:1], ALU.pow).then_inc(n_pow, 1)

            def lo(third, p, b):
                pool.wait_ge(f_hi, FT * third + p + 1)
                pool.wait_ge(gates_done, 1)
                h, l = (t[:, p] if isinstance(p, int) else t[:, bass.ds(p, 1)].rearrange("p f n -> p (f n)") for t in (G_hi, G_lo))
                nc.gpsimd.tensor_tensor(l, th[:, b], h.bitcast(F32), ALU.subtract).then_inc(f_lo, 1)

            def third_of(third, last):
                for j in range(KT):
                    split_lo(pool, unit(third, j + SPLIT), (j + SPLIT) % RAW)
                for n in range(6):
                    power(third, n)
                for n in range(3):
                    pool.wait_ge(n_hi, HALVES * third + 2 * n + 2)
                    m = (slice(None), slice(4, 8), slice(P * n, P * (n + 1)))
                    nc.gpsimd.tensor_tensor(m_lo[m], nT[:, 1], m_hi[m].bitcast(F32), ALU.subtract).then_inc(n_lo, 1)

                def in_lap(i, first, end):
                    for s in range(RAW):
                        split_lo(pool, unit(third, KT + SPLIT + s) + RAW * i, (s + SPLIT) % RAW, FK if end and s > 1 else KT)
                        if s % 2 == 0 and not (first and s == 0):
                            lo(third, 2 * i + s // 2 - 1, 1 - s // 2)
                in_lap(0, True, False)
                with pool.Fori(1, IN_LAPS - 1) as i:
                    in_lap(i, False, False)
                in_lap(IN_LAPS - 1, False, True)
                lo(third, FT - 1, 1)
                for i in range(OUT_LAPS):
                    if not last:
                        split_mix_lo(nc.gpsimd, third + 1, i)
                    for s in range(RAW):
                        end = i == OUT_LAPS - 1 and s > 1
                        if not (last and end):
                            split_lo(pool, unit(third, KT + 2 * FT + SPLIT + s + RAW * i), (s + SPLIT) % RAW, KT if end else FK)
                for n in range(6, 9):
                    power(third, n)
            pool.sem_inc(n_lo, 1)
            pool.sem_inc(f_lo, 2)
            thirds_of(pool, third_of)

        def dve_ffn(dve):
            def evac(third, c, b):
                O = TILES * third + c
                dve.wait_ge(f_turned, O + 3)
                col = c % KT if isinstance(c, int) else c - KT
                d = nat[:, :, P * col:P * (col + 1)] if isinstance(c, int) else nat[:, :, bass.ds(P * col, P)]
                nc.vector.tensor_scalar(d, PS[:, 6 + b, 0:TC].rearrange("p (n c) -> p n c", n=3), 1.0, None, ALU.mult).then_inc(f_nat, 1)

            def variance(third, n):
                dve.wait_ge(n_sq, NORMS * third + n + 2)
                nc.vector.tensor_scalar(n_v[:, n:n + 1], n_ss[:, n:n + 1], 1.0 / D, RMS_EPS, ALU.mult, ALU.add).then_inc(n_var, 1)

            def add_post(third, n, g):
                dve.wait_ge(n_pow, NORMS * third + 6 * g + n + 1)
                nc.vector.scalar_tensor_tensor(out=nat[:, n], in0=nat[:, n], scalar=n_r[:, 6 * g + n:6 * g + n + 1], in1=post[:, g],
                                               op0=ALU.mult, op1=ALU.mult).then_inc(n_post, 1)
                dve.wait_ge(n_post, 6 * third + 3 * g + n + 1)
                nc.vector.tensor_tensor(x2[:, n], x2[:, n], nat[:, n], ALU.add).then_inc(n_y if g else n_x2, 1)

            def swiglu(third, p, b):
                G = FT * third + p
                dve.wait_ge(f_th, G + 1)
                nc.vector.scalar_tensor_tensor(out=th[:, b], in0=th[:, b], scalar=1.0, in1=PS[:, 2 * b, 0:TC], op0=ALU.add, op1=ALU.mult).then_inc(f_v, 1)
                dve.wait_ge(f_v, G + 1)
                dve.wait_ge(w_used, unit(third, KT + 2) + 2 * p)
                nc.vector.scalar_tensor_tensor(out=th[:, b], in0=th[:, b], scalar=0.5, in1=PS[:, 2 * b + 1, 0:TC], op0=ALU.mult, op1=ALU.mult).then_inc(f_g, 1)

            def third_of(third, last):
                dve.wait_ge(n_y, 3 * third + 1)
                for j in range(KT):
                    evac(third, j, j % 2)
                for n in range(3):
                    variance(third, n)
                dve.wait_ge(x2_loaded, 48 * (third + 1))
                dve.wait_ge(post_loaded, 32)

                def scale(n):
                    variance(third, 3 + n)
                    dve.wait_ge(n_pow, NORMS * third + 3 + n + 1)
                    nc.vector.tensor_scalar(nat[:, n], x2[:, n], n_r[:, 3 + n:4 + n], None, ALU.mult).then_inc(n_xs, 1)

                def gain(n):
                    for h in range(2):
                        dve.wait_ge(n_turned, HALVES * third + 2 * n + h + 1)
                        dve.wait_ge(n_lo if h else n_lo0, 3 * third + n + 1)
                        nc.vector.tensor_tensor(nT[:, h], PS[:, 2 * (n % 2) + h].rearrange("p (k c) -> p k c", k=4),
                                                cols[:, V_FFN, 4 * h:4 * h + 4].unsqueeze(2).broadcast_to([P, 4, P]), ALU.mult).then_inc(n_gain, 1)
                    m = (slice(None), slice(0, 4), slice(P * n, P * (n + 1)))
                    dve.wait_ge(n_hi, HALVES * third + 2 * n + 1)
                    nc.vector.tensor_tensor(m_lo[m], nT[:, 0], m_hi[m].bitcast(F32), ALU.subtract).then_inc(n_lo0, 1)
                add_post(third, 0, 0)
                add_post(third, 1, 0)
                scale(0)
                add_post(third, 2, 0)
                scale(1)
                gain(0)
                scale(2)
                gain(1)
                gain(2)
                with dve.Fori(0, FT // 2) as i:
                    for b in range(2):
                        swiglu(third, 2 * i + b, b)
                for i in range(OUT_LAPS):
                    for c in (2 * i - 1, 2 * i):
                        if c >= 0:
                            evac(third, KT + c, c % 2)
                evac(third, TILES - 1, 1)
                for n in range(6, 9):
                    variance(third, n)
                for n in range(3):
                    add_post(third, n, 1)
            for x in (f_copied, f_turned, f_nat, f_g):
                dve.sem_inc(x, 2)
            dve.sem_inc(n_y, 1)
            dve.sem_inc(n_lo0, 1)
            split_mix_lo(nc.vector, 0, 3)
            thirds_of(dve, third_of)


        block = ctx.enter_context(nc.Block())

        @block.sync
        def _(sp):
            sp_norm(sp)
            end_phase(sp, 1)
            sp_proj(sp)
            end_phase(sp, 2)
            for b in range(2):
                sp.wait_ge(stage_stored[b], 16 * NPROJ // 2)
            sp_branch(sp, 0, lambda s: w_br_v[ORDER[1]][:, :, s * P:(s + 1) * P], sp_mlstm_ahead)
            end_phase(sp, 3)
            sp_mlstm(sp)
            sp.wait_ge(ml_lo, 2 * NT + 2)
            sp_branch(sp, 1, lambda s: w_br_v[ORDER[2]][:, :, s * P:(s + 1) * P], sp_xattn_ahead)
            end_phase(sp, 4)
            sp_xattn(sp)
            sp.wait_ge(xa_lo, 2 * NT)
            sp_branch(sp, 2, lambda s: w_out_v[:, :, s * P:(s + 1) * P])
            end_phase(sp, 5)
            sp_ffn(sp)

        @block.scalar
        def _(act):
            act_norm(act)
            end_phase(act, 1)
            act_proj(act)
            end_phase(act, 2)
            act_ln(act)
            act_branch(act, 0)
            end_phase(act, 3)
            act_mlstm(act)
            act_branch(act, 1)
            end_phase(act, 4)
            act_xattn(act)
            act_branch(act, 2)
            for r in range(3):
                split_mix_hi(act, 0, r)
            end_phase(act, 5)
            act_ffn(act)

        @block.gpsimd
        def _(pool):
            pool_norm(pool)
            end_phase(pool, 1)
            pool_proj(pool)
            end_phase(pool, 2)
            clear_early(pool)
            pool_ln(pool)
            pool_branch(pool, 0)
            end_phase(pool, 3)
            pool_mlstm(pool)
            pool_branch(pool, 1)
            end_phase(pool, 4)
            pool_xattn(pool)
            pool_branch(pool, 2)
            for r in (0, 2):
                split_mix_lo(nc.gpsimd, 0, r)
            end_phase(pool, 5)
            pool_ffn(pool)

        @block.vector
        def _(dve):
            dve_norm(dve)
            end_phase(dve, 1)
            dve_proj(dve)
            end_phase(dve, 2)
            dve_ln(dve)
            dve_branch(dve, 0)
            end_phase(dve, 3)
            dve_mlstm(dve)
            dve_branch(dve, 1)
            end_phase(dve, 4)
            dve_xattn(dve)
            dve_branch(dve, 2)
            split_mix_lo(nc.vector, 0, 1)
            end_phase(dve, 5)
            dve_ffn(dve)

        @block.tensor
        def _(pe):
            pe_norm(pe)
            end_phase(pe, 1)
            pe_proj(pe)
            end_phase(pe, 2)
            pe_branch(pe, 0, ln_lo, 3)
            end_phase(pe, 3)
            pe_mlstm(pe)
            pe_branch(pe, 1, ml_lo, 2 * NT + 2)
            end_phase(pe, 4)
            pe_xattn(pe)
            pe_branch(pe, 2, xa_lo, 2 * NT)
            end_phase(pe, 5)
            pe_ffn(pe)


_INS = ["x_prompt", "x_sample", "mem_prompt", "state_mlstm_c", "state_mlstm_n", "state_mlstm_m", "state_conv",
        "cache_mem_k", "cache_mem_v", "norm_mix_pre", "norm_mix_post", "norm_ffn_pre", "norm_ffn_post", "w_in",
        "b_gate", "mlstm_head_norm", "conv_w", "conv_b", "conv_ln_g", "conv_ln_b", "mem_norm", "w_mem_kv",
        "w_branch", "w_out", "w_ffn_in", "w_ffn_out"]
_OUTS = [("y_prompt", (1, SEQ, D)), ("y_sample", (NB, TS, D)), ("p_c", (1, 1, H, DH, DH)), ("p_n", (1, 1, H, DH)),
         ("p_m", (1, 1, H)), ("p_conv", (1, 1, CB, D)), ("p_mem_k", (1, 1, MEM, H, DH)),
         ("p_mem_v", (1, 1, MEM, H, DH)), ("s_c", (1, NB, H, DH, DH)), ("s_n", (1, NB, H, DH)), ("s_m", (1, NB, H)),
         ("s_conv", (1, NB, CB, D))]


def kernel(**inputs):
    import numpy as _np
    import concourse.bacc as _bacc
    from concourse.bass_utils import run_bass_kernel_spmd as _run

    nc = _bacc.Bacc("TRN2", target_bir_lowering=False, num_devices=1)
    arrays, ins, outs = {}, {}, {}
    for name in _INS:
        x = _np.ascontiguousarray(inputs[name])
        arrays[f"in_{name}"] = x
        ins[name] = nc.dram_tensor(f"in_{name}", x.shape, mybir.dt.from_np(x.dtype), kind="ExternalInput").ap()
    for name, shape in _OUTS:
        outs[name] = nc.dram_tensor(f"out_{name}", shape, F32, kind="ExternalOutput").ap()
    hybrid_step(nc, ins, outs)
    r = _run(nc, [arrays], core_ids=[0])
    return tuple(r.results[0][f"out_{name}"] for name, _ in _OUTS)
```
